# Optimizing a Trainium2 kernel written in Bass

```python
import math
import jax, jax.numpy as jnp
from jax import lax
import numpy as np
import math, functools

D_MODEL = 1024
BATCH = 1
SEQ = 256
DEPTH = 1

N_META = 16
CHUNK = 128
Q_BLOCK = 128
PAD = CHUNK - N_META
D_SSD = 2 * D_MODEL
SSD_HEAD_DIM = 64
H_SSD = D_SSD // SSD_HEAD_DIM
SSD_GROUPS = 4
D_STATE = 128
CONV_K = 4
CONV_DIM = D_SSD + 2 * SSD_GROUPS * D_STATE
H_ATT = 16
ATT_HEAD_DIM = 64
D_ATT = H_ATT * ATT_HEAD_DIM
N_COLS = D_SSD + CONV_DIM + H_SSD + D_ATT + 3 * D_ATT + H_ATT + 2 * D_MODEL
EPS = 1e-6


def rmsnorm(x, g):
    xf = x.astype(jnp.float32)
    y = xf * lax.rsqrt(jnp.mean(xf * xf, axis=-1, keepdims=True) + EPS)
    return (y * g.astype(jnp.float32)).astype(x.dtype)

def gated_group_rmsnorm(y, z, g):
    u = (y * jax.nn.silu(z)).astype(jnp.float32)
    shp = u.shape
    u = u.reshape(shp[:-1] + (SSD_GROUPS, shp[-1] // SSD_GROUPS))
    u = u * lax.rsqrt(jnp.mean(u * u, axis=-1, keepdims=True) + EPS)
    return (u.reshape(shp) * g.astype(jnp.float32)).astype(y.dtype)

def causal_depthwise_conv(u, w, b):
    C = u.shape[-1]
    out = lax.conv_general_dilated(u, w[:, None, :].astype(u.dtype), window_strides=(1,),
                                   padding=[(CONV_K - 1, 0)],
                                   dimension_numbers=("NWC", "WIO", "NWC"),
                                   feature_group_count=C)
    return out + b

def ssd_chunked(xh, dt, a, bmat, cmat):
    Bsz, Lp, H, P = xh.shape
    G, N = bmat.shape[-2:]
    R = H // G
    nc = Lp // CHUNK
    xdt = (xh.astype(jnp.float32) * dt[..., None]).reshape(Bsz, nc, CHUNK, G, R, P)
    adt = (dt * a).reshape(Bsz, nc, CHUNK, G, R).transpose(0, 1, 3, 4, 2)
    a_cs = jnp.cumsum(adt, axis=-1)
    bm = bmat.astype(jnp.float32).reshape(Bsz, nc, CHUNK, G, N)
    cm = cmat.astype(jnp.float32).reshape(Bsz, nc, CHUNK, G, N)
    causal = jnp.tril(jnp.ones((CHUNK, CHUNK), dtype=bool))
    seg = a_cs[..., :, None] - a_cs[..., None, :]
    decay = jnp.exp(jnp.where(causal, seg, -jnp.inf))
    cb = jnp.einsum("bclgn,bcsgn->bcgls", cm, bm)
    y_diag = jnp.einsum("bcgls,bcgrls,bcsgrp->bclgrp", cb, decay, xdt)
    decay_states = jnp.exp(a_cs[..., -1:] - a_cs)
    states = jnp.einsum("bclgn,bcgrl,bclgrp->bcgrpn", bm, decay_states, xdt)
    chunk_decay = jnp.exp(a_cs[..., -1])

    def step(h, inp):
        s, d = inp
        return h * d[..., None, None] + s, h

    h0 = jnp.zeros((Bsz, G, R, P, N), jnp.float32)
    _, h_in = lax.scan(step, h0, (jnp.swapaxes(states, 0, 1), jnp.swapaxes(chunk_decay, 0, 1)))
    h_in = jnp.swapaxes(h_in, 0, 1)
    y_off = jnp.einsum("bclgn,bcgrpn,bcgrl->bclgrp", cm, h_in, jnp.exp(a_cs))
    return (y_diag + y_off).reshape(Bsz, Lp, H, P)

def forgetting_attention(q, k, v, logf):
    Bsz, Lp, H, Dh = q.shape
    scale = 1.0 / math.sqrt(Dh)
    c = jnp.cumsum(logf, axis=1)
    c_k = jnp.transpose(c, (0, 2, 1))
    nb = Lp // Q_BLOCK
    qb = q.reshape(Bsz, nb, Q_BLOCK, H, Dh).transpose(1, 0, 2, 3, 4)
    cqb = c.reshape(Bsz, nb, Q_BLOCK, H).transpose(1, 0, 3, 2)
    kpos = jnp.arange(Lp)

    def block(args):
        i, qi, cqi = args
        qpos = i * Q_BLOCK + jnp.arange(Q_BLOCK)
        s = jnp.einsum("bthd,bshd->bhts", qi, k).astype(jnp.float32) * scale
        s = s + (cqi[..., :, None] - c_k[..., None, :])
        s = jnp.where(kpos[None, :] <= qpos[:, None], s, -jnp.inf)
        p = jax.nn.softmax(s, axis=-1).astype(v.dtype)
        return jnp.einsum("bhts,bshd->bthd", p, v)

    out = lax.map(block, (jnp.arange(nb), qb, cqb))
    return out.transpose(1, 0, 2, 3, 4).reshape(Bsz, Lp, H, Dh)

def hybrid_layer(h, norm_pre, w_in, conv_w, conv_b, dt_bias, a_log, d_skip, ssd_norm,
                 fgate_bias, gate_bias, w_proj_ssd, w_proj_att, w_out, norm_post):
    Bsz, L, _ = h.shape
    Lp = L + PAD
    u = rmsnorm(h, norm_pre)
    proj = u @ w_in
    cuts = [D_SSD, D_SSD + CONV_DIM, D_SSD + CONV_DIM + H_SSD,
            D_SSD + CONV_DIM + H_SSD + D_ATT,
            D_SSD + CONV_DIM + H_SSD + 2 * D_ATT,
            D_SSD + CONV_DIM + H_SSD + 3 * D_ATT,
            D_SSD + CONV_DIM + H_SSD + 4 * D_ATT,
            D_SSD + CONV_DIM + H_SSD + 4 * D_ATT + H_ATT]
    z_ssd, xbc, dt_raw, z_att, q, k, v, f_raw, g_raw = jnp.split(proj, cuts, axis=-1)

    xbc = jax.nn.silu(causal_depthwise_conv(xbc, conv_w, conv_b))
    xs, bm, cm = jnp.split(xbc, [D_SSD, D_SSD + SSD_GROUPS * D_STATE], axis=-1)
    dt = jax.nn.softplus(dt_raw.astype(jnp.float32) + dt_bias.astype(jnp.float32))
    a = -jnp.exp(a_log.astype(jnp.float32))
    front = ((0, 0), (PAD, 0), (0, 0))
    xs_p = jnp.pad(xs, front).reshape(Bsz, Lp, H_SSD, SSD_HEAD_DIM)
    bm_p = jnp.pad(bm, front).reshape(Bsz, Lp, SSD_GROUPS, D_STATE)
    cm_p = jnp.pad(cm, front).reshape(Bsz, Lp, SSD_GROUPS, D_STATE)
    dt_p = jnp.pad(dt, front)
    y = ssd_chunked(xs_p, dt_p, a, bm_p, cm_p)
    y = y + d_skip.astype(jnp.float32)[:, None] * xs_p.astype(jnp.float32)
    y = y[:, PAD:].reshape(Bsz, L, D_SSD).astype(h.dtype)
    y_ssd = gated_group_rmsnorm(y, z_ssd, ssd_norm)

    logf = jax.nn.log_sigmoid(f_raw.astype(jnp.float32) + fgate_bias.astype(jnp.float32))
    back = ((0, 0), (0, PAD), (0, 0))
    qh = jnp.pad(q, back).reshape(Bsz, Lp, H_ATT, ATT_HEAD_DIM)
    kh = jnp.pad(k, back).reshape(Bsz, Lp, H_ATT, ATT_HEAD_DIM)
    vh = jnp.pad(v, back).reshape(Bsz, Lp, H_ATT, ATT_HEAD_DIM)
    o = forgetting_attention(qh, kh, vh, jnp.pad(logf, back))
    o = o[:, :L].reshape(Bsz, L, D_ATT)
    y_att = o * jax.nn.silu(z_att)

    gates = jax.nn.sigmoid(g_raw + gate_bias)
    g_ssd, g_att = jnp.split(gates, 2, axis=-1)
    merged = g_ssd * (y_ssd @ w_proj_ssd) + g_att * (y_att @ w_proj_att)
    return h + rmsnorm(merged @ w_out, norm_post)

def first_inputs(seed: int = 0) -> dict:
    key = jax.random.key(seed)
    ks = jax.random.split(key, 16)
    D = D_MODEL
    nrm = jax.random.normal
    x = nrm(ks[0], (BATCH, SEQ, D), jnp.float32)
    meta_tokens = nrm(ks[1], (N_META, D), jnp.float32)
    norm_pre = 1.0 + 0.05 * nrm(ks[2], (DEPTH, D), jnp.float32)
    w_in = nrm(ks[3], (DEPTH, D, N_COLS), jnp.float32) * D ** -0.5
    conv_w = jax.random.uniform(ks[4], (DEPTH, CONV_K, CONV_DIM), jnp.float32, -0.5, 0.5)
    conv_b = 0.05 * nrm(ks[5], (DEPTH, CONV_DIM), jnp.float32)
    dt0 = jnp.exp(jax.random.uniform(ks[6], (DEPTH, H_SSD), jnp.float32,
                                     math.log(1e-3), math.log(1e-1)))
    dt_bias = dt0 + jnp.log(-jnp.expm1(-dt0))
    a_log = jnp.log(jax.random.uniform(ks[7], (DEPTH, H_SSD), jnp.float32, 1.0, 16.0))
    d_skip = 1.0 + 0.1 * nrm(ks[8], (DEPTH, H_SSD), jnp.float32)
    ssd_norm = 1.0 + 0.05 * nrm(ks[9], (DEPTH, D_SSD), jnp.float32)
    fgate_bias = jax.random.uniform(ks[10], (DEPTH, H_ATT), jnp.float32, 1.0, 6.0)
    gate_bias = 0.1 * nrm(ks[11], (DEPTH, 2 * D), jnp.float32)
    w_proj_ssd = nrm(ks[12], (DEPTH, D_SSD, D), jnp.float32) * D_SSD ** -0.5
    w_proj_att = nrm(ks[13], (DEPTH, D_ATT, D), jnp.float32) * D_ATT ** -0.5
    w_out = nrm(ks[14], (DEPTH, D, D), jnp.float32) * D ** -0.5
    norm_post = 1.0 + 0.05 * nrm(ks[15], (DEPTH, D), jnp.float32)
    return {"x": x, "meta_tokens": meta_tokens, "norm_pre": norm_pre, "w_in": w_in,
            "conv_w": conv_w, "conv_b": conv_b, "dt_bias": dt_bias, "a_log": a_log,
            "d_skip": d_skip, "ssd_norm": ssd_norm, "fgate_bias": fgate_bias,
            "gate_bias": gate_bias, "w_proj_ssd": w_proj_ssd, "w_proj_att": w_proj_att,
            "w_out": w_out, "norm_post": norm_post}

def first_block(x, meta_tokens, norm_pre, w_in, conv_w, conv_b, dt_bias, a_log, d_skip,
              ssd_norm, fgate_bias, gate_bias, w_proj_ssd, w_proj_att, w_out, norm_post):
    Bsz = x.shape[0]
    meta = jnp.broadcast_to(meta_tokens[None].astype(x.dtype), (Bsz, N_META, D_MODEL))
    h = jnp.concatenate([meta, x], axis=1)
    for i in range(DEPTH):
        h = hybrid_layer(h, norm_pre[i], w_in[i], conv_w[i], conv_b[i], dt_bias[i], a_log[i],
                         d_skip[i], ssd_norm[i], fgate_bias[i], gate_bias[i], w_proj_ssd[i],
                         w_proj_att[i], w_out[i], norm_post[i])
    return h[:, N_META:]


DEPTH_2 = 2

CONV_CH = 512
N_HEADS = 8
HEAD_DIM = 64
ATTN_CH = N_HEADS * HEAD_DIM
D_MIX = CONV_CH + ATTN_CH
D_IN = 2 * CONV_CH + 3 * ATTN_CH
CONV_K_2 = 31
GRID_W = 64
WIN_R = 8
WIN_C = 16
Q_CB = 16
N_CB = GRID_W // Q_CB
BAND_C = Q_CB + WIN_C
D_FF = 2816
N_EXPERTS = 8
TOP_K = 2
D_FF_EXPERT = 3584
MOE_BLK = 128
N_DENSE = (DEPTH_2 + 1) // 2
N_MOE = DEPTH_2 // 2
D_PLE = 256
LN_EPS = 1e-5
DEEPNORM_ALPHA = (2.0 * DEPTH_2) ** 0.25
DEEPNORM_BETA = (8.0 * DEPTH_2) ** -0.25


def layer_norm(x, g, b):
    xf = x.astype(jnp.float32)
    mu = jnp.mean(xf, axis=-1, keepdims=True)
    xc = xf - mu
    var = jnp.mean(xc * xc, axis=-1, keepdims=True)
    y = xc * lax.rsqrt(var + LN_EPS)
    return (y * g.astype(jnp.float32) + b.astype(jnp.float32)).astype(x.dtype)

def conformer_conv(a, g, w, b, ln_g, ln_b):
    u = a * jax.nn.sigmoid(g)
    c = u.shape[-1]
    pad = CONV_K_2 // 2
    y = lax.conv_general_dilated(
        u, w[:, None, :], window_strides=(1,), padding=[(pad, pad)],
        dimension_numbers=("NWC", "WIO", "NWC"), feature_group_count=c)
    y = layer_norm(y + b, ln_g, ln_b)
    return jax.nn.silu(y)

def neighbourhood_attention(q, k, v, rpb):
    B, T, H, Dh = q.shape
    rows = T // GRID_W
    kr = min(WIN_R, rows)
    scale = Dh ** -0.5
    band0 = np.clip(np.arange(N_CB) * Q_CB - WIN_C // 2, 0, GRID_W - BAND_C)
    key_col = band0[:, None] + np.arange(BAND_C)
    q_col = np.arange(GRID_W).reshape(N_CB, Q_CB)
    win0 = np.clip(q_col - WIN_C // 2, 0, GRID_W - WIN_C)
    col_mask = ((key_col[:, None, :] >= win0[:, :, None]) &
                (key_col[:, None, :] < win0[:, :, None] + WIN_C))
    dc_idx = np.clip(key_col[:, None, :] - q_col[:, :, None] + WIN_C - 1, 0, 2 * WIN_C - 2)
    rpb_c = rpb[:, :, dc_idx]
    kg = k.reshape(B, rows, GRID_W, H, Dh)
    vg = v.reshape(B, rows, GRID_W, H, Dh)
    qr = jnp.moveaxis(q.reshape(B, rows, N_CB, Q_CB, H, Dh), 1, 0)

    def row_fn(args):
        r, q_row = args
        r0 = jnp.clip(r - kr // 2, 0, rows - kr)
        k_band = lax.dynamic_slice_in_dim(kg, r0, kr, axis=1)[:, :, key_col]
        v_band = lax.dynamic_slice_in_dim(vg, r0, kr, axis=1)[:, :, key_col]
        s = jnp.einsum("bjqhd,bijkhd->bhjqik", q_row, k_band).astype(jnp.float32) * scale
        dr_idx = r0 + jnp.arange(kr) - r + WIN_R - 1
        bias = jnp.transpose(jnp.take(rpb_c, dr_idx, axis=1), (0, 2, 3, 1, 4))
        s = jnp.where(col_mask[:, :, None, :], s + bias.astype(jnp.float32), -jnp.inf)
        w = jax.nn.softmax(s.reshape(B, H, N_CB, Q_CB, kr * BAND_C), axis=-1)
        w = w.reshape(s.shape).astype(v.dtype)
        return jnp.einsum("bhjqik,bijkhd->bjqhd", w, v_band)

    out = lax.map(row_fn, (jnp.arange(rows), qr))
    return jnp.moveaxis(out, 0, 1).reshape(B, T, H * Dh)

def swiglu(x, w1, w3, w2):
    return (jax.nn.silu(x @ w1) * (x @ w3)) @ w2

def moe_swiglu(x, w_router, w1, w3, w2):
    B, T, D = x.shape
    xf = x.reshape(-1, D)
    n = xf.shape[0]
    logits = (xf @ w_router).astype(jnp.float32)
    top_vals, top_idx = lax.top_k(logits, TOP_K)
    gates = jax.nn.softmax(top_vals, axis=-1)
    n_assign = n * TOP_K
    e_flat = top_idx.reshape(-1)
    tok_flat = jnp.repeat(jnp.arange(n, dtype=jnp.int32), TOP_K)
    g_flat = gates.reshape(-1)
    order = jnp.argsort(e_flat)
    e_sorted = e_flat[order]
    tok_sorted = tok_flat[order]
    g_sorted = g_flat[order]
    counts = jnp.bincount(e_flat, length=N_EXPERTS)
    starts = jnp.cumsum(counts) - counts
    padded = (counts + MOE_BLK - 1) // MOE_BLK * MOE_BLK
    pends = jnp.cumsum(padded)
    pstarts = pends - padded
    dest = pstarts[e_sorted] + (jnp.arange(n_assign) - starts[e_sorted])
    n_blocks = -(-n_assign // MOE_BLK) + N_EXPERTS
    n_slots = n_blocks * MOE_BLK
    tok_buf = jnp.zeros((n_slots,), jnp.int32).at[dest].set(tok_sorted)
    gate_buf = jnp.zeros((n_slots,), jnp.float32).at[dest].set(g_sorted)
    block_e = jnp.minimum(
        jnp.searchsorted(pends, jnp.arange(n_blocks) * MOE_BLK, side="right"), N_EXPERTS - 1)

    def block_fn(args):
        tok, e = args
        xb = xf[tok]
        return (jax.nn.silu(xb @ w1[e]) * (xb @ w3[e])) @ w2[e]

    y = lax.map(block_fn, (tok_buf.reshape(n_blocks, MOE_BLK), block_e)).reshape(n_slots, D)
    y = y * gate_buf[:, None].astype(y.dtype)
    out = jax.ops.segment_sum(y, tok_buf, num_segments=n)
    return out.reshape(B, T, D)

def second_inputs(seed: int = 0) -> dict:
    key = jax.random.key(seed)
    ks = jax.random.split(key, 32)
    f32 = jnp.float32
    nrm = lambda k, shape, s: jax.random.normal(k, shape, f32) * s
    gain = lambda k, shape: 1.0 + 0.02 * jax.random.normal(k, shape, f32)
    return {
        "x": jax.random.normal(ks[0], (BATCH, SEQ, D_MODEL), f32),
        "p": jax.random.normal(ks[1], (DEPTH_2, BATCH, SEQ, D_PLE), f32),
        "ln_in_g": gain(ks[2], (D_MODEL,)),
        "ln_in_b": nrm(ks[3], (D_MODEL,), 0.02),
        "w_in": nrm(ks[4], (DEPTH_2, D_MODEL, D_IN), D_MODEL ** -0.5),
        "b_in": nrm(ks[5], (DEPTH_2, D_IN), 0.02),
        "conv_w": nrm(ks[6], (DEPTH_2, CONV_K_2, CONV_CH), CONV_K_2 ** -0.5),
        "conv_b": nrm(ks[7], (DEPTH_2, CONV_CH), 0.02),
        "conv_ln_g": gain(ks[8], (DEPTH_2, CONV_CH)),
        "conv_ln_b": nrm(ks[9], (DEPTH_2, CONV_CH), 0.02),
        "rpb": nrm(ks[10], (DEPTH_2, N_HEADS, 2 * WIN_R - 1, 2 * WIN_C - 1), 0.02),
        "w_out": nrm(ks[11], (DEPTH_2, D_MIX, D_MODEL), D_MIX ** -0.5 * DEEPNORM_BETA),
        "b_out": nrm(ks[12], (DEPTH_2, D_MODEL), 0.02),
        "ln1_g": gain(ks[13], (DEPTH_2, D_MODEL)),
        "ln1_b": nrm(ks[14], (DEPTH_2, D_MODEL), 0.02),
        "ffn_w1": nrm(ks[15], (N_DENSE, D_MODEL, D_FF), D_MODEL ** -0.5),
        "ffn_w3": nrm(ks[16], (N_DENSE, D_MODEL, D_FF), D_MODEL ** -0.5),
        "ffn_w2": nrm(ks[17], (N_DENSE, D_FF, D_MODEL), D_FF ** -0.5 * DEEPNORM_BETA),
        "w_router": nrm(ks[18], (N_MOE, D_MODEL, N_EXPERTS), D_MODEL ** -0.5),
        "moe_w1": nrm(ks[19], (N_MOE, N_EXPERTS, D_MODEL, D_FF_EXPERT), D_MODEL ** -0.5),
        "moe_w3": nrm(ks[20], (N_MOE, N_EXPERTS, D_MODEL, D_FF_EXPERT), D_MODEL ** -0.5),
        "moe_w2": nrm(ks[21], (N_MOE, N_EXPERTS, D_FF_EXPERT, D_MODEL), D_FF_EXPERT ** -0.5 * DEEPNORM_BETA),
        "ple_w": nrm(ks[22], (DEPTH_2, D_PLE, D_MODEL), D_PLE ** -0.5 * DEEPNORM_BETA),
        "ple_gate_w": nrm(ks[23], (DEPTH_2, D_MODEL, D_MODEL), D_MODEL ** -0.5),
        "ple_gate_b": nrm(ks[24], (DEPTH_2, D_MODEL), 0.02),
        "ln2_g": gain(ks[25], (DEPTH_2, D_MODEL)),
        "ln2_b": nrm(ks[26], (DEPTH_2, D_MODEL), 0.02),
    }

def second_block(x, p, ln_in_g, ln_in_b, w_in, b_in, conv_w, conv_b, conv_ln_g, conv_ln_b,
              rpb, w_out, b_out, ln1_g, ln1_b, ffn_w1, ffn_w3, ffn_w2, w_router,
              moe_w1, moe_w3, moe_w2, ple_w, ple_gate_w, ple_gate_b, ln2_g, ln2_b):
    B, T, _ = x.shape
    h = layer_norm(x, ln_in_g, ln_in_b)
    for i in range(DEPTH_2):
        proj = h @ w_in[i] + b_in[i]
        a = proj[..., :CONV_CH]
        g = proj[..., CONV_CH:2 * CONV_CH]
        qkv = proj[..., 2 * CONV_CH:].reshape(B, T, 3, N_HEADS, HEAD_DIM)
        conv_out = conformer_conv(a, g, conv_w[i], conv_b[i], conv_ln_g[i], conv_ln_b[i])
        attn_out = neighbourhood_attention(qkv[:, :, 0], qkv[:, :, 1], qkv[:, :, 2], rpb[i])
        mix = jnp.concatenate([conv_out, attn_out], axis=-1) @ w_out[i] + b_out[i]
        h = layer_norm(DEEPNORM_ALPHA * h + mix, ln1_g[i], ln1_b[i])
        j = i // 2
        if i % 2 == 0:
            f = swiglu(h, ffn_w1[j], ffn_w3[j], ffn_w2[j])
        else:
            f = moe_swiglu(h, w_router[j], moe_w1[j], moe_w3[j], moe_w2[j])
        e = jax.nn.sigmoid(h @ ple_gate_w[i] + ple_gate_b[i]) * (p[i] @ ple_w[i])
        h = layer_norm(DEEPNORM_ALPHA * h + f + e, ln2_g[i], ln2_b[i])
    return h


def setup_inputs(seed=0):
    out = dict(first_inputs(seed))
    for name, value in second_inputs(seed + 1).items():
        if name != "x":
            out[name + "_2"] = value
    return out


def reference(
    x, meta_tokens, norm_pre, w_in, conv_w, conv_b, dt_bias, a_log, d_skip, ssd_norm,
    fgate_bias, gate_bias, w_proj_ssd, w_proj_att, w_out, norm_post, p_2, ln_in_g_2, ln_in_b_2,
    w_in_2, b_in_2, conv_w_2, conv_b_2, conv_ln_g_2, conv_ln_b_2, rpb_2, w_out_2, b_out_2,
    ln1_g_2, ln1_b_2, ffn_w1_2, ffn_w3_2, ffn_w2_2, w_router_2, moe_w1_2, moe_w3_2, moe_w2_2,
    ple_w_2, ple_gate_w_2, ple_gate_b_2, ln2_g_2, ln2_b_2,
):
    x = first_block(
        x, meta_tokens, norm_pre, w_in, conv_w, conv_b, dt_bias, a_log, d_skip, ssd_norm,
        fgate_bias, gate_bias, w_proj_ssd, w_proj_att, w_out, norm_post,
    )
    return second_block(
        x, p_2, ln_in_g_2, ln_in_b_2, w_in_2, b_in_2, conv_w_2, conv_b_2, conv_ln_g_2,
        conv_ln_b_2, rpb_2, w_out_2, b_out_2, ln1_g_2, ln1_b_2, ffn_w1_2, ffn_w3_2, ffn_w2_2,
        w_router_2, moe_w1_2, moe_w3_2, moe_w2_2, ple_w_2, ple_gate_w_2, ple_gate_b_2, ln2_g_2,
        ln2_b_2,
    )


_drawn_inputs = setup_inputs


def setup_inputs(seed=0):
    import zlib

    import numpy as np

    out = dict(_drawn_inputs(seed))
    spreads = {}
    factors = {'b_in_2': 5.729,
     'conv_b_2': 5.953,
     'conv_ln_g_2': 7.331,
     'conv_ln_b_2': 14.11,
     'rpb_2': 64.0,
     'ple_gate_b_2': 25.535,
     'b_out_2': 3.403}
    for name, (base, spread) in spreads.items():
        noise = np.random.default_rng([zlib.crc32(name.encode()), seed]).standard_normal(out[name].shape)
        drawn = base * np.exp(spread * noise) if base else spread * noise
        out[name] = __import__('jax').numpy.asarray(drawn.astype(out[name].dtype))
    for name, factor in factors.items():
        out[name] = (out[name] * factor).astype(out[name].dtype)
    return out
```

```python
import math
from contextlib import ExitStack

import concourse.bass as bass
from concourse import mybir

ALU = mybir.AluOpType
ACT = mybir.ActivationFunctionType
F32 = mybir.dt.float32
I32 = mybir.dt.int32

P = 128
D = 1024
T = 256
NM = 16
TT = T + NM
KB = D // P
EPS = 1e-6
LN_EPS = 1e-5
ALPHA = 4.0 ** 0.25
BIG = 3.0e38
SB0 = 16512

C_ID, C_U, C_T, C_ONE, C_MASK, C_IO = 0, 128, 256, 528, 656, 928
NCONST = 1184

V_PRE, V_CW, V_CB, V_DSK, V_SSDN, V_GB = 0, 8, 104, 128, 144, 160
V_ING, V_INB, V_DTFB, V_SGN, V_ALOG = 176, 184, 192, 193, 194
V_L = 195
VL_BIN, VL_CW, VL_CB, VL_CG, VL_CBT, VL_G1, VL_B1, VL_G2, VL_B2, VL_N = 0, 16, 140, 144, 148, 152, 160, 168, 176, 184
NVEC = V_L + 2 * VL_N


def flat(ws):
    for w in ws:
        if isinstance(w, list):
            yield from flat(w)
        elif w is not None:
            yield w


class Eng:

    def __init__(self, name, sem):
        self.name, self.sem, self.n, self.q, self.seen = name, sem, 0, [], {}
        self.step, self.bodies, self.i, self.lastinc, self.inside = [0], None, 0, None, False

    def wait(self, *toks):
        for t in flat(toks):
            s, v = t[0], t[1]
            if self.seen.get(s.name, 0) < v:
                self.seen[s.name] = v
                if len(t) == 2:
                    self.q.append(lambda e, s=s, v=v: e.wait_ge(s, v))
                else:
                    self.q.append(lambda e, s=s, v=v, k=t[2]: e.wait_ge(s, self.i * k[0] + v))

    def do(self, fn, *toks, inc=True):
        self.wait(*toks)
        if not inc:
            self.q.append(fn)
            return None
        if inc is not True:
            self.q.append(lambda e: fn(e).then_inc(inc, 1))
            return None
        self.n += 1
        add = [1]
        self.lastinc = add
        self.q.append(lambda e: fn(e).then_inc(self.sem, add[0]))
        return self.last()

    def last(self):
        return (self.sem, self.n, self.step) if self.inside else (self.sem, self.n)

    def loop(self):
        self.pre, self.n0, self.bodies, self.inside = self.q, self.n, [], True

    def variant(self):
        self.q, self.n, self.seen = [], self.n0, {}

    def end_variant(self):
        self.bodies.append((self.q, self.n - self.n0, self.lastinc))

    def end_loop(self, iters):
        self.step[0] = max(n for _, n, _ in self.bodies)
        for _, n, add in self.bodies:
            add[0] += self.step[0] - n
        self.q, self.seen, self.inside = [], {}, False
        self.n = self.n0 + iters * self.step[0]

    def start(self):
        return (self.sem, self.n0, self.step)

    def emit(self, e, iters=0, count=None, limits=None):
        if self.bodies is not None:
            for f in self.pre:
                f(e)
            with e.Fori(0, iters) as i:
                self.i = i
                n = e.value_load(count(i), min_val=0, max_val=T)

                def pick(v):
                    if v == len(self.bodies) - 1:
                        for f in self.bodies[v][0]:
                            f(e)
                        return
                    with e.If(n < limits[v] + 1):
                        for f in self.bodies[v][0]:
                            f(e)
                    with e.Else():
                        pick(v + 1)

                pick(0)
        for f in self.q:
            f(e)


class Load:

    def __init__(self, eng, sems):
        self.eng, self.sems, self.count, self.next = eng, sems, {}, 0

    def slot(self):
        s = self.sems[self.next]
        self.next += 1
        return s

    def start(self, sem, dst, src, *toks):
        self.eng.wait(*toks)
        self.count[sem.name] = self.count.get(sem.name, 0) + 16
        self.eng.q.append(lambda e: e.dma_start(dst, src).then_inc(sem, 16))
        return (sem, self.count[sem.name])

    def once(self, dst, src, *toks):
        return self.start(self.slot(), dst, src, *toks)


class Ring:

    def __init__(self, load, slots):
        self.load, self.slots = load, slots
        self.sems = [load.slot() for _ in slots]
        self.plan, self.landed = [], []
        self.taken = self.given = self.issued = 0
        self.back = []

    def issue(self, *toks):
        i = self.issued
        if i >= len(self.plan):
            return
        j = i % len(self.slots)
        k, c, src = self.plan[i]
        dst = self.slots[j][:, 0:k * c].rearrange("p (k c) -> p k c", k=k)
        self.landed.append(self.load.start(self.sems[j], dst, src, *toks))
        self.issued += 1

    def take(self):
        i = self.taken
        self.taken += 1
        k, c, _ = self.plan[i]
        return self.slots[i % len(self.slots)][:, 0:k * c].rearrange("p (k c) -> p k c", k=k), self.landed[i]

    def give(self, tok):
        self.back.append(tok)
        self.issue(tok)


def weave(main, fill, n):
    live = True
    acc = 0.0
    for _ in main:
        acc += n
        while live and acc >= 1.0:
            acc -= 1.0
            live = next(fill, None) is not None
    return live


def run(gen):
    for _ in gen:
        pass


def bass_hybrid_conformer_moe(nc, x, meta, consts, vecs, w_in, norm_post, w_att, w_ssd, w_out, a_log, ln_in_g, ln_in_b,
                              w_in2, b_in2, na_bias, w_out2, b_out2, ln1_g, ln1_b, w1, w3, w2, pT, ple_w, gate_w,
                              gate_b, ln2_g, ln2_b, w_router, mw1, mw3, mw2, out):
    with ExitStack() as ctx:
        def sem(name):
            return ctx.enter_context(nc.semaphore(name))

        PE, VE, AC, GP, SP = (Eng(n, sem("s_" + n)) for n in ("pe", "dve", "act", "pool", "sp"))
        ld = Load(SP, [sem(f"d{i}") for i in range(40)])
        ldg = Load(GP, [sem(f"g{i}") for i in range(40)])
        ps = ctx.enter_context(nc.psum_tensor("ps", [P, 8, 512], F32))
        BF = [[] for _ in range(8)]

        top = [SB0]

        def sb(name, shape, off=None, dt=F32):
            n = 4
            for s in shape[1:]:
                n *= s
            n = (n + 31) // 32 * 32
            if off is None:
                off = top[0]
                top[0] += n
            assert off + n <= 229344, (name, off, n)
            return nc.alloc_sbuf_tensor_at(name, shape, dt, offset=off)

        def mm(o, l, r, start, stop, *w, inc=False):
            return PE.do(lambda e: e.matmul(o, l, r, start=start, stop=stop), *w, inc=inc)

        def tr(o, i, *w, inc=False):
            n = i.shape[0]
            b = i.base_partition() if callable(i.base_partition) else i.base_partition
            return PE.do(lambda e: e.transpose(o, i, ident[b:b + n, b:b + n]), *w, inc=inc)

        def act(o, i, f, *w, bias=0.0, scale=1.0, acc=None):
            if acc is None:
                return AC.do(lambda e: e.activation(o, i, f, bias=bias, scale=scale), *w)
            return AC.do(lambda e: e.activation(o, i, f, bias=bias, scale=scale, accum_out=acc), *w)

        def ts(E, o, i, s1, s2, op0, op1, *w):
            if s2 is None:
                return E.do(lambda e: e.tensor_scalar(o, i, s1, None, op0), *w)
            return E.do(lambda e: e.tensor_scalar(o, i, s1, s2, op0, op1), *w)

        def stt(o, i0, s, i1, op0, op1, *w):
            return VE.do(lambda e: e.scalar_tensor_tensor(out=o, in0=i0, scalar=s, in1=i1, op0=op0, op1=op1), *w)

        def tt(E, o, a, b, op, *w):
            return E.do(lambda e: e.tensor_tensor(o, a, b, op=op), *w)

        def cp(E, o, i, *w):
            if E is AC:
                return act(o, i, ACT.Copy, *w)
            return E.do(lambda e: e.tensor_copy(o, i), *w)

        def ms(E, o, v, *w):
            return E.do(lambda e: e.memset(o, v), *w)

        def rcp(o, i, *w):
            return VE.do(lambda e: e.reciprocal(o, i), *w)

        def neg_max(o, i0, i1, acc, *w):
            return VE.do(lambda e: e.tensor_tensor_reduce(o, i0, i1, -1.0, BIG, ALU.add, ALU.min, acc), *w)

        MUL, ADD, SUB, MAX = ALU.mult, ALU.add, ALU.subtract, ALU.max

        def mark(b, *toks):
            BF[b] = list(toks)

        def take(b):
            w = BF[b]
            BF[b] = []
            return w

        cst = sb("cst", [P, NCONST])
        vec = sb("vec", [P, NVEC])
        small = sb("small", [P, 256])
        tokv = sb("tokv", [P, 3, 48])
        adt = sb("adt", [P, 3, 32])
        dth = sb("dth", [P, 2, 32])
        dsx = sb("dsx", [P, 4, 32])
        ecsT = sb("ecsT", [32, T])
        arow = sb("arow", [P, 32])
        ident = cst[:, C_ID:C_ID + 128]
        strict = cst[:, C_U:C_U + 128]
        tri = cst[:, C_T:C_T + TT]
        ones = cst[:, C_ONE:C_ONE + 128]
        fmask = cst[:, C_MASK:C_MASK + TT]

        def v(c, n=1, p=P):
            return vec[0:p, c:c + n]

        ring = Ring(ld, [sb(f"ring{i}", [P, 4096]) for i in range(3)])
        res = sb("res", [P, 2, D])
        row = [sb(f"row{i}", [P, D]) for i in range(2)]
        W0 = top[0]

        def wk(name, shape, off):
            return sb(name, shape, W0 + off)

        def cols(w, c0, n, k0=0, nk=8):
            ring.plan.append((nk, n, w[k0 * P:(k0 + nk) * P, c0:c0 + n].rearrange("(k p) c -> p k c", p=P)))

        XB, DT, ZA, Q, K, V, FG, GA = 2048, 5120, 5152, 6176, 7200, 8224, 9248, 9264
        for c0, n in ((K, 2), (Q, 2), (V, 2), (XB + 2048, 2), (XB, 4), (0, 4), (ZA, 2), (GA + 1024, 2), (GA, 2)):
            for i in range(n):
                cols(w_in, c0 + 512 * i, 512)
        cols(w_att, 0, 512)
        cols(w_att, 512, 512)
        for c in range(2):
            cols(w_ssd, 512 * c, 512, 0)
            cols(w_ssd, 512 * c, 512, 8)
        cols(w_out, 0, 1024, 0, 4)
        cols(w_out, 0, 1024, 4, 4)

        def layer_plan(l):
            for c0 in (2048, 0, 512, 1024, 1536):
                if c0 == 2048:
                    ring.plan.append((2, 1024, ple_w[l].rearrange("(k p) c -> p k c", p=P)))
                cols(w_in2[l], c0, 512)
            for w in (w_out2[l], gate_w[l]):
                cols(w, 0, 1024, 0, 4)
                cols(w, 0, 1024, 4, 4)

        layer_plan(0)
        for i in range(6):
            n = 512 if i < 5 else 256
            cols(w1, 512 * i, n)
            cols(w3, 512 * i, n)
        for i in range(6):
            cols(w2, 0, 1024, 4 * i, 4 if i < 5 else 2)
        layer_plan(1)

        uT = wk("uT", [P, KB, TT], 0)
        xhat = wk("xhat", [P, 2, D], 8704)
        mhat = wk("mhat", [NM, D], 16896)
        min_ = wk("min_", [NM, D], 20992)
        sq = wk("sqj", [P, D], 25088)
        sp = wk("sp", [48, TT], 29184)
        dx = wk("dx", [48, 6, TT], 30272)
        wdf = wk("wdf", [P, KB, 48], 36800)

        t_x = [ld.once(res[:, h, :], x[0, 128 * h:128 * h + 128, :]) for h in range(2)]
        t_m = ld.once(min_[:, :], meta)
        t_c = ld.once(cst[:, :], consts)
        t_v = ld.once(vec[:, :], vecs)
        s_df = ld.slot()
        ld.start(s_df, wdf[:, :, 0:32], w_in[:, DT:DT + 32].rearrange("(k p) c -> p k c", p=P))
        t_df = ld.start(s_df, wdf[:, :, 32:48], w_in[:, FG:FG + 16].rearrange("(k p) c -> p k c", p=P))
        t_al = ld.once(arow[:, :], a_log.broadcast_to([P, 32]))
        for _ in range(3):
            ring.issue()
        t_np = ld.once(row[0][:, :], norm_post.broadcast_to([P, D]))

        t_half = ms(GP, small[:, 0:1], -0.5)
        t_eps = ms(GP, small[:, 2:3], EPS)

        def rsqrt(o, i, *w):
            n, c = i.shape
            return GP.do(lambda e: e.tensor_tensor(o, i, small[0:n, 0:1].broadcast_to([n, c]), op=ALU.pow), t_half, *w)

        def norm_rows(src, dst, n, i, *w):
            ss, mq, rs = small[0:n, 4 + i:5 + i], small[0:n, 8 + i:9 + i], small[0:n, 12 + i:13 + i]
            t = act(sq[0:n, :], src, ACT.Square, AC.last(), *w, acc=ss)
            t = ts(VE, mq, ss, 1.0 / D, EPS, MUL, ADD, t)
            t = rsqrt(rs, mq, t)
            return ts(VE, dst, src, rs, None, MUL, None, t)

        t_u = []
        for h, src, dst, n, col, t in ((0, res[:, 0, :], xhat[:, 0, :], P, NM, t_x[0]),
                                       (1, res[:, 1, :], xhat[:, 1, :], P, NM + P, t_x[1]),
                                       (2, min_[:, :], mhat[:, :], NM, 0, t_m)):
            t = norm_rows(src, dst, n, h, t)
            for g in range(2):
                b = 2 * h + g
                w = take(b)
                for k in range(4):
                    kk = 4 * g + k
                    tk = tr(ps[:, b, n * k:n * k + n], dst[:, 128 * kk:128 * kk + 128], t, t_c, w, inc=k == 3)
                for k in range(4):
                    kk = 4 * g + k
                    o, i, s = uT[:, kk, col:col + n], ps[:, b, n * k:n * k + n], v(V_PRE + kk)
                    if g:
                        te = act(o, i, ACT.Copy, tk, t_v, scale=s)
                    else:
                        te = ts(VE, o, i, s, None, MUL, None, tk, t_v)
                mark(b, te)
                t_u.append(te)

        b = 6
        w = take(b)
        for k in range(KB):
            tk = mm(ps[0:48, b, 0:TT], wdf[:, k, :], uT[:, k, :], k == 0, k == 7, w, t_df, t_u, inc=k == 7)
        X, E_, S1, S2, R, A6 = (dx[:, i, :] for i in range(6))
        t1 = ts(VE, X, ps[0:48, b, 0:TT], v(V_DTFB, p=48), v(V_SGN, p=48), ADD, MUL, tk, t_v)
        mark(b, t1)
        t2 = stt(S1, X, -1.0, X, MUL, MAX, t1)
        te = act(E_, S1, ACT.Exp, t2, scale=-1.0)
        t3 = ts(VE, S1, E_, 2.0, None, ADD, None, te)
        t4 = rcp(R, S1, t3)
        t5 = tt(VE, S1, E_, R, MUL, t4)
        t6 = tt(VE, S2, S1, S1, MUL, t5)
        t7 = ts(VE, A6, S2, 1.0 / 15, None, MUL, None, t6)
        for n in (13, 11, 9, 7, 5, 3):
            t7 = stt(A6, A6, 1.0 / n, S2, ADD, MUL, t7)
        t7 = stt(A6, A6, 1.0, S1, ADD, MUL, t7)
        t8 = ts(VE, X, X, 0.0, None, MAX, None, t1)
        t_sp = stt(sp[:, :], A6, 2.0, X, MUL, ADD, t7, t8)
        b = 7
        w = take(b)
        for c, (c0, n) in enumerate(((0, NM), (NM, P), (NM + P, P))):
            tk = tr(ps[0:n, b, 48 * c:48 * c + 48], sp[:, c0:c0 + n], t_sp, w, inc=c == 2)
        tv1 = cp(VE, tokv[0:NM, 0, :], ps[0:NM, b, 0:48], tk)
        tv2 = cp(VE, tokv[:, 1:3, :], ps[:, b, 48:144].rearrange("p (c f) -> p c f", c=2), tk)
        mark(b, tv2)
        t_a = act(arow[:, :], arow[:, :], ACT.Exp, t_al)
        for c, n in enumerate((NM, P, P)):
            t_adt = stt(adt[0:n, c, :], tokv[0:n, c, 0:32], -1.0, arow[0:n, :], MUL, MUL, tv1, tv2, t_a)
        t_dth = ts(VE, dth[:, :, :], tokv[:, 1:3, 0:32], 0.5, None, MUL, None, tv2)

        PB = [0]

        def block(wt, tw, c, rhs, n, acts, *extra):
            b = PB[0]
            PB[0] = 1 - b
            w = take(b)
            for k in range(KB):
                tk = mm(ps[:, b, 0:n], wt[:, k, c:c + 128], rhs(k), k == 0, k == KB - 1, w, tw, acts, *extra, inc=k == KB - 1)
            return b, ps[:, b, 0:n], tk

        def u_all(k):
            return uT[:, k, :]

        def u_x(k):
            return uT[:, k, NM:TT]

        xbcT = wk("xbcT", [P, 24, TT], 8704)
        oT = wk("oT", [P, 8, T], 34816)
        qa = wk("qa", [80, 16, T], 43008)
        ka = wk("ka", [80, 16, TT], 59392)
        vt = wk("vt", [P, 3, D], 76800)
        Pb = [wk(f"Pb{i}", [P, 416], 89088 + 1664 * i) for i in range(4)]
        PTb = [wk(f"PTb{i}", [P, 384], 95744 + 1536 * i) for i in range(4)]
        PMb = [wk(f"PMb{i}", [NM, 512], 101888 + 2048 * i) for i in range(2)]
        cacc = [wk(f"cacc{i}", [P, TT], 105984 + 1088 * i) for i in range(3)]
        ctn = [wk(f"ctn{i}", [P, TT], 109248 + 1088 * i) for i in range(2)]
        vtmp = [wk(f"vtmp{i}", [P, TT], 111424 + 1088 * i) for i in range(2)]

        t_oh = GP.do(lambda e: e.tensor_copy(qa[64:80, :, :], ident[64:80, 64:80].unsqueeze(2).broadcast_to([16, 16, T])), t_c)
        b = 6
        w = take(b)
        mm(ps[0:NM, b, 0:TT], tokv[0:NM, 0, 32:48], tri[0:NM, 0:TT], True, False, w, tv1, tv2)
        mm(ps[0:NM, b, NM:TT], tokv[:, 1, 32:48], tri[:, 0:T], False, False)
        tk = mm(ps[0:NM, b, NM + P:TT], tokv[:, 2, 32:48], tri[:, 0:P], False, True, inc=True)
        t_ck = []
        for i in range(4):
            o = ka[64:80, 4 * i:4 * i + 4, :]
            s = ps[0:NM, b, 0:TT].unsqueeze(1).broadcast_to([NM, 4, TT])
            t_ck.append(act(o, s, ACT.Copy, tk))
        mark(b, t_ck[-1])

        t_q, t_k = [None] * 16, [None] * 16
        for dst, rhs, n, sc, tl in ((ka, u_all, TT, 1.0, t_k), (qa, u_x, T, 0.125, t_q)):
            for i in range(2):
                wt, tw = ring.take()
                for j in range(4):
                    b, pb, tk = block(wt, tw, 128 * j, rhs, n, t_u)
                    hd = 8 * i + 2 * j
                    tl[hd] = act(dst[0:64, hd, :], pb[0:64], ACT.Copy, tk, scale=sc)
                    tl[hd + 1] = ts(VE, dst[0:64, hd + 1, :], pb[64:128], sc, None, MUL, None, tk)
                    mark(b, tl[hd], tl[hd + 1])
                ring.give(tk)
        t_vt = []
        use = [None, None]
        for i in range(2):
            wt, tw = ring.take()
            for j in range(4):
                jj = 4 * i + j
                b, pb, tk = block(wt, tw, 128 * j, u_all, TT, t_u)
                te = act(vtmp[jj % 2][:, :], pb, ACT.Copy, tk, use[jj % 2])
                mark(b, te)
                b = 6 + jj % 2
                w = take(b)
                for c, (c0, n) in enumerate(((0, NM), (NM, P), (NM + P, P))):
                    use[jj % 2] = tr(ps[0:n, b, 128 * c:128 * c + 128], vtmp[jj % 2][:, c0:c0 + n], te, w, inc=c == 2)
                ta = cp(VE, vt[0:NM, 0, 128 * jj:128 * jj + 128], ps[0:NM, b, 0:128], use[jj % 2])
                tb = cp(VE, vt[:, 1:3, 128 * jj:128 * jj + 128], ps[:, b, 128:384].rearrange("p (c f) -> p c f", c=2), use[jj % 2])
                mark(b, ta, tb)
                t_vt += [ta, tb]
            ring.give(tk)

        t_xb = [None] * 24

        def xbc():
            rel = [None] * 3
            rel2 = [None] * 2
            n = 0
            for j0 in (16, 20, 0, 4, 8, 12):
                wt, tw = ring.take()
                for j in range(j0, j0 + 4):
                    b, pb, tk = block(wt, tw, 128 * (j - j0), u_all, TT, t_u)
                    a, z = cacc[n % 3], ctn[n % 2]
                    cw = V_CW + 4 * j
                    t = ts(VE, a[:, :], pb, v(cw + 3), v(V_CB + j), MUL, ADD, tk, rel[n % 3])
                    for d in (1, 2, 3):
                        t = stt(a[:, d:TT], pb[:, 0:TT - d], v(cw + 3 - d), a[:, d:TT], MUL, ADD, t)
                    mark(b, t)
                    te = act(z[:, :], a[:, :], ACT.Tanh, t, rel2[n % 2], scale=0.5)
                    t_xb[j] = rel[n % 3] = rel2[n % 2] = stt(xbcT[:, j, :], z[:, :], 1.0, a[:, :], ADD, MUL, te, fr_x)
                    n += 1
                    yield 1
                ring.give(tk)

        t_o = [None] * 8
        nmx = small[:, 32:64]
        rsm = small[:, 64:96]
        riv = small[:, 96:128]

        def fox():
            pn = [None] * 16
            ptt, pmt = [None] * 16, [None] * 8
            trd, od = [None] * 16, [None] * 8
            for st in range(10):
                if st < 8:
                    for h in (2 * st, 2 * st + 1):
                        b = 2 + h % 2
                        w = take(b)
                        mm(ps[:, b, 0:144], qa[:, h, 0:P], ka[:, h, 0:144], True, True, w, t_q[h], t_k[h], t_oh, t_ck[h // 4])
                        tk = mm(ps[:, b, 144:416], qa[:, h, P:T], ka[:, h, :], True, True, inc=True)
                        p = Pb[h % 4]
                        t0 = neg_max(p[:, 0:144], ps[:, b, 0:144], fmask[:, 128:272], nmx[:, 2 * h:2 * h + 1], tk, trd[h - 4] if h > 3 else None)
                        t1 = neg_max(p[:, 144:416], ps[:, b, 144:416], fmask, nmx[:, 2 * h + 1:2 * h + 2], tk)
                        mark(b, t1)
                        e0 = act(p[:, 0:144], p[:, 0:144], ACT.Exp, t0, bias=nmx[:, 2 * h:2 * h + 1], scale=-1.0, acc=rsm[:, 2 * h:2 * h + 1])
                        e1 = act(p[:, 144:416], p[:, 144:416], ACT.Exp, t1, bias=nmx[:, 2 * h + 1:2 * h + 2], scale=-1.0, acc=rsm[:, 2 * h + 1:2 * h + 2])
                        r = rcp(riv[:, 2 * h:2 * h + 2], rsm[:, 2 * h:2 * h + 2], e0, e1)
                        ts(VE, p[:, 0:144], p[:, 0:144], riv[:, 2 * h:2 * h + 1], None, MUL, None, r)
                        pn[h] = ts(VE, p[:, 144:416], p[:, 144:416], riv[:, 2 * h + 1:2 * h + 2], None, MUL, None, r)
                if 1 <= st <= 8:
                    wm = take(6)
                    i = st - 1
                    for h in (2 * i, 2 * i + 1):
                        b = 4 + h % 2
                        w = take(b)
                        p = Pb[h % 4]
                        m0 = 256 * (h % 2)
                        tr(ps[:, b, 0:128], p[:, 16:144], w, pn[h])
                        tr(ps[:, b, 128:256], p[:, 160:288])
                        tk = tr(ps[:, b, 256:384], p[:, 288:416], inc=True)
                        tr(ps[0:NM, 6, m0:m0 + 128], p[:, 0:16], wm)
                        trd[h] = tr(ps[0:NM, 6, m0 + 128:m0 + 256], p[:, 144:160], inc=True)
                        ptt[h] = act(PTb[h % 4][:, :], ps[:, b, 0:384], ACT.Copy, tk, od[i - 2] if i > 1 else None)
                        mark(b, ptt[h])
                    pmt[i] = cp(VE, PMb[i % 2][:, :], ps[0:NM, 6, :], trd[2 * i + 1], od[i - 2] if i > 1 else None)
                    mark(6, pmt[i])
                if st >= 2:
                    i = st - 2
                    w = take(7)
                    for c in range(3):
                        for h in (2 * i, 2 * i + 1):
                            r0 = 64 * (h % 2)
                            o = ps[r0:r0 + 64, 7, 0:T]
                            hs = slice(64 * h, 64 * h + 64)
                            if c == 0:
                                mm(o, vt[:, 1, hs], PTb[h % 4][:, 0:256], True, False, w, ptt[h], t_vt)
                            elif c == 1:
                                mm(o, vt[0:NM, 0, hs], PMb[i % 2][:, 256 * (h % 2):256 * (h % 2) + 256], False, False, pmt[i])
                            else:
                                tk = mm(ps[r0:r0 + 64, 7, P:T], vt[:, 2, hs], PTb[h % 4][:, 256:384], False, True, inc=True)
                    od[i] = tk
                    t_o[i] = act(oT[:, i, :], ps[:, 7, 0:T], ACT.Copy, tk)
                    mark(7, t_o[i])
                yield 1

        fr_x = [t_u, t_sp, tv2]
        f = xbc()
        weave(fox(), f, 2.4)
        run(f)
        t_fox = [PE.last(), VE.last(), AC.last()]

        zT = wk("zT", [P, 16, T], 43008)
        xdt = wk("xdt", [P, 2, 2048], 59392)
        hin = wk("hin", [P, 2, 2048], 75776)
        cbT = wk("cbT", [P, 8, P], 92160)
        Btok = wk("Btok", [P, 512], 96256)
        Bm = wk("Bm", [NM, 512], 98304)
        xds = [wk(f"xds{i}", [P, 512], 100352 + 2048 * i) for i in range(2)]
        adT = [wk(f"adT{i}", [P, 4, P], 104448 + 2048 * i) for i in range(2)]
        Eb = [wk(f"Eb{i}", [P, 4, P], 108544 + 2048 * i) for i in range(2)]
        Mb = [wk(f"Mb{i}", [P, 4, P], 112640 + 2048 * i) for i in range(2)]
        ecB = [wk(f"ecB{i}", [P, 2, T], 116736 + 2048 * i) for i in range(2)]
        t1b = [wk(f"t1b{i}", [P, 2, T], 120832 + 2048 * i) for i in range(2)]
        sqb = [wk(f"sqb{i}", [P, 2, T], 124928 + 2048 * i) for i in range(2)]
        ztn = [wk(f"ztn{i}", [P, T], 129024 + 1024 * i) for i in range(3)]
        gsm = small[0:4, 0:4]
        rst = wk("rst", [4, T], 132096)
        rst2 = wk("rst2", [4, T], 133120)
        t_z = [None] * 16
        t_ya = [None] * 8

        def zproj():
            rel = [None] * 3
            n = 0
            for i in range(6):
                wt, tw = ring.take()
                for j in range(4):
                    jj = 4 * i + j
                    b, pb, tk = block(wt, tw, 128 * j, u_x, T, t_u)
                    z = ztn[n % 3]
                    te = act(z[:, :], pb, ACT.Tanh, tk, rel[n % 3], t_fox, scale=0.5)
                    if jj < 16:
                        t_z[jj] = rel[n % 3] = stt(zT[:, jj, :], z[:, :], 1.0, pb, ADD, MUL, te, t_fox)
                        mark(b, t_z[jj])
                    else:
                        t = stt(z[:, :], z[:, :], 1.0, pb, ADD, MUL, te)
                        mark(b, t)
                        k = jj - 16
                        t_ya[k] = rel[n % 3] = stt(oT[:, k, :], oT[:, k, :], 0.5, z[:, :], MUL, MUL, t, t_o[k])
                    n += 1
                    yield 1
                ring.give(tk)

        t_yd = [None] * 8

        def ssd():
            nb = [0]

            def nxt():
                b = 2 + nb[0] % 5
                nb[0] += 1
                return b, take(b)

            bf3 = lambda ap, n: ap.unsqueeze(2).broadcast_to([n, 8, 64])
            b, w = nxt()
            for c in range(2):
                mm(ps[0:32, b, P * c:P * c + P], adt[:, c + 1, :], tri[:, 0:P], True, True, w, t_adt)
            mm(ps[0:NM, b, 256:288], strict[0:NM, 0:NM], adt[0:NM, 0, :], True, True)
            mm(ps[:, b, 288:320], strict, adt[:, 1, :], True, True)
            tk = mm(ps[:, b, 320:352], ones, adt[:, 1, :], True, True, inc=True)
            t_ecs = act(ecsT[:, :], ps[0:32, b, 0:T], ACT.Exp, tk)
            te0 = act(dsx[0:NM, 0, :], ps[0:NM, b, 256:288], ACT.Exp, tk)
            te1 = act(dsx[:, 1:3, :], ps[:, b, 288:352].rearrange("p (c f) -> p c f", c=2), ACT.Exp, tk)
            mark(b, te1)
            t_d0 = stt(dsx[0:NM, 0, :], tokv[0:NM, 0, 0:32], 0.25, dsx[0:NM, 0, :], MUL, MUL, te0)
            t_d1 = stt(dsx[:, 1, :], tokv[:, 1, 0:32], 0.25, dsx[:, 1, :], MUL, MUL, te1)
            for c in range(2):
                b, w = nxt()
                c0 = NM + P * c
                for g in range(4):
                    tk = mm(ps[:, b, P * g:P * g + P], xbcT[:, 16 + g, c0:c0 + P], xbcT[:, 20 + g, c0:c0 + P], True, True, w, t_xb[16 + g], t_xb[20 + g], inc=g == 3)
                t_cb = stt(cbT[:, 4 * c:4 * c + 4, :], ps[:, b, :].rearrange("p (g s) -> p g s", g=4), 0.25,
                           tri[:, 0:P].unsqueeze(1).broadcast_to([P, 4, P]), MUL, MUL, tk, t_fox)
                mark(b, t_cb)
                yield 1
            b, w = nxt()
            for g in range(4):
                tk = tr(ps[:, b, P * g:P * g + P], xbcT[:, 16 + g, NM:NM + P], w, inc=g == 3)
            t_b1 = act(Btok[:, :], ps[:, b, :], ACT.Copy, tk, t_fox)
            mark(b, t_b1)
            b, w = nxt()
            for g in range(4):
                tk = tr(ps[0:NM, b, P * g:P * g + P], xbcT[:, 16 + g, 0:NM], w, inc=g == 3)
            t_b0 = act(Bm[:, :], ps[0:NM, b, :], ACT.Copy, tk, t_fox)
            mark(b, t_b0)
            yield 1
            rel = [None, None]
            t_xd = [[None] * 4 for _ in range(2)]
            t_h = [[None] * 4 for _ in range(2)]
            n = 0
            for g in range(4):
                gs = slice(512 * g, 512 * g + 512)
                g8 = slice(8 * g, 8 * g + 8)
                for c, (c0, m) in enumerate(((0, NM), (NM, P), (NM + P, P))):
                    b, w = nxt()
                    for j in range(4):
                        tk = tr(ps[0:m, b, P * j:P * j + P], xbcT[:, 4 * g + j, c0:c0 + m], w, t_xb[4 * g + j], inc=j == 3)
                    src = ps[0:m, b, :].rearrange("p (h d) -> p h d", h=8)
                    if c > 0:
                        t = tt(VE, xdt[:, c - 1, gs].rearrange("p (h d) -> p h d", h=8), src, bf3(dth[:, c - 1, g8], P), MUL, tk, t_fox, t_dth)
                        t_xd[c - 1][g] = t
                        mark(b, t)
                    if c < 2:
                        xd = xds[n % 2]
                        t = tt(VE, xd[0:m, :].rearrange("p (h d) -> p h d", h=8), src, bf3(dsx[0:m, c, g8], m), MUL, tk, rel[n % 2], t_d0, t_d1, t_fox)
                        mark(b, t)
                        b, w = nxt()
                        bt = Bm if c == 0 else Btok
                        rel[n % 2] = tk = mm(ps[:, b, :], bt[0:m, P * g:P * g + P], xd[0:m, :], True, True, w, t, t_b0, t_b1, inc=True)
                        n += 1
                        if c == 0:
                            t_h[0][g] = act(hin[:, 0, gs], ps[:, b, :], ACT.Copy, tk, t_fox)
                            mark(b, t_h[0][g])
                        else:
                            t = tt(VE, hin[:, 1, gs].rearrange("p (h d) -> p h d", h=8), hin[:, 0, gs].rearrange("p (h d) -> p h d", h=8), bf3(dsx[:, 2, g8], P), MUL, t_h[0][g], te1, t_fox)
                            t_h[1][g] = tt(VE, hin[:, 1, gs], hin[:, 1, gs], ps[:, b, :], ADD, t, tk)
                            mark(b, t_h[1][g])
                yield 1
            ta = [[None, None] for _ in range(9)]
            tM = [None, None]
            yrel = [None, None]
            wsum = take(7)
            sqt = []

            def prep(q):
                for c in range(2):
                    o = adT[c]
                    ta[q][c] = tt(GP, o[:, :, :], tri[:, 0:P].unsqueeze(1).broadcast_to([P, 4, P]),
                                  adt[:, c + 1, 4 * q:4 * q + 4].unsqueeze(2).broadcast_to([P, 4, P]), MUL, t_adt, t_fox, segd[c])

            segd = [None, None]
            Mrd = [None, None]
            prep(0)

            def sums(q):
                for j in range(2):
                    i = 2 * q + j
                    mm(ps[0:4, 7, 0:T], gsel[:, i // 4, :], sqb[q % 2][:, j, :], i == 0, i == 15, wsum, sqt[q], inc=(i % 2 == 1))
                return PE.last()

            srd = [None, None]
            for q in range(8):
                g = q // 2
                tm = [None, None]
                for c in range(2):
                    b = 2 + c
                    w = take(b)
                    segd[c] = tk = mm(ps[:, b, :], strict, adT[c][:, :, :].rearrange("p h l -> p (h l)"), True, True, w, ta[q][c], inc=True)
                    te = act(Eb[c][:, :, :].rearrange("p h l -> p (h l)"), ps[:, b, :], ACT.Exp, tk, tM[c], t_fox)
                    mark(b, te)
                    tM[c] = tm[c] = tt(VE, Mb[c][:, :, :], Eb[c][:, :, :], cbT[:, 4 * c + g:4 * c + g + 1, :].broadcast_to([P, 4, P]), MUL, te, t_cb, Mrd[c])
                if q < 7:
                    prep(q + 1)
                w = take(5)
                for j in range(2):
                    i = 2 * q + j
                    for c in range(2):
                        c0 = NM + P * c
                        ty = mm(ps[:, 5, 256 * j + P * c:256 * j + P * c + P], hin[:, c, P * i:P * i + P], xbcT[:, 20 + g, c0:c0 + P], True, True, w, t_h[c][g], inc=(j == 1 and c == 1))
                w = take(6)
                for j in range(2):
                    for r in range(2):
                        h = 4 * q + 2 * j + r
                        te = mm(ps[64 * r:64 * r + 64, 6, 256 * j:256 * j + 256], ident[0:32, h:h + 1].broadcast_to([32, 64]), ecsT[:, :], True, True, w, t_ecs, inc=j == 1 and r == 1)
                tb = act(ecB[q % 2][:, :, :].rearrange("p j t -> p (j t)"), ps[:, 6, :], ACT.Copy, te, yrel[q % 2], t_fox)
                mark(6, tb)
                yield 1
                w = take(4)
                for c in range(2):
                    for j in range(2):
                        for r in range(2):
                            h = 4 * q + 2 * j + r
                            tk = mm(ps[64 * r:64 * r + 64, 4, 256 * j + P * c:256 * j + P * c + P], xdt[:, c, 64 * h:64 * h + 64], Mb[c][:, 2 * j + r, :], True, True, w, tm[c], t_xd[c][g], inc=(j == 1 and r == 1))
                    Mrd[c] = tk
                f2 = lambda a: a[:, :, :].rearrange("p j t -> p (j t)")
                y = t1b[q % 2]
                t = stt(f2(y), ps[:, 5, :], 0.5, f2(ecB[q % 2]), MUL, MUL, ty, tb, srd[q % 2], t_fox)
                mark(5, t)
                yrel[q % 2] = t
                t = tt(VE, f2(y), f2(y), ps[:, 4, :], ADD, t, tk)
                mark(4, t)
                for j in range(2):
                    i = 2 * q + j
                    t2 = stt(y[:, j, :], xbcT[:, i, NM:TT], dskh[:, i:i + 1], y[:, j, :], MUL, ADD, t)
                zq = zT[:, 2 * q:2 * q + 2, :].rearrange("p j t -> p (j t)")
                t = stt(zq, f2(y), 0.5, zq, MUL, MUL, t2, t_z[2 * q], t_z[2 * q + 1])
                srd[q % 2] = t
                sqt.append(act(f2(sqb[q % 2]), zq, ACT.Square, t, sqrd[q % 2], t_fox))
                t_yd[q] = sqt[q]
                if q > 0:
                    sqrd[(q - 1) % 2] = sums(q - 1)
                yield 1
            sqrd[1] = sums(7)

        sqrd = [None, None]
        gsel = wk("gsel", [P, 4, 4], 134144)
        dskh = small[:, 128:144]
        t = ms(GP, gsel[:, :, :], 0.0, t_fox)
        for g in range(4):
            t = ms(GP, gsel[:, g, g:g + 1], 1.0, t)
        t_gs = t
        PE.wait(t_gs)
        t_dk = ts(VE, dskh, v(V_DSK, 16), 0.5, None, MUL, None, t_v)
        VE.wait(t_dk)
        f = zproj()
        weave(ssd(), f, 24.0 / 23)
        run(f)

        t_ssd = [PE.last(), VE.last(), AC.last(), GP.last()]
        t = act(rst[:, :], ps[0:4, 7, 0:T], ACT.Sqrt, sqrd[1], t_eps, scale=1.0 / 512, bias=small[0:4, 2:3])
        mark(7, t)
        t_rs = rcp(rst2[:, :], rst[:, :], t)

        gT = wk("gT", [P, 16, T], 59392)
        gbh = small[:, 144:160]
        t_gb = ts(VE, gbh, v(V_GB, 16), 0.5, None, MUL, None, t_v)
        t_g = [None] * 16
        for i in range(4):
            wt, tw = ring.take()
            for j in range(4):
                jj = 4 * i + j
                b, pb, tk = block(wt, tw, 128 * j, u_x, T, t_u)
                sl = (jj + 8) % 16
                t_g[jj] = act(gT[:, jj, :], pb, ACT.Tanh, tk, t_ssd, t_gb, bias=gbh[:, sl:sl + 1], scale=0.5)
                mark(b, t_g[jj])
            ring.give(tk)
            if i == 0:
                w2_, w3_ = take(2), take(3)
                for g in range(4):
                    tk = mm(ps[:, 2 + g // 2, 256 * (g % 2):256 * (g % 2) + 256], ident[0:4, g:g + 1].broadcast_to([4, P]), rst2[:, :], True, True, w2_, w3_, t_rs, inc=True)
                t_y = [None] * 16
                for k in range(16):
                    g = k // 4
                    t_y[k] = stt(zT[:, k, :], zT[:, k, :], v(V_SSDN + k), ps[:, 2 + g // 2, 256 * (g % 2):256 * (g % 2) + 256], MUL, MUL, tk, t_yd[k // 2])
                mark(2, t_y[15])
                mark(3, t_y[15])

        for i in range(2):
            wt, tw = ring.take()
            for j in range(4):
                jj = 4 * i + j
                b, pb, tk = block(wt, tw, 128 * j, lambda k: oT[:, k, :], T, t_ya)
                t_g[jj] = stt(gT[:, jj, :], gT[:, jj, :], 1.0, pb, ADD, MUL, tk, t_g[jj])
                mark(b, t_g[jj])
            ring.give(tk)
        t_mg = [None] * 8
        for i in range(2):
            wa, ta_ = ring.take()
            wb, tb_ = ring.take()
            for j in range(4):
                jj = 4 * i + j
                b = PB[0]
                PB[0] = 1 - b
                w = take(b)
                for k in range(16):
                    wt = wa if k < 8 else wb
                    tk = mm(ps[:, b, 0:T], wt[:, k % 8, 128 * j:128 * j + 128], zT[:, k, :], k == 0, k == 15, w, ta_, tb_, t_y[k], inc=k == 15)
                t = stt(gT[:, 8 + jj, :], gT[:, 8 + jj, :], 1.0, ps[:, b, 0:T], ADD, MUL, tk, t_g[8 + jj])
                mark(b, t)
                t_mg[jj] = tt(GP, gT[:, jj, :], gT[:, jj, :], gT[:, 8 + jj, :], ADD, t, t_g[jj])
            ring.give(tk)
            ring.give(tk)
        t_b1 = [PE.last(), VE.last(), AC.last()]

        hT = [wk(f"hT{i}", [P, KB, T], 8192 * i) for i in range(2)]
        xn = wk("xn", [P, 2, D], 16384)
        R = [wk(f"R{i}", [P, D], 24576 + 4096 * i) for i in range(6)]
        acc = wk("acc", [P, 2, D], 49152)
        lst = small[:, 160:184].rearrange("p (h f) -> p h f", h=2)
        lmv = small[:, 184:192].rearrange("p (h f) -> p h f", h=2)

        def ln_stats(src, h, n, *w):
            st, mv = lst[:, h, 0:6 * n], lmv[:, h, :]
            for i in range(n):
                t = VE.do(lambda e, i=i, x=src(i): e.bn_stats(st[:, 6 * i:6 * i + 6], x), *w)
            t = VE.do(lambda e: e.bn_aggr(mv[:, 0:2], st), t)
            t = ts(VE, mv[:, 2:3], mv[:, 1:2], LN_EPS, None, ADD, None, t)
            return rsqrt(mv[:, 3:4], mv[:, 2:3], t)

        def ln_a(src, h, grow, brow, dst, trow, *w):
            t = ln_stats(lambda i: src[:, 512 * i:512 * i + 512], h, 2, *w)
            tx = ts(VE, xn[:, h, :], src, lmv[:, h, 0:1], lmv[:, h, 3:4], SUB, MUL, t)
            t = tt(GP, dst, xn[:, h, :], grow, MUL, tx, trow)
            t = tt(GP, dst, dst, brow, ADD, t)
            return tx, t

        def ln_b(h, dT, gv, bv, b0, tx):
            out_t = []
            for g in range(2):
                b = b0 + g
                w = take(b)
                for k in range(4):
                    kk = 4 * g + k
                    tk = tr(ps[:, b, P * k:P * k + P], xn[:, h, P * kk:P * kk + P], tx, w, inc=k == 3)
                for k in range(4):
                    kk = 4 * g + k
                    o, i = dT[:, kk, P * h:P * h + P], ps[:, b, P * k:P * k + P]
                    if g:
                        te = act(o, i, ACT.Identity, tk, scale=v(gv + kk), bias=v(bv + kk))
                    else:
                        te = ts(VE, o, i, v(gv + kk), v(bv + kk), MUL, ADD, tk)
                    out_t.append(te)
                mark(b, te)
            return out_t

        def rows(W2, lhs, b, h, tw, tl, n=2, nk=8, k0=0, first=True, last=True):
            for j in range(n):
                w = take(b + j) if first else None
                for k in range(nk):
                    tk = mm(ps[:, b + j, :], lhs(k0 + k)[:, P * h:P * h + P], W2(k0 + k)[:, 512 * j:512 * j + 512],
                            first and k == 0, last and k == nk - 1, w, tw, tl, inc=k == nk - 1)
            return tk

        t_ig = ldg.once(row[1][:, :], ln_in_g.broadcast_to([P, D]))
        t_ib = ldg.once(R[0][:, :], ln_in_b.broadcast_to([P, D]), t_ssd)
        wa, ta_ = ring.take()
        wb, tb_ = ring.take()
        WO = lambda k: (wa if k < 4 else wb)[:, k % 4, :]
        t_hT, t_h = [None, None], [None, None]
        tw_o = [rows(WO, lambda k: gT[:, k, :], 2 + 2 * h, h, [ta_, tb_], t_mg) for h in range(2)]
        ring.give(tw_o[1])
        ring.give(tw_o[1])
        t_xn = [None, None]
        for h in range(2):
            b = 2 + 2 * h
            src = ps[:, b:b + 2, :].rearrange("p j f -> p (j f)")
            ss, mq, rs = small[:, 20 + h:21 + h], small[:, 22 + h:23 + h], small[:, 24 + h:25 + h]
            t = act(acc[:, h, :], src, ACT.Square, tw_o[h], t_b1, acc=ss)
            t = ts(VE, mq, ss, 0.25 / D, EPS, MUL, ADD, t)
            t = rsqrt(rs, mq, t)
            t = stt(acc[:, h, :], src, rs, row[0][:, :], MUL, MUL, t, t_np)
            mark(b, t)
            mark(b + 1, t)
            t = stt(res[:, h, :], acc[:, h, :], 0.5, res[:, h, :], MUL, ADD, t)
            t_xn[h], t_h[h] = ln_a(res[:, h, :], h, row[1][:, :], R[0][:, :], res[:, h, :], [t_ig, t_ib], t, t_b1)
        t_row = [t_np, t_ig]

        plev = wk("plev", [P, 2, D], 59392)
        upad = wk("upad", [P, 4, 286], 67584)
        yb = wk("yb", [P, 4, T], 72160)
        qT = wk("qT", [P, 4, T], 76256)
        kT = wk("kT", [P, 4, T], 80352)
        vk = wk("vk", [P, 2, 512], 84448)
        et = wk("et", [P, 2, D], 0)
        aT = wk("aT", [P, 22, T], 67584)
        na = wk("na", [P, 2, 8, T], 90112)
        mixT = wk("mixT", [P, 8, T], 106496)
        Pn = [wk(f"Pn{i}", [P, 2, T], 114688 + 2048 * i) for i in range(4)]
        PTn = [wk(f"PTn{i}", [P, 2, T], 122880 + 2048 * i) for i in range(4)]
        tmp = [wk(f"tmp{i}", [P, T], 131072 + 1024 * i) for i in range(3)]
        pTs = wk("pTs", [P, 2, T], 134144)
        free_na = t_ssd
        free_row = [None] * 2
        free_R = [t_h, None, None, None, None, None]
        free_p = t_ssd
        t_res = t_h

        rb = [0]

        def rt(name, shape, dt=F32):
            n = 4
            for d in shape[1:]:
                n *= d
            o = W0 + 57344 + rb[0]
            rb[0] += (n + 31) // 32 * 32
            assert rb[0] <= 2048
            return sb(name, shape, o, dt)

        wr = rt("wr", [P, KB, 8])
        tab = rt("tab", [P, 8, 4])
        cnt = rt("cnt", [1, 8], I32)
        cur = rt("cur", [P, 4])
        lg = rt("lg", [P, 2, 8])
        m8 = rt("m8", [P, 2, 8])
        ixf = rt("ixf", [P, 2, 8])
        ix = rt("ix", [P, 2, 8], mybir.dt.uint32)
        gv = rt("gv", [P, 2, 4])
        sel = rt("sel", [P, 2, 8])
        g2 = rt("g2", [P, 2, 8])
        t_wr = ldg.once(wr[:, :, :], w_router.rearrange("(k p) c -> p k c", p=P), t_ssd)

        def route(t_in, t_free):
            io8 = cst[:, C_IO:C_IO + 8]
            b = 0
            w = take(b)
            for h in range(2):
                for k in range(KB):
                    tk = mm(ps[:, b, 8 * h:8 * h + 8], hT[1][:, k, P * h:P * h + P], wr[:, k, :], k == 0, k == 7, w, t_in, t_wr, inc=k == 7)
            tl = cp(VE, lg[:, :, :], ps[:, b, 0:16].rearrange("p (h e) -> p h e", h=2), tk, t_free)
            mark(b, tl)
            ts_ = []
            for h in range(2):
                t = VE.do(lambda e, h=h: e.max(out=m8[:, h, :], in_=lg[:, h, :]), tl)
                t = VE.do(lambda e, h=h: e.max_index(out=ix[:, h, :], in_max=m8[:, h, :], in_values=lg[:, h, :]), t)
                t = cp(VE, ixf[:, h, :], ix[:, h, :], t)
                tm = tt(VE, gv[:, h, 0:1], m8[:, h, 1:2], m8[:, h, 0:1], SUB, t)
                te = act(gv[:, h, 1:2], gv[:, h, 0:1], ACT.Exp, tm)
                tm = ts(VE, gv[:, h, 2:3], gv[:, h, 1:2], 1.0, None, ADD, None, te)
                tm = rcp(gv[:, h, 2:3], gv[:, h, 2:3], tm)
                tm = tt(VE, gv[:, h, 3:4], gv[:, h, 1:2], gv[:, h, 2:3], MUL, tm)
                ta = ts(VE, sel[:, h, :], io8, ixf[:, h, 0:1], None, ALU.is_equal, None, t)
                ts_.append(stt(sel[:, h, :], io8, ixf[:, h, 1:2], sel[:, h, :], ALU.is_equal, ADD, ta))
                ta = ts(VE, g2[:, h, :], io8, ixf[:, h, 0:1], gv[:, h, 2:3], ALU.is_equal, MUL, tm)
                tb = ts(VE, lg[:, h, :], io8, ixf[:, h, 1:2], gv[:, h, 3:4], ALU.is_equal, MUL, tm)
                tg = tt(VE, tab[:, :, 2 + h:3 + h].rearrange("p e o -> p (e o)"), g2[:, h, :], lg[:, h, :], ADD, ta, tb)
            b = 1
            w = take(b)
            mm(ps[:, b, 0:8], tri[:, 0:P], sel[:, 0, :], True, True, w, ts_)
            mm(ps[:, b, 8:16], tri[:, 0:P], sel[:, 1, :], True, False)
            mm(ps[:, b, 8:16], ones, sel[:, 0, :], False, True)
            mm(ps[:, b, 16:24], ones, sel[:, 0, :], True, False)
            tk = mm(ps[:, b, 16:24], ones, sel[:, 1, :], False, True, inc=True)
            t = tt(VE, sel[:, :, :], sel[:, :, :], ps[:, b, 0:16].rearrange("p (h e) -> p h e", h=2), MUL, tk)
            tc = cp(VE, cnt[:, :], ps[0:1, b, 16:24], tk)
            mark(b, tc, t)
            tp = ts(VE, tab[:, :, 0:2].rearrange("p e h -> p h e"), sel[:, :, :], -1.0, None, ADD, None, t)
            return [tc, tp, tg]

        def bc(dst, src, n, *w):
            return ldg.once(dst[:, 0:n], src.broadcast_to([P, n]), *w)

        for l in range(2):
            vo = V_L + VL_N * l
            hin_, h1T = hT[0], hT[1]
            t_bv = bc(R[1], b_in2[l:l + 1, 2048:2560], 512, free_R[1])
            t_na = ldg.once(na[:, :, :, :], na_bias[l], free_na)
            t_bo = bc(R[2], b_out2[l:l + 1, :], D, free_R[2])
            t_pT = ldg.once(pTs[:, :, :], pT[l].rearrange("(k p) t -> p k t", p=P), free_p)
            t_gbr = bc(R[3], gate_b[l:l + 1, :], D, free_R[3])
            t_l1 = [bc(R[4], ln1_g[l:l + 1, :], D, free_R[4]), bc(R[5], ln1_b[l:l + 1, :], D, free_R[5])]
            wt, tw = ring.take()
            t_pl = [None, None]
            for h in range(2):
                b = 2 + 2 * h
                tk = rows(lambda k: wt[:, k, :], lambda k: pTs[:, k, :], b, h, [tw, t_pT], None, nk=2)
                t_pl[h] = act(plev[:, h, :], ps[:, b:b + 2, :].rearrange("p j f -> p (j f)"), ACT.Copy, tk, free_p)
                mark(b, t_pl[h])
                mark(b + 1, t_pl[h])
            ring.give(tk)
            free_p = tk
            wt, tw = ring.take()
            t_v = []
            for h in range(2):
                t_hT[h] = ln_b(h, hin_, V_ING if l == 0 else V_L + VL_G2, V_INB if l == 0 else V_L + VL_B2, 6, t_xn[h])
                tk = rows(lambda k: wt[:, k, :], lambda k: hin_[:, k, :], 2 + h, h, tw, t_hT[h], n=1)
                t_v.append(tt(VE, vk[:, h, :], ps[:, 2 + h, :], R[1][:, 0:512], ADD, tk, t_bv))
                mark(2 + h, t_v[h])
            ring.give(tk)
            free_R[1] = t_v
            t_ac = []
            for h in range(2):
                t = ts(GP, acc[:, h, :], res[:, h, :], ALPHA, None, MUL, None, t_h[h])
                t_ac.append(tt(GP, acc[:, h, :], acc[:, h, :], R[2][:, :], ADD, t, t_bo))
            free_R[2] = t_ac
            bgh, bq8 = small[:, 192 + 8 * l:196 + 8 * l], small[:, 196 + 8 * l:200 + 8 * l]
            t_bg = ts(VE, bgh, v(vo + VL_BIN + 4, 4), 0.5, None, MUL, None)
            t_bq = ts(VE, bq8, v(vo + VL_BIN + 8, 4), 0.125, None, MUL, None)
            h_all = lambda k: hin_[:, k, :]
            ta_, tb_ = None, None
            wa, ta_ = ring.take()
            wb, tb_ = ring.take()
            if l == 0:
                tz = [ms(GP, upad[:, :, 0:15], 0.0, t_b1), ms(GP, upad[:, :, 271:286], 0.0)]
            else:
                tz = [ms(GP, upad[:, :, 0:15], 0.0, t_act), ms(GP, upad[:, :, 271:286], 0.0)]
            t_uu = []
            trel = [None] * 3
            for j in range(4):
                b, pb, tk = block(wa, ta_, 128 * j, h_all, T, t_hT)
                a_ = act(yb[:, j, :], pb, ACT.Identity, tk, bias=v(vo + VL_BIN + j))
                mark(b, a_)
                b, pb, tk = block(wb, tb_, 128 * j, h_all, T, t_hT)
                g_ = act(tmp[j % 3][:, :], pb, ACT.Tanh, tk, t_bg, trel[j % 3], bias=bgh[:, j:j + 1], scale=0.5)
                mark(b, g_)
                trel[j % 3] = stt(upad[:, j, 15:271], tmp[j % 3][:, :], 1.0, yb[:, j, :], ADD, MUL, a_, g_, tz)
                t_uu.append(trel[j % 3])
            ring.give(tk)
            ring.give(tk)
            t_y = [None] * 4

            def conv():
                for j in range(4):
                    cw = vo + VL_CW + 31 * j
                    t = ts(VE, yb[:, j, :], upad[:, j, 0:T], v(cw), None, MUL, None, t_uu[j])
                    for d in range(1, 31):
                        t = stt(yb[:, j, :], upad[:, j, d:d + T], v(cw + d), yb[:, j, :], MUL, ADD, t)
                        if d % 4 == 0:
                            yield 1
                    t_y[j] = act(yb[:, j, :], yb[:, j, :], ACT.Identity, t, scale=0.5, bias=v(vo + VL_CB + j))
                    yield 1

            t_q, t_k = [None] * 4, [None] * 4
            t_mix = [None] * 8

            def qk():
                for dst, tl, bias, sc in ((qT, t_q, bq8, 0.125), (kT, t_k, v(vo + VL_BIN + 12, 4), 1.0)):
                    wt, tw = ring.take()
                    for j in range(4):
                        b, pb, tk = block(wt, tw, 128 * j, h_all, T, t_hT)
                        tl[j] = act(dst[:, j, :], pb, ACT.Identity, tk, t_bq, bias=bias[:, j:j + 1], scale=sc)
                        mark(b, tl[j])
                        yield 1
                    ring.give(tk)

            def nattn():
                pn, ptt, trd, od = [None] * 8, [None] * 8, [None] * 8, [None] * 4
                for st in range(6):
                    if st < 4:
                        for h in (2 * st, 2 * st + 1):
                            b, r = 2 + h % 2, 64 * (h % 2)
                            w = take(b)
                            for t in range(2):
                                tk = mm(ps[:, b, T * t:T * t + T], qT[r:r + 64, st, P * t:P * t + P], kT[r:r + 64, st, :], True, True, w, t_q[st], t_k[st], inc=t == 1)
                            p = Pn[h % 4]
                            c = 2 * h
                            es = []
                            for t in range(2):
                                tm = neg_max(p[:, t, :], ps[:, b, T * t:T * t + T], na[:, t, h, :], nmx[:, c + t:c + t + 1], tk, t_na, trd[h - 4] if h > 3 else None, t_ssd)
                                es.append(act(p[:, t, :], p[:, t, :], ACT.Exp, tm, bias=nmx[:, c + t:c + t + 1], scale=-1.0, acc=rsm[:, c + t:c + t + 1]))
                            mark(b, tm)
                            rr = rcp(riv[:, c:c + 2], rsm[:, c:c + 2], es)
                            for t in range(2):
                                pn[h] = ts(VE, p[:, t, :], p[:, t, :], riv[:, c + t:c + t + 1], None, MUL, None, rr)
                    if 1 <= st <= 4:
                        for h in (2 * st - 2, 2 * st - 1):
                            b = 4 + h % 2
                            w = take(b)
                            for kb in range(2):
                                for t in range(2):
                                    trd[h] = tr(ps[:, b, T * kb + P * t:T * kb + P * t + P], Pn[h % 4][:, t, P * kb:P * kb + P], w, pn[h], inc=kb + t == 2)
                            ptt[h] = act(PTn[h % 4][:, :, :].rearrange("p k t -> p (k t)"), ps[:, b, :], ACT.Copy, trd[h], od[h // 2 - 2] if h > 3 else None, t_ssd)
                            mark(b, ptt[h])
                    if st >= 2:
                        i = st - 2
                        w = take(7)
                        for kb in range(2):
                            for h in (2 * i, 2 * i + 1):
                                r = 64 * (h % 2)
                                tk = mm(ps[r:r + 64, 7, 0:T], vk[:, kb, 64 * h:64 * h + 64], PTn[h % 4][:, kb, :], kb == 0, kb == 1, w, ptt[h], t_v, inc=kb == 1)
                        od[i] = tk
                        t_mix[4 + i] = act(mixT[:, 4 + i, :], ps[:, 7, 0:T], ACT.Copy, tk, t_ssd, scale=2.0)
                        mark(7, t_mix[4 + i])
                    yield 1
                return

            def chain():
                yield from qk()
                yield from nattn()

            f = conv()
            weave(chain(), f, 2.3)
            run(f)
            free_na = VE.last()
            t_m = [None, None]
            for h in range(2):
                w = take(6)
                for j in range(4):
                    tk = tr(ps[:, 6, P * j:P * j + P], yb[:, j, P * h:P * h + P], w, t_y[j], inc=j == 3)
                t = ln_stats(lambda i: ps[:, 6, :], h, 1, tk)
                tx = ts(VE, xn[:, h, 0:512], ps[:, 6, :], lmv[:, h, 0:1], lmv[:, h, 3:4], SUB, MUL, t, t_h[h])
                mark(6, tx)
                w = take(6)
                for j in range(4):
                    tk = tr(ps[:, 6, P * j:P * j + P], xn[:, h, P * j:P * j + P], w, tx, inc=j == 3)
                for j in range(4):
                    tz_ = act(xn[:, h, 512 + P * j:640 + P * j], ps[:, 6, P * j:P * j + P], ACT.Identity, tk, scale=v(vo + VL_CG + j), bias=v(vo + VL_CBT + j))
                mark(6, tz_)
                t = act(xn[:, h, 0:512], xn[:, h, 512:1024], ACT.Tanh, tz_, scale=0.5)
                t_m[h] = stt(mixT[:, 0:4, P * h:P * h + P], xn[:, h, 0:512].rearrange("p (j t) -> p j t", j=4), 1.0,
                             xn[:, h, 512:1024].rearrange("p (j t) -> p j t", j=4), ADD, MUL, t)
            wa, ta_ = ring.take()
            wb, tb_ = ring.take()
            WO = lambda k: (wa if k < 4 else wb)[:, k % 4, :]
            tk2 = [rows(WO, lambda k: mixT[:, k, :], 2 + 2 * h, h, [ta_, tb_], [t_m, t_mix]) for h in range(2)]
            ring.give(tk2[1])
            ring.give(tk2[1])
            for h in range(2):
                b = 2 + 2 * h
                t = stt(res[:, h, :], ps[:, b:b + 2, :].rearrange("p j f -> p (j f)"), 0.5, acc[:, h, :], MUL, ADD, tk2[h], t_ac)
                mark(b, t)
                mark(b + 1, t)
                t_xn[h], t_h[h] = ln_a(res[:, h, :], h, R[4][:, :], R[5][:, :], res[:, h, :], t_l1, t, t_m[h])
            free_R[4] = free_R[5] = t_h
            t_l2 = [bc(row[0], ln2_g[l:l + 1, :], D, t_row[0], VE.last(), GP.last()), bc(row[1], ln2_b[l:l + 1, :], D, GP.last())]
            wa, ta_ = ring.take()
            wb, tb_ = ring.take()
            t_e = [None, None]
            t_w2 = [tk2[1], VE.last(), AC.last()]
            for h in range(2):
                b = 2 + 2 * h
                t_hT[h] = ln_b(h, h1T, vo + VL_G1, vo + VL_B1, 6, t_xn[h])
                if l == 1 and h == 1:
                    t_route = route(t_hT, t_w2)
                tk = rows(WO, lambda k: h1T[:, k, :], b, h, [ta_, tb_], t_hT[h])
                t = tt(VE, et[:, h, :], ps[:, b:b + 2, :].rearrange("p j f -> p (j f)"), R[3][:, :], ADD, tk, t_gbr)
                mark(b, t)
                mark(b + 1, t)
                free_R[3] = t
                t = act(et[:, h, :], et[:, h, :], ACT.Tanh, t, scale=0.5)
                t = stt(et[:, h, :], et[:, h, :], 1.0, plev[:, h, :], ADD, MUL, t, t_pl[h])
                ta = ts(GP, acc[:, h, :], res[:, h, :], ALPHA, None, MUL, None, t_h[h])
                t_e[h] = stt(acc[:, h, :], et[:, h, :], 0.5, acc[:, h, :], MUL, ADD, t, ta)
            ring.give(tk)
            ring.give(tk)
            if l == 1:
                break
            h1 = lambda k: h1T[:, k, :]
            t_a = [None] * 22
            trel = [None] * 3
            jj = 0
            for i in range(6):
                wa, ta_ = ring.take()
                wb, tb_ = ring.take()
                for j in range(4 if i < 5 else 2):
                    b1, p1, tk1 = block(wa, ta_, 128 * j, h1, T, t_hT)
                    z = tmp[jj % 3]
                    t = act(z[:, :], p1, ACT.Silu, tk1, trel[jj % 3])
                    mark(b1, t)
                    b3, p3, tk3 = block(wb, tb_, 128 * j, h1, T, t_hT)
                    t_a[jj] = trel[jj % 3] = tt(VE, aT[:, jj, :], z[:, :], p3, MUL, t, tk3, t_e)
                    mark(b3, t_a[jj])
                    jj += 1
                ring.give(tk3)
                ring.give(tk3)
            at = lambda k: aT[:, k, :]
            for i in range(4):
                wt, tw = ring.take()
                for h in range(2):
                    tk = rows(lambda k: wt[:, k - 4 * i, :], at, 4 + 2 * h, h, tw, t_a[4 * i:4 * i + 4], nk=4, k0=4 * i, first=i == 0, last=False)
                ring.give(tk)
            wa, ta_ = ring.take()
            wb, tb_ = ring.take()
            WL = lambda k: wa[:, k - 16, :] if k < 20 else wb[:, k - 20, :]
            for h in range(2):
                b = 4 + 2 * h
                tk = rows(WL, at, b, h, [ta_, tb_], t_a, nk=6, k0=16, first=False, last=True)
                t = tt(VE, res[:, h, :], ps[:, b:b + 2, :].rearrange("p j f -> p (j f)"), acc[:, h, :], ADD, tk, t_e[h])
                mark(b, t)
                mark(b + 1, t)
                t_xn[h], t_h[h] = ln_a(res[:, h, :], h, row[0][:, :], row[1][:, :], res[:, h, :], t_l2, t)
            t_act = tk
            ring.give(tk)
            ring.give(tk)

        VAR = ((32, [(32, 0)]), (64, [(64, 0)]), (96, [(64, 0), (32, 64)]), (128, [(128, 0)]),
               (160, [(128, 0), (32, 128)]), (192, [(128, 0), (64, 128)]), (256, [(128, 0), (128, 128)]))
        NE, NT, NS = 8, 21, 7
        order = [("1", 0), ("3", 0)]
        for i in range(1, 7):
            order += [("1", i), ("3", i), ("2", i - 1)]
        order.append(("2", 6))
        slots = []
        for i in range(3):
            slots.append(ring.slots[(len(ring.plan) + i) % 3])
        free_s = ring.back[-3:] + [[t_w2, t_e]] * 4
        slots += [wk(f"eslot{i}", [P, 4096], 70848 + 16384 * i) for i in range(4)]
        s_m = [sem(f"m{i}") for i in range(NS)]
        s_rel = sem("rel")
        STEP_D, STEP_R = [48], [NT]
        wv = {}
        for n, (kind, i) in enumerate(order):
            k = 4 if kind == "2" else 8
            wv[kind, i] = (slots[n % NS][:, :].rearrange("p (k c) -> p k c", k=k), (s_m[n % NS], 16 * (n // NS + 1), STEP_D),
                           (s_rel, n + 1, STEP_R))
        for e_ in range(NE):
            for n, (kind, i) in enumerate(order):
                g = e_ * NT + n
                if kind == "2":
                    src = mw2[e_, 512 * i:512 * i + 512, :]
                else:
                    src = (mw1 if kind == "1" else mw3)[e_, :, 512 * i:512 * i + 512]
                k = 4 if kind == "2" else 8
                ld.start(s_m[n % NS], slots[n % NS][:, :].rearrange("p (k c) -> p k c", k=k),
                         src.rearrange("(k p) c -> p k c", p=P), free_s[g] if g < NS else (s_rel, g - NS + 1))

        xT = wk("xT", [P, KB, T], 0)
        ysb = wk("ysb", [P, 2, D], 16384)
        s1 = [wk(f"s1_{i}", [P, 512], 24576 + 2048 * i) for i in range(2)]
        ab = [wk(f"ab{i}", [P, 512], 28672 + 2048 * i) for i in range(2)]
        aTe = [wk(f"aTe{i}", [P, 4, T], 32768 + 4096 * i) for i in range(2)]
        Pt = wk("Pt", [P, 2, T], 40960)
        Pgt = wk("Pgt", [P, 2, 2, P], 43008)
        Pg = wk("Pg", [P, 2, T], 45056)
        for E in (PE, VE, AC):
            E.wait(t_route, t_e, t_h, PE.last(), VE.last(), AC.last(), GP.last())
            E.loop()
        for limit, blocks in VAR:
            for E in (PE, VE, AC):
                E.variant()
            BF = [[VE.start(), AC.start()] for _ in range(8)]
            ns = 128 if limit <= 128 else 256
            t_c = VE.do(lambda e: e.tensor_copy(cur[:, :], tab[:, bass.ds(VE.i, 1), :].rearrange("p o f -> p (o f)")))
            t_pt = []
            for h in range(2):
                t_pt.append(ts(VE, Pt[:, h, 0:ns], cst[:, C_IO:C_IO + ns], cur[:, h:h + 1], None, ALU.is_equal, None, t_c, PE.start()))
            t_pg = []
            for k, (B, off) in enumerate(blocks):
                nq = P // B
                for h in range(2):
                    t_pg.append(ts(VE, Pgt[:, k, h, :].rearrange("p (q b) -> p q b", q=nq),
                                   cst[:, C_IO + off:C_IO + off + B].unsqueeze(1).broadcast_to([P, nq, B]),
                                   cur[:, h:h + 1], cur[:, 2 + h:3 + h], ALU.is_equal, MUL, t_c, PE.start()))
            t_x = []
            for k in range(KB):
                b = 4 + k // 2
                w = take(b) if k % 2 == 0 else None
                for h in range(2):
                    tk = mm(ps[:, b, T * (k % 2):T * (k % 2) + ns], res[:, h, P * k:P * k + P], Pt[:, h, 0:ns], h == 0, h == 1, w, t_pt, inc=h == 1)
                if k % 2:
                    E = AC if k % 4 == 1 else VE
                    t = cp(E, xT[:, k - 1:k + 1, 0:ns], ps[:, b, :].rearrange("p (k t) -> p k t", k=2)[:, :, 0:ns], tk, PE.start())
                    mark(b, t)
                    t_x.append(t)
            w = take(3)
            for k in range(len(blocks)):
                for h in range(2):
                    tk = tr(ps[:, 3, T * k + P * h:T * k + P * h + P], Pgt[:, k, h, :], w, t_pg, inc=h == 1)
            nbk = len(blocks)
            t_P = cp(VE, Pg[:, 0:nbk, :], ps[:, 3, 0:T * nbk].rearrange("p (k t) -> p k t", k=nbk), tk, PE.start())
            mark(3, t_P)
            hb = [0]

            def up(kind, i, k):
                wt, tw, tr_ = wv[kind, i]
                B, off = blocks[k]
                nq = P // B
                N = 512 // nq
                b = hb[0] % 3
                hb[0] += 1
                w = take(b)
                for kk in range(8):
                    for q in range(nq):
                        end = kk == 7 and q == nq - 1
                        inc = False if not end else s_rel if k == nbk - 1 else True
                        t = mm(ps[B * q:B * q + B, b, 0:N], xT[:, kk, off:off + B], wt[:, kk, N * q:N * q + N], kk == 0, kk == 7, w, tw, t_x, inc=inc)
                return b, N, tr_ if k == nbk - 1 else t

            t_s, t_ab, t_at = [None] * 2, [None] * 2, [[None] * 2, [None] * 2]
            t_tr = [PE.start(), PE.start()]
            t_y = [None, None]

            def tile1(i):
                for k in range(nbk):
                    b, N, t = up("1", i, k)
                    t_s[k] = act(s1[k][:, 0:N], ps[:, b, 0:N], ACT.Silu, t, t_ab[k] or VE.start())
                    mark(b, t_s[k])

            def tile3(i):
                for k in range(nbk):
                    b, N, t = up("3", i, k)
                    t_ab[k] = tt(VE, ab[k][:, 0:N], s1[k][:, 0:N], ps[:, b, 0:N], MUL, t, t_s[k], t_tr[k])
                    mark(b, t_ab[k])

            def turn(i):
                for k, (B, off) in enumerate(blocks):
                    nq = P // B
                    nn = 4 // nq
                    w = take(3)
                    for n in range(nn):
                        t_tr[k] = tr(ps[:, 3, P * n:P * n + P], ab[k][:, P * n:P * n + P], w, t_ab[k], inc=n == nn - 1)
                    o = aTe[i % 2][:, :, off:off + B].rearrange("p (q n) b -> p n q b", q=nq)
                    s_ = ps[:, 3, 0:P * nn].rearrange("p (n q b) -> p n q b", n=nn, q=nq)
                    t_at[i % 2][k] = cp(VE, o, s_, t_tr[k], (s_rel, wv["2", i - 2][2][1], STEP_R) if i > 1 else PE.start())
                    mark(3, t_at[i % 2][k])

            def tile2(i):
                wt, tw, tr_ = wv["2", i]
                for k, (B, off) in enumerate(blocks):
                    nq = P // B
                    for j in range(2):
                        b = 4 + 2 * k + j
                        w = take(b) if i == 0 else None
                        for kk in range(4):
                            q = kk % nq
                            first = i == 0 and kk < nq
                            last = i == 6 and kk >= 4 - nq
                            end = j == 1 and kk == 3 and k == nbk - 1
                            t_y[k] = mm(ps[B * q:B * q + B, b, :], aTe[i % 2][:, kk, off:off + B], wt[:, kk, 512 * j:512 * j + 512],
                                        first, last, w, tw, t_at[i % 2][k], inc=s_rel if end else (i == 6 and kk == 3))
                    if k == nbk - 1:
                        t_y[k] = tr_

            tile1(0)
            tile3(0)
            for i in range(1, 7):
                tile1(i)
                turn(i - 1)
                tile3(i)
                tile2(i - 1)
            turn(6)
            tile2(6)
            t_yy = []
            for k in range(nbk):
                ta = act(ysb[:, k, 0:512], ps[:, 4 + 2 * k, :], ACT.Copy, t_y[k], PE.start())
                tb = cp(VE, ysb[:, k, 512:1024], ps[:, 5 + 2 * k, :], t_y[k], PE.start())
                t_yy.append([ta, tb])
            for h in range(2):
                for j in range(2):
                    b = 2 * h + j
                    w = take(b)
                    for k in range(nbk):
                        tk = mm(ps[:, b, :], Pg[:, k, P * h:P * h + P], ysb[:, k, 512 * j:512 * j + 512], k == 0, k == nbk - 1, w, t_P, t_yy[k], inc=k == nbk - 1)
                tt(VE, acc[:, h, :], acc[:, h, :], ps[:, 2 * h:2 * h + 2, :].rearrange("p j f -> p (j f)"), ADD, tk)
            for E in (PE, VE, AC):
                E.end_variant()
        for E in (PE, VE, AC):
            E.end_loop(NE)

        orow = wk("orow", [P, 2, D], 16384)
        t_out = []
        t_end = [VE.last(), PE.last()]
        for h in range(2):
            t = ln_stats(lambda i: acc[:, h, 512 * i:512 * i + 512], h, 2, t_end)
            t = stt(orow[:, h, :], acc[:, h, :], lmv[:, h, 0:1], row[0][:, :], SUB, MUL, t, t_l2)
            t = stt(orow[:, h, :], orow[:, h, :], lmv[:, h, 3:4], row[1][:, :], MUL, ADD, t)
            t_out.append(ld.once(out[0, P * h:P * h + P, :], orow[:, h, :], t))
        SP.wait(t_out)

        block_ = ctx.enter_context(nc.Block())
        block_.sync(lambda e: SP.emit(e))
        def count(i):
            return cnt[0:1, bass.ds(i, 1)]

        limits = [lim for lim, _ in VAR]
        block_.tensor(lambda e: PE.emit(e, NE, count, limits))
        block_.vector(lambda e: VE.emit(e, NE, count, limits))
        block_.scalar(lambda e: AC.emit(e, NE, count, limits))
        block_.gpsimd(lambda e: GP.emit(e))


def fcols(a):
    return a.reshape(-1, P).T


def layout(inputs):
    import numpy as np

    g = {k: np.asarray(a) for k, a in inputs.items()}
    i = np.arange(P)
    c = np.zeros((P, NCONST), np.float32)
    c[:, C_ID:C_ID + 128] = i[:, None] == i
    c[:, C_U:C_U + 128] = i[:, None] > i
    c[:, C_T:C_T + TT] = i[:, None] <= np.arange(TT)
    c[:, C_ONE:C_ONE + 128] = 1.0
    c[:, C_MASK:C_MASK + TT] = np.where(np.arange(TT) - 144 <= i[:, None], 0.0, -1e30)
    c[:, C_IO:C_IO + T] = np.arange(T)
    v = np.zeros((P, NVEC), np.float32)
    v[:, V_PRE:V_PRE + 8] = fcols(g["norm_pre"][0])
    v[:, V_CW:V_CW + 96] = g["conv_w"][0].reshape(4, 24, P).transpose(2, 1, 0).reshape(P, 96)
    v[:, V_CB:V_CB + 24] = fcols(g["conv_b"][0])
    v[:, V_DSK:V_DSK + 16] = fcols(np.repeat(g["d_skip"][0], 64))
    v[:, V_SSDN:V_SSDN + 16] = fcols(g["ssd_norm"][0])
    v[:, V_GB:V_GB + 16] = fcols(g["gate_bias"][0])
    v[:, V_ING:V_ING + 8] = fcols(g["ln_in_g_2"])
    v[:, V_INB:V_INB + 8] = fcols(g["ln_in_b_2"])
    v[0:32, V_DTFB] = g["dt_bias"][0]
    v[32:48, V_DTFB] = g["fgate_bias"][0]
    v[0:32, V_SGN] = 1.0
    v[32:48, V_SGN] = -1.0
    for l in range(2):
        o = V_L + l * VL_N
        v[:, o + VL_BIN:o + VL_BIN + 16] = fcols(g["b_in_2"][l, 0:2048])
        v[:, o + VL_CW:o + VL_CW + 124] = g["conv_w_2"][l].reshape(31, 4, P).transpose(2, 1, 0).reshape(P, 124)
        for col, name in ((VL_CB, "conv_b_2"), (VL_CG, "conv_ln_g_2"), (VL_CBT, "conv_ln_b_2"), (VL_G1, "ln1_g_2"),
                          (VL_B1, "ln1_b_2"), (VL_G2, "ln2_g_2"), (VL_B2, "ln2_b_2")):
            a = fcols(g[name][l])
            v[:, o + col:o + col + a.shape[1]] = a
    q = np.arange(T)
    r, cc = q // 64, q % 64
    dr = r[None, :] - r[:, None] + 7
    dc = np.clip(cc[None, :] - cc[:, None] + 15, 0, 30)
    win = np.clip(cc - 8, 0, 48)[:, None]
    ok = (cc[None, :] >= win) & (cc[None, :] < win + 16)
    nb = g["rpb_2"][:, :, dr, dc]
    nb = np.where(ok, nb, np.float32(-1e30)).astype(np.float32)
    nb = nb.reshape(2, 8, 2, P, T).transpose(0, 3, 2, 1, 4)
    d = {
        "x": g["x"], "meta": g["meta_tokens"], "consts": c, "vecs": v, "w_in": g["w_in"][0], "norm_post": g["norm_post"],
        "w_att": g["w_proj_att"][0], "w_ssd": g["w_proj_ssd"][0], "w_out": g["w_out"][0], "a_log": g["a_log"],
        "ln_in_g": g["ln_in_g_2"][None], "ln_in_b": g["ln_in_b_2"][None], "w_in2": g["w_in_2"], "b_in2": g["b_in_2"],
        "na_bias": nb, "w_out2": g["w_out_2"], "b_out2": g["b_out_2"], "ln1_g": g["ln1_g_2"], "ln1_b": g["ln1_b_2"],
        "w1": g["ffn_w1_2"][0], "w3": g["ffn_w3_2"][0], "w2": g["ffn_w2_2"][0],
        "pT": g["p_2"][:, 0].transpose(0, 2, 1), "ple_w": g["ple_w_2"], "gate_w": g["ple_gate_w_2"],
        "gate_b": g["ple_gate_b_2"], "ln2_g": g["ln2_g_2"], "ln2_b": g["ln2_b_2"], "w_router": g["w_router_2"][0],
        "mw1": g["moe_w1_2"][0], "mw3": g["moe_w3_2"][0], "mw2": g["moe_w2_2"][0],
    }
    return {k: np.ascontiguousarray(a) for k, a in d.items()}


def kernel(**inputs):
    import numpy as np
    import concourse.bacc as _bacc
    from concourse.bass_utils import run_bass_kernel_spmd as _run

    arrays = layout(inputs)
    nc = _bacc.Bacc("TRN2", target_bir_lowering=False, num_devices=1)
    args = [nc.dram_tensor(k, a.shape, mybir.dt.from_np(a.dtype), kind="ExternalInput").ap() for k, a in arrays.items()]
    out = nc.dram_tensor("out", (1, T, D), F32, kind="ExternalOutput").ap()
    bass_hybrid_conformer_moe(nc, *args, out)
    return _run(nc, [arrays], core_ids=[0]).results[0]["out"]
```

```python
import math
from contextlib import ExitStack

import concourse.bass as bass
from concourse import mybir

ALU = mybir.AluOpType
ACT = mybir.ActivationFunctionType
F32 = mybir.dt.float32
F32R = mybir.dt.float32r
I32 = mybir.dt.int32

P = 128
D = 1024
T = 256
NM = 16
TT = T + NM
KB = D // P
EPS = 1e-6
RANKS = (0, 1, 6, 2, 5, 3, 4, 7)
LN_EPS = 1e-5
ALPHA = 4.0 ** 0.25
BIG = 3.0e38
SB0 = 16512

C_ID, C_U, C_T, C_ONE, C_MASK, C_IO = 0, 128, 256, 528, 656, 928
C_KEY, C_RANK = 1184, 1192
NCONST = 1200

V_PRE, V_CW, V_CB, V_DSK, V_SSDN, V_GB = 0, 8, 104, 128, 144, 160
V_ING, V_INB, V_DTFB, V_SGN, V_ALOG = 176, 184, 192, 193, 194
V_L = 195
VL_BIN, VL_CW, VL_CB, VL_CG, VL_CBT, VL_G1, VL_B1, VL_G2, VL_B2, VL_N = 0, 16, 140, 144, 148, 152, 160, 168, 176, 184
NVEC = V_L + 2 * VL_N


def flat(ws):
    for w in ws:
        if isinstance(w, list):
            yield from flat(w)
        elif w is not None:
            yield w


class Eng:

    def __init__(self, name, sem):
        self.name, self.sem, self.n, self.q, self.seen = name, sem, 0, [], {}
        self.step, self.bodies, self.i, self.lastinc, self.inside = [0], None, 0, None, False

    def wait(self, *toks):
        for t in flat(toks):
            s, v = t[0], t[1]
            if self.seen.get(s.name, 0) < v:
                self.seen[s.name] = v
                if len(t) == 2:
                    self.q.append(lambda e, s=s, v=v: e.wait_ge(s, v))
                else:
                    self.q.append(lambda e, s=s, v=v, k=t[2]: e.wait_ge(s, self.i * k[0] + v))

    def do(self, fn, *toks, inc=True):
        self.wait(*toks)
        if not inc:
            self.q.append(fn)
            return None
        if inc is not True:
            self.q.append(lambda e: fn(e).then_inc(inc, 1))
            return None
        self.n += 1
        add = [1]
        self.lastinc = add
        self.q.append(lambda e: fn(e).then_inc(self.sem, add[0]))
        return self.last()

    def last(self):
        return (self.sem, self.n, self.step) if self.inside else (self.sem, self.n)

    def loop(self):
        self.pre, self.n0, self.bodies, self.inside = self.q, self.n, [], True

    def variant(self):
        self.q, self.n, self.seen = [], self.n0, {}

    def end_variant(self):
        self.bodies.append((self.q, self.n - self.n0, self.lastinc))

    def end_loop(self, iters):
        self.step[0] = max(n for _, n, _ in self.bodies)
        for _, n, add in self.bodies:
            add[0] += self.step[0] - n
        self.q, self.seen, self.inside = [], {}, False
        self.n = self.n0 + iters * self.step[0]

    def start(self):
        return (self.sem, self.n0, self.step)

    def emit(self, e, iters=0, count=None, limits=None):
        if self.bodies is not None:
            for f in self.pre:
                f(e)
            with e.Fori(0, iters) as i:
                self.i = i
                n = e.value_load(count(i), min_val=0, max_val=T)

                def pick(v):
                    if v == len(self.bodies) - 1:
                        for f in self.bodies[v][0]:
                            f(e)
                        return
                    with e.If(n < limits[v] + 1):
                        for f in self.bodies[v][0]:
                            f(e)
                    with e.Else():
                        pick(v + 1)

                pick(0)
        for f in self.q:
            f(e)


class Load:

    def __init__(self, eng, sems):
        self.eng, self.sems, self.count, self.next = eng, sems, {}, 0

    def slot(self):
        s = self.sems[self.next]
        self.next += 1
        return s

    def start(self, sem, dst, src, *toks):
        self.eng.wait(*toks)
        self.count[sem.name] = self.count.get(sem.name, 0) + 16
        self.eng.q.append(lambda e: e.dma_start(dst, src).then_inc(sem, 16))
        return (sem, self.count[sem.name])

    def once(self, dst, src, *toks):
        return self.start(self.slot(), dst, src, *toks)


class Ring:

    def __init__(self, load, slots):
        self.load, self.slots = load, slots
        self.sems = [load.slot() for _ in slots]
        self.plan, self.landed = [], []
        self.issued = 0
        self.back = []

    def issue(self, *toks):
        i = self.issued
        if i >= len(self.plan):
            return
        j = i % len(self.slots)
        k, c, src = self.plan[i]
        dst = self.slots[j][:, 0:k * c].rearrange("p (k c) -> p k c", k=k)
        self.landed.append(self.load.start(self.sems[j], dst, src, *toks))
        self.issued += 1

    def view(self, i):
        k, c, _ = self.plan[i]
        return self.slots[i % len(self.slots)][:, 0:k * c].rearrange("p (k c) -> p k c", k=k), self.landed[i]

    def give(self, tok):
        self.back.append(tok)
        self.issue(tok)


class Units:

    def __init__(self, ring, parts, split):
        self.ring, self.split = ring, split
        self.plan, self.made, self.where, self.cut = [], [], [], []
        self.free, self.rest = [(p, None, None) for p in parts], []
        self.taken = 0

    def tile(self, k, c, src, units):
        self.ring.plan.append((k, c, src))
        for n, u in enumerate(units):
            self.plan.append((len(self.ring.plan) - 1, u, n == len(units) - 1))

    def ahead(self):
        while len(self.made) < len(self.plan):
            m = len(self.made)
            i = next((i for i, f in enumerate(self.free) if f[2] is None or m < f[2]), None)
            if i is None:
                return
            part, last, limit = self.free.pop(i)
            t, (k0, k1, c0, c1), end = self.plan[m]
            raw, landed = self.ring.view(t)
            H, L = (x[:, :].rearrange("p (k c) -> p k c", k=k1 - k0) for x in part)
            tok = self.split(m, raw[:, k0:k1, c0:c1], H, L, landed, last)
            self.made.append((H, L, tok, m))
            self.where.append((part, limit))
            self.cut.append(tok)
            if end:
                self.ring.give(self.cut)
                self.cut = []

    def lend(self, parts, limit, *toks):
        self.free += [(p, list(toks), limit) for p in parts]
        self.ahead()

    def flush(self):
        self.free += self.rest
        self.rest = []
        self.ahead()

    def get(self):
        if self.taken == len(self.made):
            self.flush()
        self.taken += 1
        return self.made[self.taken - 1]

    def give(self, unit, tok):
        part, limit = self.where[unit[3]]
        self.free += self.rest
        self.rest = [(part, tok, limit)]
        self.ahead()


    def left(self, parts):
        n = len(self.ring.slots)
        raw = [self.ring.back[max(i for i in range(len(self.ring.back)) if i % n == j)] for j in range(n)]
        return raw, [next(t for p, t, _ in self.free + self.rest if p is q) for q in parts]


def weave(main, fill, n):
    acc = 0.0
    for m in main:
        acc += m * n
        while acc > 0:
            w = next(fill, None)
            acc = acc - w if w else -1e9


def run(gen):
    for _ in gen:
        pass


def bass_hybrid_conformer_moe(nc, x, meta, consts, vecs, onehot, w_in, norm_post, w_att, w_ssd, w_out, a_log, ln_in_g, ln_in_b,
                              w_in2, b_in2, na_bias, w_out2, b_out2, ln1_g, ln1_b, w1, w3, w2, pT, ple_w, gate_w,
                              gate_b, ln2_g, ln2_b, w_router, mw1, mw3, mw2, out):
    with ExitStack() as ctx:
        def sem(name):
            return ctx.enter_context(nc.semaphore(name))

        PE, VE, AC, GP, SP = (Eng(n, sem("s_" + n)) for n in ("pe", "dve", "act", "pool", "sp"))
        ld = Load(SP, [sem(f"d{i}") for i in range(40)])
        ldg = Load(GP, [sem(f"g{i}") for i in range(40)])
        ps = ctx.enter_context(nc.psum_tensor("ps", [P, 8, 512], F32))
        BF = [[] for _ in range(8)]

        top = [SB0]

        def sb(name, shape, off=None, dt=F32):
            n = 4
            for s in shape[1:]:
                n *= s
            n = (n + 31) // 32 * 32
            if off is None:
                off = top[0]
                top[0] += n
            assert off + n <= 229344, (name, off, n)
            return nc.alloc_sbuf_tensor_at(name, shape, dt, offset=off)

        def mm(o, l, r, start, stop, *w, inc=False):
            return PE.do(lambda e: e.matmul(o, l, r, start=start, stop=stop), *w, inc=inc)

        def tr(o, i, *w, inc=False):
            n = i.shape[0]
            b = i.base_partition() if callable(i.base_partition) else i.base_partition
            return PE.do(lambda e: e.transpose(o, i, ident[b:b + n, b:b + n]), *w, inc=inc)

        def act(o, i, f, *w, bias=0.0, scale=1.0, acc=None):
            if acc is None:
                return AC.do(lambda e: e.activation(o, i, f, bias=bias, scale=scale), *w)
            return AC.do(lambda e: e.activation(o, i, f, bias=bias, scale=scale, accum_out=acc), *w)

        def ts(E, o, i, s1, s2, op0, op1, *w):
            if s2 is None:
                return E.do(lambda e: e.tensor_scalar(o, i, s1, None, op0), *w)
            return E.do(lambda e: e.tensor_scalar(o, i, s1, s2, op0, op1), *w)

        def stt(o, i0, s, i1, op0, op1, *w):
            return VE.do(lambda e: e.scalar_tensor_tensor(out=o, in0=i0, scalar=s, in1=i1, op0=op0, op1=op1), *w)

        def tt(E, o, a, b, op, *w):
            return E.do(lambda e: e.tensor_tensor(o, a, b, op=op), *w)

        def cp(E, o, i, *w):
            if E is AC:
                return act(o, i, ACT.Copy, *w)
            return E.do(lambda e: e.tensor_copy(o, i), *w)

        def ms(E, o, v, *w):
            return E.do(lambda e: e.memset(o, v), *w)

        def rcp(o, i, *w):
            return VE.do(lambda e: e.reciprocal(o, i), *w)

        def neg_max(o, i0, i1, acc, *w):
            return VE.do(lambda e: e.tensor_tensor_reduce(o, i0, i1, -1.0, BIG, ALU.add, ALU.min, acc), *w)

        MUL, ADD, SUB, MAX = ALU.mult, ALU.add, ALU.subtract, ALU.max

        def mark(b, *toks):
            BF[b] = list(toks)

        def take(b):
            w = BF[b]
            BF[b] = []
            return w

        cst = sb("cst", [P, NCONST])
        vec = sb("vec", [P, NVEC])
        small = sb("small", [P, 256])
        tokv = sb("tokv", [P, 3, 48])
        adt = sb("adt", [P, 3, 32])
        dth = sb("dth", [P, 2, 32])
        dsx = sb("dsx", [P, 4, 32])
        ecsT = sb("ecsT", [32, T])
        arow = sb("arow", [P, 32])
        ident = cst[:, C_ID:C_ID + 128]
        strict = cst[:, C_U:C_U + 128]
        tri = cst[:, C_T:C_T + TT]
        ones = cst[:, C_ONE:C_ONE + 128]
        fmask = cst[:, C_MASK:C_MASK + TT]

        def v(c, n=1, p=P):
            return vec[0:p, c:c + n]

        res = sb("res", [P, 2, D])
        W0 = top[0]
        NR, NU = 3, 5
        ring = Ring(ld, [sb(f"raw{i}", [P, 2048], 229344 - 8192 * (i + 1)) for i in range(NR)])
        parts = [[sb(f"u{c}{i}", [P, 1024], 229344 - 8192 * (NR + i + 1) + 4096 * n, F32R) for n, c in enumerate("HL")]
                 for i in range(NU)]
        WTOP = 229344 - 8192 * (NR + NU) - W0

        def wk(name, shape, off, dt=F32):
            n = 4
            for d in shape[1:]:
                n *= d
            assert off + n <= WTOP, (name, off + n, WTOP)
            return sb(name, shape, W0 + off, dt)

        def pair(name, shape, off):
            n = 4
            for d in shape[1:]:
                n *= d
            return wk(name + "H", shape, off, F32R), wk(name + "L", shape, off + n, F32R)

        def f32(ap):
            return ap.bitcast(F32)

        lows = [VE, GP]

        def split(m, raw, H, L, *w):
            t = act(H, raw, ACT.Copy, *w)
            return [t, tt(lows[m % len(lows)], L, raw, f32(H), SUB, t, *w)]

        U = Units(ring, parts, split)

        def fm(w, c0, n, k0=0):
            for c in range(c0, c0 + n, 256):
                m = min(256, c0 + n - c)
                U.tile(8, m, w[k0 * P:(k0 + 8) * P, c:c + m].rearrange("(k p) c -> p k c", p=P),
                       [(0, 8, i, i + 128) for i in range(0, m, 128)])

        def tm(w, c0, nk):
            for k in range(0, nk, 4):
                m = min(4, nk - k)
                U.tile(m, 512, w[k * P:(k + m) * P, c0:c0 + 512].rearrange("(k p) c -> p k c", p=P),
                       [(i, i + 2, 0, 512) for i in range(0, m, 2)])

        XB, DT, ZA, Q, K, V, FG, GA = 2048, 5120, 5152, 6176, 7200, 8224, 9248, 9264
        U.tile(8, 128, None, [(0, 8, 0, 128)])
        for c0, n in ((K, 1024), (Q, 1024), (V, 1024), (XB + 2048, 1024), (XB, 2048), (0, 2048), (ZA, 1024),
                      (GA + 1024, 1024), (GA, 1024)):
            fm(w_in, c0, n)
        fm(w_att, 0, 1024)
        for c in range(0, 1024, 256):
            fm(w_ssd, c, 256, 0)
            fm(w_ssd, c, 256, 8)
        tm(w_out, 0, 8)
        tm(w_out, 512, 8)
        UB = [len(U.plan)]

        def layer_plan(l):
            tm(ple_w[l], 0, 2)
            tm(w_in2[l], 2048, 8)
            for c in (0, 512, 256, 768, 1024, 1536, 1280, 1792):
                fm(w_in2[l], c, 256)
            tm(ple_w[l], 512, 2)
            tm(w_out2[l], 0, 8)
            tm(w_out2[l], 512, 8)
            tm(gate_w[l], 0, 8)
            tm(gate_w[l], 512, 8)
            UB.append(len(U.plan))

        layer_plan(0)
        for c in range(0, 2816, 256):
            fm(w1, c, 256)
            fm(w3, c, 256)
        tm(w2, 0, 22)
        tm(w2, 512, 22)
        UB.append(len(U.plan))
        layer_plan(1)

        uH, uL = pair("u", [P, KB, TT], 0)
        xhat = wk("xhat", [P, 2, D], 17408)
        mhat = wk("mhat", [NM, D], 25600)
        min_ = wk("min_", [NM, D], 29696)
        sq = wk("sqj", [P, D], 33792)
        sp = wk("sp", [48, TT], 37888)
        dx = wk("dx", [48, 6, TT], 38976)

        t_x = [ld.once(res[:, h, :], x[0, 128 * h:128 * h + 128, :]) for h in range(2)]
        t_m = ld.once(min_[:, :], meta)
        t_c = ld.once(cst[:, :], consts)
        t_v = ld.once(vec[:, :], vecs)
        qa = wk("qa", [80, 16, T], 51712)
        wdf = ring.slots[0][:, 0:1024].rearrange("p (k c) -> p k c", k=8)
        t = ms(GP, ring.slots[0][:, 0:1024], 0.0)
        ld.start(ring.sems[0], wdf[:, :, 0:32], w_in[:, DT:DT + 32].rearrange("(k p) c -> p k c", p=P), t)
        ring.landed.append(ld.start(ring.sems[0], wdf[:, :, 32:48], w_in[:, FG:FG + 16].rearrange("(k p) c -> p k c", p=P)))
        ring.issued = 1
        t_oh = ld.once(qa[64:80, :, :], onehot)
        t_al = ld.once(arow[:, :], a_log.broadcast_to([P, 32]))
        for _ in range(2):
            ring.issue()

        t_half = ms(GP, small[:, 0:1], -0.5)
        t_eps = ms(GP, small[:, 2:3], EPS)

        def rsqrt(o, i, *w):
            n, c = i.shape
            return GP.do(lambda e: e.tensor_tensor(o, i, small[0:n, 0:1].broadcast_to([n, c]), op=ALU.pow), t_half, *w)

        toks = ((0, res[:, 0, :], xhat[:, 0, :], P, NM, t_x[0]), (1, res[:, 1, :], xhat[:, 1, :], P, NM + P, t_x[1]),
                (2, min_[:, :], mhat[:, :], NM, 0, t_m))
        t_n = []
        for i, src, dst, n, col, t in toks:
            ss, mq, rs = small[0:n, 4 + i:5 + i], small[0:n, 8 + i:9 + i], small[0:n, 12 + i:13 + i]
            if i == 1:
                t = VE.do(lambda e, src=src, ss=ss: e.tensor_tensor_reduce(xhat[:, 1, :], src, src, 1.0, 0.0, MUL, ADD, ss), t)
            else:
                t = act(sq[0:n, :], src, ACT.Square, AC.last(), t, acc=ss)
            t = ts(VE, mq, ss, 1.0 / D, EPS, MUL, ADD, t)
            t = rsqrt(rs, mq, t)
            t_n.append(ts(VE, dst, src, rs, None, MUL, None, t))
        t_u = []
        for i, src, dst, n, col, _ in toks:
            for g in range(2):
                b = 2 * i + g
                for k in range(4):
                    kk = 4 * g + k
                    tk = tr(ps[:, b, n * k:n * k + n], dst[:, 128 * kk:128 * kk + 128], t_n[i], t_c, inc=k == 3)
                for k in range(4):
                    kk = 4 * g + k
                    te = act(uH[:, kk, col:col + n], ps[:, b, n * k:n * k + n], ACT.Copy, tk, t_v, scale=v(V_PRE + kk))
                for k in range(4):
                    kk = 4 * g + k
                    tl = stt(uL[:, kk, col:col + n], ps[:, b, n * k:n * k + n], v(V_PRE + kk), f32(uH[:, kk, col:col + n]), MUL, SUB, te)
                t_u.append(tl)
                mark(b, tl)
        U.ahead()

        PB = [0]

        def mm3(o, xH, xL, k, n, h, first, last, *w, inc=False):
            H, L, tu, _ = h
            mm(o, H[:, k, :], xH, first, False, tu, *w)
            mm(o, H[:, k, :], xL, False, False)
            return mm(o, L[:, k, :], xH, False, last, inc=inc)

        def block(rH, rL, n, *acts, b=None, part=(True, True)):
            h = U.get()
            if b is None:
                b = PB[0]
                PB[0] = 1 - b
            w = take(b) if part[0] else None
            for k in range(KB):
                tk = mm3(ps[:, b, 0:n], rH(k), rL(k), k, n, h, part[0] and k == 0, part[1] and k == KB - 1, w, list(acts), inc=k == KB - 1)
            U.give(h, tk)
            return b, ps[:, b, 0:n], tk

        u_all = (lambda k: uH[:, k, :], lambda k: uL[:, k, :])
        u_x = (lambda k: uH[:, k, NM:TT], lambda k: uL[:, k, NM:TT])

        b, pb, tk = block(*u_all, TT, t_u, b=6)
        X, E_, S1, S2, R, A6 = (dx[:, i, :] for i in range(6))
        t1 = ts(VE, X, pb[0:48], v(V_DTFB, p=48), v(V_SGN, p=48), ADD, MUL, tk, t_v)
        mark(6, t1)

        def softplus():
            t2 = stt(S1, X, -1.0, X, MUL, MAX, t1)
            te = act(E_, S1, ACT.Exp, t2, scale=-1.0)
            yield
            t3 = ts(VE, S1, E_, 2.0, None, ADD, None, te)
            t4 = rcp(R, S1, t3)
            yield
            t5 = tt(VE, S1, E_, R, MUL, t4)
            t6 = tt(VE, S2, S1, S1, MUL, t5)
            yield
            t7 = ts(VE, A6, S2, 1.0 / 15, None, MUL, None, t6)
            for n in (13, 11, 9, 7, 5, 3):
                t7 = stt(A6, A6, 1.0 / n, S2, ADD, MUL, t7)
                if n in (11, 7, 3):
                    yield
            t7 = stt(A6, A6, 1.0, S1, ADD, MUL, t7)
            yield
            t8 = ts(VE, X, X, 0.0, None, MAX, None, t1)
            t_sp.append(stt(sp[:, :], A6, 2.0, X, MUL, ADD, t7, t8))
            yield

        t_sp = []
        f_sp = softplus()

        def token_decays():
            b = 7
            w = take(b)
            for c, (c0, n) in enumerate(((0, NM), (NM, P), (NM + P, P))):
                tk = tr(ps[0:n, b, 48 * c:48 * c + 48], sp[:, c0:c0 + n], t_sp, w, inc=c == 2)
            tv1 = cp(VE, tokv[0:NM, 0, :], ps[0:NM, b, 0:48], tk)
            tv2 = cp(VE, tokv[:, 1:3, :], ps[:, b, 48:144].rearrange("p (c f) -> p c f", c=2), tk)
            mark(b, tv2)
            t_a = act(arow[:, :], arow[:, :], ACT.Exp, t_al)
            for c, n in enumerate((NM, P, P)):
                t_adt = stt(adt[0:n, c, :], tokv[0:n, c, 0:32], -1.0, arow[0:n, :], MUL, MUL, tv1, tv2, t_a)
            t_dth = ts(VE, dth[:, :, :], tokv[:, 1:3, 0:32], 0.5, None, MUL, None, tv2)
            b = 6
            w = take(b)
            mm(ps[0:NM, b, 0:TT], tokv[0:NM, 0, 32:48], tri[0:NM, 0:TT], True, False, w, tv1, tv2)
            mm(ps[0:NM, b, NM:TT], tokv[:, 1, 32:48], tri[:, 0:T], False, False)
            tk = mm(ps[0:NM, b, NM + P:TT], tokv[:, 2, 32:48], tri[:, 0:P], False, True, inc=True)
            t_ck = []
            for i in range(4):
                o = ka[64:80, 4 * i:4 * i + 4, :]
                s = ps[0:NM, b, 0:TT].unsqueeze(1).broadcast_to([NM, 4, TT])
                t_ck.append(act(o, s, ACT.Copy, tk))
            mark(b, t_ck[-1])
            return tv1, tv2, t_adt, t_dth, t_ck

        xbcT = wk("xbcT", [P, 24, TT], 17408)
        oT = wk("oT", [P, 8, T], 43520)
        ka = wk("ka", [80, 16, TT], 68096)
        vt = wk("vt", [P, 3, D], 85504)
        Pb = [wk(f"Pb{i}", [P, 416], 97792 + 1664 * i) for i in range(4)]
        PTb = [wk(f"PTb{i}", [P, 384], 104448 + 1536 * i) for i in range(4)]
        PMb = [wk(f"PMb{i}", [NM, 512], 110592 + 2048 * i) for i in range(2)]
        cacc = [wk(f"cacc{i}", [P, TT], 114688 + 1088 * i) for i in range(4)]
        ctn = [wk(f"ctn{i}", [P, TT], 119040 + 1088 * i) for i in range(2)]
        xc = [wk(f"xc{i}", [P, TT], 121216 + 1088 * i) for i in range(4)]
        vtmp = [wk(f"vtmp{i}", [P, TT], 125568 + 1088 * i) for i in range(2)]

        t_q, t_k = [None] * 16, [None] * 16
        for dst, rhs, n, sc, tl in ((ka, u_all, TT, 1.0, t_k), (qa, u_x, T, 0.125, t_q)):
            for j in range(8):
                b, pb, tk = block(*rhs, n, t_u)
                tl[2 * j] = act(dst[0:64, 2 * j, :], pb[0:64], ACT.Copy, tk, scale=sc)
                tl[2 * j + 1] = ts(VE, dst[0:64, 2 * j + 1, :], pb[64:128], sc, None, MUL, None, tk)
                mark(b, tl[2 * j], tl[2 * j + 1])
                next(f_sp, None)
            if dst is ka:
                tv1, tv2, t_adt, t_dth, t_ck = token_decays()
        t_vt = []
        use = [None, None]

        def turn_v(j, te):
            b = 6 + j % 2
            w = take(b)
            for c, (c0, n) in enumerate(((0, NM), (NM, P), (NM + P, P))):
                use[j % 2] = tr(ps[0:n, b, 128 * c:128 * c + 128], vtmp[j % 2][:, c0:c0 + n], te, w, inc=c == 2)
            ta = cp(VE, vt[0:NM, 0, 128 * j:128 * j + 128], ps[0:NM, b, 0:128], use[j % 2])
            tb = cp(VE, vt[:, 1:3, 128 * j:128 * j + 128], ps[:, b, 128:384].rearrange("p (c f) -> p c f", c=2), use[j % 2])
            mark(b, ta, tb)
            t_vt.extend([ta, tb])

        te = None
        for j in range(8):
            b, pb, tk = block(*u_all, TT, t_u)
            if j:
                turn_v(j - 1, te)
            te = act(vtmp[j % 2][:, :], pb, ACT.Copy, tk, use[j % 2])
            mark(b, te)
        turn_v(7, te)

        t_xb = [None] * 24

        def xbc():
            rel, relz = [None] * 4, [None] * 2
            pend = []

            def finish(j, n, t):
                a, z = cacc[n % 4], ctn[n % 2]
                te = act(z[:, :], a[:, :], ACT.Tanh, t, relz[n % 2], scale=0.5)
                t_xb[j] = rel[n % 4] = relz[n % 2] = stt(xbcT[:, j, :], z[:, :], 1.0, a[:, :], ADD, MUL, te, fr_x)

            for n, j in enumerate([j0 + i for j0 in (16, 20, 0, 4, 8, 12) for i in range(4)]):
                b, pb, tk = block(*u_all, TT, t_u)
                a, x_ = cacc[n % 4], xc[n % 4]
                cw = V_CW + 4 * j
                act(x_[:, :], pb, ACT.Copy, tk, rel[n % 4])
                t = act(a[:, :], pb, ACT.Identity, scale=v(cw + 3), bias=v(V_CB + j))
                mark(b, t)
                for d in (1, 2, 3):
                    t = stt(a[:, d:TT], x_[:, 0:TT - d], v(cw + 3 - d), a[:, d:TT], MUL, ADD, t)
                pend.append((j, n, t))
                if n > 1:
                    finish(*pend.pop(0))
                yield 1
            for p in pend:
                finish(*p)
            yield 1

        t_o = [None] * 8
        nmx = small[:, 32:64]
        rsm = small[:, 64:96]
        riv = small[:, 96:128]

        def fox():
            pn = [None] * 16
            ptt, pmt = [None] * 16, [None] * 8
            trd, od = [None] * 16, [None] * 8
            for st in range(10):
                if st < 8:
                    for h in (2 * st, 2 * st + 1):
                        b = 2 + h % 2
                        w = take(b)
                        mm(ps[:, b, 0:144], qa[:, h, 0:P], ka[:, h, 0:144], True, True, w, t_q[h], t_k[h], t_oh, t_ck[h // 4])
                        tk = mm(ps[:, b, 144:416], qa[:, h, P:T], ka[:, h, :], True, True, inc=True)
                        p = Pb[h % 4]
                        t0 = neg_max(p[:, 0:144], ps[:, b, 0:144], fmask[:, 128:272], nmx[:, 2 * h:2 * h + 1], tk, trd[h - 4] if h > 3 else None)
                        t1 = neg_max(p[:, 144:416], ps[:, b, 144:416], fmask, nmx[:, 2 * h + 1:2 * h + 2], tk)
                        mark(b, t1)
                        e0 = act(p[:, 0:144], p[:, 0:144], ACT.Exp, t0, bias=nmx[:, 2 * h:2 * h + 1], scale=-1.0, acc=rsm[:, 2 * h:2 * h + 1])
                        e1 = act(p[:, 144:416], p[:, 144:416], ACT.Exp, t1, bias=nmx[:, 2 * h + 1:2 * h + 2], scale=-1.0, acc=rsm[:, 2 * h + 1:2 * h + 2])
                        r = rcp(riv[:, 2 * h:2 * h + 2], rsm[:, 2 * h:2 * h + 2], e0, e1)
                        ts(VE, p[:, 0:144], p[:, 0:144], riv[:, 2 * h:2 * h + 1], None, MUL, None, r)
                        pn[h] = ts(VE, p[:, 144:416], p[:, 144:416], riv[:, 2 * h + 1:2 * h + 2], None, MUL, None, r)
                    yield 1
                if 1 <= st <= 8:
                    wm = take(6)
                    i = st - 1
                    for h in (2 * i, 2 * i + 1):
                        b = 4 + h % 2
                        w = take(b)
                        p = Pb[h % 4]
                        m0 = 256 * (h % 2)
                        tr(ps[:, b, 0:128], p[:, 16:144], w, pn[h])
                        tr(ps[:, b, 128:256], p[:, 160:288])
                        tk = tr(ps[:, b, 256:384], p[:, 288:416], inc=True)
                        tr(ps[0:NM, 6, m0:m0 + 128], p[:, 0:16], wm)
                        trd[h] = tr(ps[0:NM, 6, m0 + 128:m0 + 256], p[:, 144:160], inc=True)
                        ptt[h] = act(PTb[h % 4][:, :], ps[:, b, 0:384], ACT.Copy, tk, od[i - 2] if i > 1 else None)
                        mark(b, ptt[h])
                    pmt[i] = cp(VE, PMb[i % 2][:, :], ps[0:NM, 6, :], trd[2 * i + 1], od[i - 2] if i > 1 else None)
                    mark(6, pmt[i])
                    yield 1
                if st >= 2:
                    i = st - 2
                    w = take(7)
                    for c in range(3):
                        for h in (2 * i, 2 * i + 1):
                            r0 = 64 * (h % 2)
                            o = ps[r0:r0 + 64, 7, 0:T]
                            hs = slice(64 * h, 64 * h + 64)
                            if c == 0:
                                mm(o, vt[:, 1, hs], PTb[h % 4][:, 0:256], True, False, w, ptt[h], t_vt)
                            elif c == 1:
                                mm(o, vt[0:NM, 0, hs], PMb[i % 2][:, 256 * (h % 2):256 * (h % 2) + 256], False, False, pmt[i])
                            else:
                                tk = mm(ps[r0:r0 + 64, 7, P:T], vt[:, 2, hs], PTb[h % 4][:, 256:384], False, True, inc=True)
                    od[i] = tk
                    t_o[i] = act(oT[:, i, :], ps[:, 7, 0:T], ACT.Copy, tk)
                    mark(7, t_o[i])
                    yield 0.6

        fr_x = [t_u, t_sp, tv2]
        f = xbc()
        lows[:] = [GP, VE, GP]
        weave(fox(), f, 1)
        run(f)
        t_fox = [PE.last(), VE.last(), AC.last()]

        zT = wk("zT", [P, 16, T], 51712)
        xdt = [wk(f"xdt{i}", [P, 2, 512], 68096 + 4096 * i) for i in range(2)]
        hin = [wk(f"hin{i}", [P, 2, 512], 76288 + 4096 * i) for i in range(2)]
        cbT = wk("cbT", [P, 8, P], 84480)
        Btok = wk("Btok", [P, 512], 88576)
        Bm = wk("Bm", [NM, 512], 90624)
        xds = [wk(f"xds{i}", [P, 512], 92672 + 2048 * i) for i in range(2)]
        adT = [wk(f"adT{i}", [P, 4, P], 96768 + 2048 * i) for i in range(2)]
        Eb = [wk(f"Eb{i}", [P, 4, P], 100864 + 2048 * i) for i in range(2)]
        Mb = [[wk(f"Mb{i}{c}", [P, 4, P], 104960 + 4096 * i + 2048 * c) for c in range(2)] for i in range(2)]
        ecB = wk("ecB", [P, 2, T], 113152)
        t1b = [wk(f"t1b{i}", [P, 2, T], 115200 + 2048 * i) for i in range(2)]
        sqb = [wk(f"sqb{i}", [P, 2, T], 119296 + 2048 * i) for i in range(2)]
        ztn = [wk(f"ztn{i}", [P, T], 123392 + 1024 * i) for i in range(3)]
        gsel = wk("gsel", [P, 4, 4], 126464)
        rst = wk("rst", [4, T], 92672)
        rst2 = wk("rst2", [4, T], 94720)
        dskh = small[:, 128:144]
        t_gs = ms(GP, gsel[:, :, :], 0.0, t_fox)
        for g in range(4):
            t_gs = ms(GP, gsel[:, g, g:g + 1], 1.0, t_gs)
        t_dk = ts(VE, dskh, v(V_DSK, 16), 0.5, None, MUL, None, t_v)
        t_z = [None] * 16
        t_oz = [None] * 8
        t_yd = [None] * 8
        zrel = [None] * 3

        def zproj():
            for j in range(16):
                b, pb, tk = block(*u_x, T, t_u)
                z = ztn[j % 3]
                te = act(z[:, :], pb, ACT.Tanh, tk, zrel[j % 3], t_fox, scale=0.5)
                t_z[j] = zrel[j % 3] = stt(zT[:, j, :], z[:, :], 1.0, pb, ADD, MUL, te, t_fox)
                mark(b, t_z[j])
                yield 1
            for k in range(8):
                b, pb, tk = block(*u_x, T, t_u)
                z = ztn[k % 3]
                te = act(z[:, :], pb, ACT.Tanh, tk, zrel[k % 3], scale=0.5)
                t = stt(z[:, :], z[:, :], 1.0, pb, ADD, MUL, te)
                mark(b, t)
                t_oz[k] = zrel[k % 3] = stt(oT[:, k, :], oT[:, k, :], 0.5, z[:, :], MUL, MUL, t, t_o[k])
                yield 1

        def h8(ap, n):
            return ap.unsqueeze(2).broadcast_to([n, 8, 64])

        def hd(ap):
            return ap.rearrange("p (h d) -> p h d", h=8)

        def f2(a):
            return a[:, :, :].rearrange("p j t -> p (j t)")

        sqrd = [None, None]

        def ssd():
            w = take(2)
            for c in range(2):
                mm(ps[0:32, 2, P * c:P * c + P], adt[:, c + 1, :], tri[:, 0:P], True, True, w, t_adt)
            mm(ps[0:NM, 2, 256:288], strict[0:NM, 0:NM], adt[0:NM, 0, :], True, True)
            mm(ps[:, 2, 288:320], strict, adt[:, 1, :], True, True)
            tk = mm(ps[:, 2, 320:352], ones, adt[:, 1, :], True, True, inc=True)
            t_ecs = act(ecsT[:, :], ps[0:32, 2, 0:T], ACT.Exp, tk)
            te0 = act(dsx[0:NM, 0, :], ps[0:NM, 2, 256:288], ACT.Exp, tk)
            te1 = act(dsx[:, 1:3, :], ps[:, 2, 288:352].rearrange("p (c f) -> p c f", c=2), ACT.Exp, tk)
            mark(2, te1)
            w = take(3)
            for g in range(4):
                tk = tr(ps[:, 3, P * g:P * g + P], xbcT[:, 16 + g, NM:NM + P], w, t_xb[16:20], inc=g == 3)
            t_b1 = act(Btok[:, :], ps[:, 3, :], ACT.Copy, tk, t_fox)
            mark(3, t_b1)
            w = take(4)
            for g in range(4):
                tk = tr(ps[0:NM, 4, P * g:P * g + P], xbcT[:, 16 + g, 0:NM], w, inc=g == 3)
            t_b0 = act(Bm[:, :], ps[0:NM, 4, :], ACT.Copy, tk, t_fox)
            mark(4, t_b0)
            t_d0 = stt(dsx[0:NM, 0, :], tokv[0:NM, 0, 0:32], 0.25, dsx[0:NM, 0, :], MUL, MUL, te0)
            t_d1 = stt(dsx[:, 1, :], tokv[:, 1, 0:32], 0.25, dsx[:, 1, :], MUL, MUL, te1)
            yield 1
            t_cb = []
            for c in range(2):
                b = 2 + c
                w = take(b)
                c0 = NM + P * c
                for g in range(4):
                    tk = mm(ps[:, b, P * g:P * g + P], xbcT[:, 16 + g, c0:c0 + P], xbcT[:, 20 + g, c0:c0 + P], True, True, w, t_xb[20 + g], inc=g == 3)
                t_cb.append(stt(cbT[:, 4 * c:4 * c + 4, :], ps[:, b, :].rearrange("p (g s) -> p g s", g=4), 0.25,
                                tri[:, 0:P].unsqueeze(1).broadcast_to([P, 4, P]), MUL, MUL, tk, t_fox))
                mark(b, t_cb[c])
                yield 1
            rel = [None, None]
            t_xd = [[None] * 4 for _ in range(2)]
            t_h = [[None] * 4 for _ in range(2)]
            fr_x, fr_h = [None, None], [None, None]
            cnt_ = [0]

            def gprep(g, c):
                c0, m = ((0, NM), (NM, P), (NM + P, P))[c]
                g8 = slice(8 * g, 8 * g + 8)
                w = take(6)
                for j in range(4):
                    tk = tr(ps[0:m, 6, P * j:P * j + P], xbcT[:, 4 * g + j, c0:c0 + m], w, t_xb[4 * g + j], inc=j == 3)
                src = hd(ps[0:m, 6, :])
                if c > 0:
                    t = t_xd[c - 1][g] = tt(VE, hd(xdt[g % 2][:, c - 1, :]), src, h8(dth[:, c - 1, g8], P), MUL, tk, t_fox, t_dth, fr_x[g % 2])
                if c < 2:
                    n = cnt_[0]
                    cnt_[0] += 1
                    xd = xds[n % 2]
                    t = tt(VE, hd(xd[0:m, :]), src, h8(dsx[0:m, c, g8], m), MUL, tk, rel[n % 2], t_d0, t_d1, t_fox)
                mark(6, t)
                if c < 2:
                    yield 1
                    w = take(5)
                    bt = Bm if c == 0 else Btok
                    rel[n % 2] = tk = mm(ps[:, 5, :], bt[0:m, P * g:P * g + P], xd[0:m, :], True, True, w, t, t_b0, t_b1, inc=True)
                    if c == 0:
                        t_h[0][g] = act(hin[g % 2][:, 0, :], ps[:, 5, :], ACT.Copy, tk, t_fox, fr_h[g % 2])
                        mark(5, t_h[0][g])
                    else:
                        t = tt(VE, hd(hin[g % 2][:, 1, :]), hd(hin[g % 2][:, 0, :]), h8(dsx[:, 2, g8], P), MUL, t_h[0][g], te1, t_fox, fr_h[g % 2])
                        t_h[1][g] = tt(VE, hin[g % 2][:, 1, :], hin[g % 2][:, 1, :], ps[:, 5, :], ADD, t, tk)
                        mark(5, t_h[1][g])

            for c in range(3):
                yield from gprep(0, c)
            ta = [None, None]
            segd = [None, None]
            tE, tM = [None, None], [[None, None], [None, None]]
            Mrd = [[None, None], [None, None]]
            yrel, srd = [None], [None, None]
            wsum = take(7)
            sqt = []

            def prep(q):
                for c in range(2):
                    ta[c] = tt(GP, adT[c][:, :, :], tri[:, 0:P].unsqueeze(1).broadcast_to([P, 4, P]),
                               adt[:, c + 1, 4 * q:4 * q + 4].unsqueeze(2).broadcast_to([P, 4, P]), MUL, t_adt, t_fox, segd[c])

            def seg(q):
                g = q // 2
                for c in range(2):
                    b = 2 + c
                    w = take(b)
                    segd[c] = tk = mm(ps[:, b, :], strict, f2(adT[c]), True, True, w, ta[c], inc=True)
                    te = act(f2(Eb[c]), ps[:, b, :], ACT.Exp, tk, tE[c], t_fox)
                    mark(b, te)
                    tE[c] = tM[q % 2][c] = tt(VE, Mb[q % 2][c][:, :, :], Eb[c][:, :, :], cbT[:, 4 * c + g:4 * c + g + 1, :].broadcast_to([P, 4, P]), MUL, te, t_cb, Mrd[q % 2][c])
                if q < 7:
                    prep(q + 1)

            def sums(q):
                for j in range(2):
                    i = 2 * q + j
                    tk = mm(ps[0:4, 7, 0:T], gsel[:, i // 4, :], sqb[q % 2][:, j, :], i == 0, i == 15, wsum, sqt[q], t_gs, inc=j == 1)
                sqrd[q % 2] = tk

            prep(0)
            seg(0)
            for q in range(8):
                g = q // 2
                if q < 7:
                    seg(q + 1)
                w = take(5)
                for j in range(2):
                    for c in range(2):
                        c0 = NM + P * c
                        r0 = P * (2 * (q % 2) + j)
                        ty = mm(ps[:, 5, 256 * j + P * c:256 * j + P * c + P], hin[g % 2][:, c, r0:r0 + P], xbcT[:, 20 + g, c0:c0 + P], True, True, w, t_h[c][g], inc=(j == 1 and c == 1))
                fr_h[g % 2] = ty
                w = take(6)
                for j in range(2):
                    for r in range(2):
                        h = 4 * q + 2 * j + r
                        te = mm(ps[64 * r:64 * r + 64, 6, 256 * j:256 * j + 256], ident[0:32, h:h + 1].broadcast_to([32, 64]), ecsT[:, :], True, True, w, t_ecs, inc=j == 1 and r == 1)
                tb = act(f2(ecB), ps[:, 6, :], ACT.Copy, te, yrel[0], t_fox)
                mark(6, tb)
                y = t1b[q % 2]
                t = yrel[0] = stt(f2(y), ps[:, 5, :], 0.5, f2(ecB), MUL, MUL, ty, tb, srd[q % 2], t_fox)
                mark(5, t)
                if q % 2 == 0 and g < 3:
                    yield from gprep(g + 1, 0)
                yield 0.6
                w = take(4)
                for c in range(2):
                    for j in range(2):
                        for r in range(2):
                            hl = 4 * (q % 2) + 2 * j + r
                            tk = mm(ps[64 * r:64 * r + 64, 4, 256 * j + P * c:256 * j + P * c + P], xdt[g % 2][:, c, 64 * hl:64 * hl + 64], Mb[q % 2][c][:, 2 * j + r, :], True, True, w, tM[q % 2][c], t_xd[c][g], inc=(j == 1 and r == 1))
                    Mrd[q % 2][c] = tk
                fr_x[g % 2] = tk
                t = tt(VE, f2(y), f2(y), ps[:, 4, :], ADD, t, tk)
                mark(4, t)
                for j in range(2):
                    i = 2 * q + j
                    t2 = stt(y[:, j, :], xbcT[:, i, NM:TT], dskh[:, i:i + 1], y[:, j, :], MUL, ADD, t, t_dk)
                zq = zT[:, 2 * q:2 * q + 2, :].rearrange("p j t -> p (j t)")
                t = stt(zq, f2(y), 0.5, zq, MUL, MUL, t2, t_z[2 * q], t_z[2 * q + 1])
                srd[q % 2] = t
                sqt.append(act(f2(sqb[q % 2]), zq, ACT.Square, t, sqrd[q % 2], t_fox))
                t_yd[q] = sqt[q]
                if q > 0:
                    sums(q - 1)
                if g < 3:
                    yield from gprep(g + 1, 1 + q % 2)
                yield 0.6
            yield 1
            sums(7)
            yield 1

        lows[:] = [GP, VE]
        f = zproj()
        weave(ssd(), f, 1)
        run(f)
        t_ssd = [PE.last(), VE.last(), AC.last(), GP.last()]
        t = act(rst[:, :], ps[0:4, 7, 0:T], ACT.Sqrt, sqrd[1], t_eps, t_ssd, scale=1.0 / 512, bias=small[0:4, 2:3])
        mark(7, t)
        t_rs = rcp(rst2[:, :], rst[:, :], t)

        pTs = wk("pTs", [P, 2, T], 34 * 1024)
        pp = pair("pp", [P, 2, T], 36 * 1024)

        def ple_load(l, *w):
            return ld.once(pTs[:, :, :], pT[l].rearrange("(k p) t -> p k t", p=P), *w)

        def ple_parts(t, *w):
            te = act(pp[0][:, :, :], pTs[:, :, :], ACT.Copy, t, *w)
            return tt(VE, pp[1][:, :, :], pTs[:, :, :], f32(pp[0][:, :, :]), SUB, te, *w)

        t_pT = ple_load(0, t_ssd)

        yaH, yaL = pair("ya", [P, 8, T], 68096)
        yH = wk("yH", [P, 16, T], 84480, F32R)
        yL = wk("yL", [P, 16, T], 51712, F32R)
        mH, mL = pair("mg", [P, 8, T], WTOP - 16384)
        gT = wk("gT", [P, 16, T], 17408)
        t_ya = [None] * 8
        for k in range(8):
            te = act(yaH[:, k, :], oT[:, k, :], ACT.Copy, t_oz[k], t_ssd)
            t_ya[k] = tt(VE, yaL[:, k, :], oT[:, k, :], f32(yaH[:, k, :]), SUB, te)

        gbh = small[:, 144:160]
        t_gb = ts(VE, gbh, v(V_GB, 16), 0.5, None, MUL, None, t_v)
        t_g = [None] * 16
        t_y = [None] * 16

        def norm(j):
            g = j // 4
            t = stt(zT[:, j, :], zT[:, j, :], v(V_SSDN + j), ps[:, 2 + g // 2, 256 * (g % 2):256 * (g % 2) + 256], MUL, MUL, t_bcs, t_yd[j // 2])
            if j % 8 == 7:
                mark(2 + j // 8, t)
            te = act(yH[:, j, :], zT[:, j, :], ACT.Copy, t, t_ssd)
            t_y[j] = tt(VE, yL[:, j, :], zT[:, j, :], f32(yH[:, j, :]), SUB, te)

        for j in range(16):
            b, pb, tg = block(*u_x, T, t_u)
            sl = (j + 8) % 16
            t_g[j] = act(gT[:, j, :], pb, ACT.Tanh, tg, t_ssd, t_gb, bias=gbh[:, sl:sl + 1], scale=0.5)
            mark(b, t_g[j])
            if j == 1:
                w = [take(2), take(3)]
                for g in range(4):
                    t_bcs = mm(ps[:, 2 + g // 2, 256 * (g % 2):256 * (g % 2) + 256], ident[0:4, g:g + 1].broadcast_to([4, P]), rst2[:, :], True, True, w, t_rs, inc=True)
            if j > 1:
                norm(j - 2)
        norm(14)
        norm(15)

        t_pp = ple_parts(t_pT, t_ssd)

        for j in range(8):
            b, pb, tk = block(lambda k: yaH[:, k, :], lambda k: yaL[:, k, :], T, t_ya)
            t_g[j] = stt(gT[:, j, :], gT[:, j, :], 1.0, pb, ADD, MUL, tk, t_g[j])
            mark(b, t_g[j])
        t_mg = []
        U.lend([pair(f"la{i}", [P, D], 68096 + 8192 * i) for i in range(2)], UB[0], PE.last())
        for i in range(4):
            for part in range(2):
                for j in range(2):
                    o = 8 * part
                    b, pb, tk = block(lambda k: yH[:, o + k, :], lambda k: yL[:, o + k, :], T, t_y[o:o + 8], b=2 + 2 * (i % 2) + j, part=(part == 0, part == 1))
                    if part:
                        jj = 2 * i + j
                        t = stt(gT[:, 8 + jj, :], gT[:, 8 + jj, :], 1.0, pb, ADD, MUL, tk, t_g[8 + jj])
                        mark(b, t)
                        t = tt(VE, gT[:, jj, :], gT[:, jj, :], gT[:, 8 + jj, :], ADD, t, t_g[jj])
                        te = act(mH[:, jj, :], gT[:, jj, :], ACT.Copy, t, t_ssd)
                        t_mg.append(tt(VE, mL[:, jj, :], gT[:, jj, :], f32(mH[:, jj, :]), SUB, te))
        t_b1 = [PE.last(), VE.last(), AC.last()]

        KI = 1024
        hT = pair("h", [P, KB, T], 0)
        R = [wk(f"R{i}", [P, D], (16 + 4 * i if i < 4 else 60) * KI) for i in range(5)]
        tmp = [wk(f"tmp{i}", [P, T], 56 * KI + 1024 * i) for i in range(4)]
        acc = wk("acc", [P, 2, D], 40 * KI)
        rows_ = [0]
        rfree = [t_b1] * 5

        def bc(src, n=D):
            i = rows_[0] % 5
            rows_[0] += 1
            return i, R[i][:, 0:n], ld.once(R[i][:, 0:n], src.broadcast_to([P, n]), rfree[i])

        lst = small[:, 160:184].rearrange("p (h f) -> p h f", h=2)
        lmv = small[:, 184:192].rearrange("p (h f) -> p h f", h=2)

        def ln_stats(src, h, n, *w):
            st, mv = lst[:, h, 0:6 * n], lmv[:, h, :]
            for i in range(n):
                t = VE.do(lambda e, i=i, x=src(i): e.bn_stats(st[:, 6 * i:6 * i + 6], x), *w)
            t = VE.do(lambda e: e.bn_aggr(mv[:, 0:2], st), t)
            t = ts(VE, mv[:, 2:3], mv[:, 1:2], LN_EPS, None, ADD, None, t)
            return rsqrt(mv[:, 3:4], mv[:, 2:3], t)

        def ln(src, h, grow, brow, *w):
            t = ln_stats(lambda i: src[:, 512 * i:512 * i + 512], h, 2, *w)
            t = stt(src, src, lmv[:, h, 0:1], grow, SUB, MUL, t)
            return stt(src, src, lmv[:, h, 3:4], brow, MUL, ADD, t)

        def turn_h(h, *w):
            out_t = []
            for g in range(2):
                b = 6 + g
                wb_ = take(b)
                for k in range(4):
                    kk = 4 * g + k
                    tk = tr(ps[:, b, P * k:P * k + P], res[:, h, P * kk:P * kk + P], wb_, list(w), inc=k == 3)
                s_ = ps[:, b, :].rearrange("p (k t) -> p k t", k=4)
                oH, oL = (x[:, 4 * g:4 * g + 4, P * h:P * h + P] for x in hT)
                te = act(oH, s_, ACT.Copy, tk)
                tl = tt(VE, oL, s_, f32(oH), SUB, te)
                mark(b, tl)
                out_t.append(tl)
            return out_t

        def xh(p):
            return (lambda k: p[0][:, k, :]), (lambda k: p[1][:, k, :])

        def rows(us, x, b, h, k0, first, last, *w, give=False):
            wb_ = take(b) if first else None
            hs = slice(P * h, P * h + P)
            n = 0
            for i, u in enumerate(us):
                H, L, tu, _ = u
                for k in range(2):
                    kk = k0 + 2 * i + k
                    mm(ps[:, b, :], x[0][:, kk, hs], H[:, k, :], first and n == 0, False, wb_, tu, [t(kk) if callable(t) else t for t in w])
                    mm(ps[:, b, :], x[0][:, kk, hs], L[:, k, :], False, False)
                    n += 1
                    tk = mm(ps[:, b, :], x[1][:, kk, hs], H[:, k, :], False, last and n == 2 * len(us), inc=True)
                if give:
                    U.give(u, tk)
            return tk

        def late(us, n, x, b, h, k0, first, middle, *w):
            m = len(us) - n
            rows(us[:m], x, b, h, k0, first, False, *w, give=True)
            middle()
            return rows(us[m:], x, b, h, k0 + 2 * m, False, True, *w, give=True)

        def product(x, before, after, wide, middle=None):
            us, w = {}, {}
            U.flush()
            for h, j in ((0, 0), (0, 1), (1, 0), (1, 1)) if wide else ((0, 0), (1, 0), (0, 1), (1, 1)):
                if j == 0:
                    w[h] = before(h)
                    if h == 1 and wide:
                        after(0, tk)
                if h == 0:
                    us[j] = [U.get() for _ in range(4)]
                if middle and h == 1 and j == 1:
                    tk = late(us[j], 2, x, 5, 1, 0, True, middle, w[h])
                else:
                    tk = rows(us[j], x, 2 + 2 * h + j, h, 0, True, True, w[h], give=h == 1)
                if j == 1 and h == 0 and not wide:
                    after(h, tk)
            return tk

        def both(h):
            b = 2 + 2 * h

            def done(t):
                mark(b, t)
                mark(b + 1, t)
            return ps[:, b:b + 2, :].rearrange("p j f -> p (j f)"), done

        rb = [0]

        def rt(name, shape, dt=F32):
            n = 4
            for d in shape[1:]:
                n *= d
            o = W0 + 32 * KI + rb[0]
            rb[0] += (n + 31) // 32 * 32
            assert rb[0] <= 2048, rb[0]
            return sb(name, shape, o, dt)

        wr = rt("wr", [P, KB, 8])
        wrs = rt("wrs", [P, KB, 16], F32R)
        tab = rt("tab", [P, 8, 6])
        stab = rt("stab", [P, 9, 6])
        cnt = rt("cnt", [1, 2, 8], I32)
        key = rt("key", [P, 2, 8])
        cmp_ = rt("cmp", [P, 8, 8])
        lg = rt("lg", [P, 2, 8])
        m8 = rt("m8", [P, 2, 8])
        ixf = rt("ixf", [P, 2, 8])
        ix = rt("ix", [P, 2, 8], mybir.dt.uint32)
        gv = rt("gv", [P, 2, 4])
        sel = rt("sel", [P, 2, 8])
        g2 = rt("g2", [P, 2, 8])

        def route(t_in):
            io8 = cst[:, C_IO:C_IO + 8]
            te = act(wrs[:, :, 0:8], wr[:, :, :], ACT.Copy, t_wr)
            tw = tt(VE, wrs[:, :, 8:16], wr[:, :, :], f32(wrs[:, :, 0:8]), SUB, te)
            b = 0
            w = take(b)
            for h in range(2):
                hs = slice(P * h, P * h + P)
                for k in range(KB):
                    mm(ps[:, b, 16 * h:16 * h + 16], hT[0][:, k, hs], wrs[:, k, :], k == 0, False, w, t_in, tw)
                    tk = mm(ps[:, b, 16 * h:16 * h + 8], hT[1][:, k, hs], wrs[:, k, 0:8], False, k == 7, inc=k == 7)
            lp = ps[:, b, 0:32].rearrange("p (h c e) -> p h c e", h=2, c=2)
            tl = cp(VE, lg[:, :, :], lp[:, :, 1, :], tk)
            tl = tt(VE, lg[:, :, :], lg[:, :, :], lp[:, :, 0, :], ADD, tl)
            mark(b, tl)
            ts_ = []
            for h in range(2):
                t = VE.do(lambda e, h=h: e.max(out=m8[:, h, :], in_=lg[:, h, :]), tl)
                t = VE.do(lambda e, h=h: e.max_index(out=ix[:, h, :], in_max=m8[:, h, :], in_values=lg[:, h, :]), t)
                t = cp(VE, ixf[:, h, :], ix[:, h, :], t)
                tm = tt(VE, gv[:, h, 0:1], m8[:, h, 1:2], m8[:, h, 0:1], SUB, t)
                te = act(gv[:, h, 1:2], gv[:, h, 0:1], ACT.Exp, tm)
                tm = ts(VE, gv[:, h, 2:3], gv[:, h, 1:2], 1.0, None, ADD, None, te)
                tm = rcp(gv[:, h, 2:3], gv[:, h, 2:3], tm)
                tm = tt(VE, gv[:, h, 3:4], gv[:, h, 1:2], gv[:, h, 2:3], MUL, tm)
                ta = ts(VE, sel[:, h, :], io8, ixf[:, h, 0:1], None, ALU.is_equal, None, t)
                ts_.append(stt(sel[:, h, :], io8, ixf[:, h, 1:2], sel[:, h, :], ALU.is_equal, ADD, ta))
                ta = ts(VE, g2[:, h, :], io8, ixf[:, h, 0:1], gv[:, h, 2:3], ALU.is_equal, MUL, tm)
                tb = ts(VE, lg[:, h, :], io8, ixf[:, h, 1:2], gv[:, h, 3:4], ALU.is_equal, MUL, tm)
                tg = tt(VE, tab[:, :, 2 + h:3 + h].rearrange("p e o -> p (e o)"), g2[:, h, :], lg[:, h, :], ADD, ta, tb)
            return ts_, tg

        def slots_of(ts_, tg):
            b = 1
            w = take(b)
            mm(ps[:, b, 0:8], tri[:, 0:P], sel[:, 0, :], True, True, w, ts_)
            mm(ps[:, b, 8:16], tri[:, 0:P], sel[:, 1, :], True, False)
            mm(ps[:, b, 8:16], ones, sel[:, 0, :], False, True)
            mm(ps[:, b, 16:24], ones, sel[:, 0, :], True, False)
            tk = mm(ps[:, b, 16:24], ones, sel[:, 1, :], False, True, inc=True)

            def field(a, b=None):
                x = tab[:, :, a:b or a + 1]
                return x.rearrange("p e f -> p f e") if b else x.rearrange("p e f -> p (e f)")

            tot = ps[:, b, 16:24]
            io8 = cst[:, C_IO:C_IO + 8]
            t = tt(VE, sel[:, :, :], sel[:, :, :], ps[:, b, 0:16].rearrange("p (h e) -> p h e", h=2), MUL, tk)
            ti = cp(VE, field(5), io8)
            tc = cp(VE, field(4), tot, tk)
            tq = stt(key[:, 0, :], tot, 8.0, cst[:, C_KEY:C_KEY + 8], MUL, ADD)
            mark(b, tq)
            tp = ts(VE, field(0, 2), sel[:, :, :], -1.0, None, ADD, None, t)
            t = tt(VE, cmp_[:, :, :], key[:, 0:1, :].broadcast_to([P, 8, 8]), key[:, 0, :].unsqueeze(2).broadcast_to([P, 8, 8]), ALU.is_gt, tq)
            t = VE.do(lambda e: e.tensor_reduce(key[:, 1, :], cmp_[:, :, :], mybir.AxisListType.X, ADD), t)
            t = tt(VE, cmp_[:, :, :], key[:, 1:2, :].broadcast_to([P, 8, 8]), cst[:, C_RANK:C_RANK + 8].unsqueeze(2).broadcast_to([P, 8, 8]), ALU.is_equal, t)
            t = tt(VE, prod[:, :, :, :], cmp_[:, :, :].unsqueeze(2).broadcast_to([P, 8, 6, 8]), field(0, 6).unsqueeze(1).broadcast_to([P, 8, 6, 8]), MUL, t, ti, tc, tp, tg)
            t = VE.do(lambda e: e.tensor_reduce(stab[:, 0:8, :], prod[:, :, :, :], mybir.AxisListType.X, ADD), t)
            tm = ms(VE, stab[:, 8, :], -1.0)
            return [tm, cp(VE, cnt[:, :, :], stab[0:1, 0:8, 4:6].rearrange("p e f -> p f e"), t)]

        VAR = ((32, [(32, 0, 0)]), (64, [(64, 0, 0)]), (128, [(128, 0, 1)]), (160, [(128, 0, 1), (32, 128, 0)]),
               (192, [(128, 0, 1), (64, 128, 0)]), (256, [(128, 0, 1), (128, 128, 1)]))
        NE, NT, NS, NH = 8, 21, 7, 5
        order = [("1", 0), ("3", 0)]
        for i in range(1, 7):
            order += [("1", i), ("3", i), ("2", i - 1)]
        order.append(("2", 6))
        where = [229344 - 16384 * (NS - i) for i in (0, 1, 2, 6, 5, 4, 3)]
        slots = [sb(f"eslot{i}", [P, 4096], o) for i, o in enumerate(where)]
        lowp = [sb(f"elow{i}", [P, 4096], o, F32R) for i, o in enumerate(where)]
        s_m = [sem(f"m{i}") for i in range(NS)]
        s_rel = sem("rel")
        STEP_D, STEP_R = [48], [NT]
        num = {o: n for n, o in enumerate(order)}
        landed = [(s_m[n % NS], 16 * (n // NS + 1), STEP_D) for n in range(NT)]

        def tile_of(n, e):
            kind, i = order[n]
            c = slice(512 * i, 512 * i + 512)
            src = mw2[e, c, :] if kind == "2" else (mw1 if kind == "1" else mw3)[e, :, c]
            return src.rearrange("o (k p) c -> p (o k) c", p=P)

        def slot(n):
            return slots[n % NS][:, :].rearrange("p (k c) -> p k c", k=4 if order[n][0] == "2" else 8)

        def load_first(n, *w):
            ld.start(s_m[n % NS], slot(n), tile_of(n, slice(0, 1)), *w)

        def load_others(e):
            with e.Fori(1, NE) as i:
                x = e.value_load(cnt[0:1, 1, bass.ds(i, 1)], min_val=0, max_val=NE - 1)
                for n in range(NT):
                    e.wait_ge(s_rel, i * NT + (n - NS + 1))
                    e.dma_start(slot(n), tile_of(n, bass.ds(x, 1))).then_inc(s_m[n % NS], 16)

        plev = wk("plev", [P, 2, D], 48 * KI)
        upad = wk("upad", [P, 4, 286], 64 * KI)
        cz = [wk(f"cz{i}", [P, 4, P], 64 * KI + 2048 * i) for i in range(2)]
        ct = [wk(f"ct{i}", [P, 4, P], 56 * KI + 2048 * i) for i in range(2)]
        et = wk("et", [P, 2, D], 64 * KI)
        aT = pair("aT", [P, 22, T], 73 * KI)
        yb = wk("yb", [P, 4, T], 68 * KI + 512)
        qT = wk("qT", [P, 4, T], 72 * KI + 512)
        kT = wk("kT", [P, 4, T], 76 * KI + 512)
        vk = wk("vk", [P, 2, 512], 80 * KI + 512)
        Pn = [wk(f"Pn{i}", [P, 2, T], 84 * KI + 512 + 2048 * i) for i in range(4)]
        PTn = [wk(f"PTn{i}", [P, 2, T], 92 * KI + 512 + 2048 * i) for i in range(4)]
        na = [wk(f"na{i}", [P, 2, 2, T], 100 * KI + 512 + 4096 * i) for i in range(2)]
        ctap = [wk(f"ctap{i}", [P, T], 108 * KI + 512 + 1024 * i) for i in range(2)]
        mix = pair("mix", [P, 8, T], WTOP - 16 * KI)
        prod = wk("prod", [P, 8, 6, 8], 56 * KI)

        def unit_at(name, off):
            return pair(name, [P, D], off)

        t_pl = []

        def ple(j, t_pp, *w):
            us = [U.get()]
            for h in range(2):
                b = h if j == 0 else 1 - h
                tk = rows(us, pp, b, h, 0, True, True, t_pp, give=h == 1)
                t_pl.append(act(plev[:, h, 512 * j:512 * j + 512], ps[:, b, :], ACT.Copy, tk, *w, scale=0.5))
                mark(b, t_pl[-1])
                yield 1

        Pt = wk("Pt", [P, 2, T], 72 * KI)
        Pgt = wk("Pgt", [P, 2, 2, P], 74 * KI)
        cur = rt("cur", [P, 2, 6])
        s_pt, s_ysb = sem("pt"), sem("ysb")
        EACH = [1]

        def places(i, *w):
            t = VE.do(lambda e: e.tensor_copy(cur[:, 1, :], stab[:, i(), :].rearrange("p o f -> p (o f)")), *w)
            for h in range(2):
                VE.do(lambda e, h=h: e.tensor_scalar(Pt[:, h, :], cst[:, C_IO:C_IO + T], cur[:, 1, h:h + 1], None, ALU.is_equal), t,
                      inc=True if h == 0 else s_pt)

        def place_first():
            t_route.extend(slots_of(*routed[0]))
            places(lambda: slice(0, 1), t_route)

        i_np, r_np, t_np = bc(norm_post)
        i_ig, r_ig, t_ig = bc(ln_in_g)
        i_ib, r_ib, t_ib = bc(ln_in_b)
        U.lend([unit_at(f"lw{i}", 84480 + 8192 * i) for i in range(2)], UB[0], t_b1)
        t_h = [None, None]

        def after_out(h, tk):
            src, done = both(h)
            ss, mq, rs = small[:, 20 + h:21 + h], small[:, 22 + h:23 + h], small[:, 24 + h:25 + h]
            t = act(acc[:, h, :], src, ACT.Square, tk, t_b1, acc=ss)
            t = ts(VE, mq, ss, 0.25 / D, EPS, MUL, ADD, t)
            t = rsqrt(rs, mq, t)
            t = stt(acc[:, h, :], src, rs, r_np, MUL, MUL, t, t_np)
            done(t)
            t = stt(res[:, h, :], acc[:, h, :], 0.5, res[:, h, :], MUL, ADD, t)
            t_h[h] = ln(res[:, h, :], h, r_ig, r_ib, t, t_ig, t_ib)

        t_hT, t_route = [], []

        def turn_first(*w):
            t_hT[:] = turn_h(0, t_h[0], *w)

        tk_o = product((mH, mL), lambda h: lambda k: t_mg[k], after_out, True, lambda: turn_first(t_b1))

        def second_half():
            after_out(1, tk_o)
            rfree[i_np] = rfree[i_ig] = rfree[i_ib] = t_h[1]


        t_w2 = None
        t_old = t_b1
        for l in range(2):
            vo = V_L + VL_N * l
            if l == 0:
                i_bv, r_bv, t_bv = bc(b_in2[0:1, 2048:2560], 512)
                i_bo, r_bo, t_bo = bc(b_out2[0:1, :])
            t_lay = [PE.last(), VE.last(), AC.last()]
            t_v = []
            t_pl.clear()
            for h in range(2):
                if h:
                    t_hT += turn_h(1, t_h[1], t_old)
                if h == 0:
                    second_half()
                if h == 0:
                    run(ple(0, t_pp, t_old))
                    us = [U.get() for _ in range(4)]
                tk = rows(us, hT, 2 + h, h, 0, True, True, t_hT, give=h == 1)
                t_v.append(tt(VE, vk[:, h, :], ps[:, 2 + h, :], r_bv, ADD, tk, t_bv, t_lay))
                mark(2 + h, t_v[h])
            rfree[i_bv] = t_v[1]
            bgh, bq8 = small[:, 192 + 8 * l:196 + 8 * l], small[:, 196 + 8 * l:200 + 8 * l]
            t_bg = ts(VE, bgh, v(vo + VL_BIN + 4, 4), 0.5, None, MUL, None)
            t_bq = ts(VE, bq8, v(vo + VL_BIN + 8, 4), 0.125, None, MUL, None)
            hh = xh(hT)
            lows[:] = [GP]
            tz = [ms(GP, upad[:, :, 0:15], 0.0, t_lay), ms(GP, upad[:, :, 271:286], 0.0)]
            t_uu = []
            trel = [None] * 4
            t_y = [None] * 4
            t_q, t_k = [None] * 4, [None] * 4
            t_mix = [None] * 8
            t_na = [None] * 4
            na_rd = [t_lay, t_lay]

            def load_na(i):
                t_na[i] = ld.once(na[i % 2][:, :, :, :], na_bias[l][:, :, 2 * i:2 * i + 2, :], na_rd[i % 2])

            load_na(0)
            load_na(1)

            def ag():
                for i in range(2):
                    ta = []
                    for j in (2 * i, 2 * i + 1):
                        b, pb, tk = block(*hh, T, t_hT)
                        t = act(yb[:, j, :], pb, ACT.Identity, tk, t_lay, bias=v(vo + VL_BIN + j))
                        mark(b, t)
                        ta.append(t)
                        yield 2.6
                    for j in (2 * i, 2 * i + 1):
                        b, pb, tk = block(*hh, T, t_hT)
                        g_ = act(tmp[j % 4][:, :], pb, ACT.Tanh, tk, t_bg, trel[j % 4], bias=bgh[:, j:j + 1], scale=0.5)
                        mark(b, g_)
                        trel[j % 4] = stt(upad[:, j, 15:271], tmp[j % 4][:, :], 1.0, yb[:, j, :], ADD, MUL, ta, g_, tz)
                        t_uu.append(trel[j % 4])
                        yield 2.4

            CP = 28

            def taps(E, out, j, d, t):
                cw = v(vo + VL_CW + 31 * j + d)
                if t is None:
                    return ts(E, out, upad[:, j, d:d + T], cw, None, MUL, None, t_uu[j])
                if E is GP:
                    t = ts(E, ctap[j % 2][:, :], upad[:, j, d:d + T], cw, None, MUL, None, t, t_lay)
                    return tt(E, out, out, ctap[j % 2][:, :], ADD, t)
                return stt(out, upad[:, j, d:d + T], cw, out, MUL, ADD, t)

            def conv():
                for i in range(2):
                    blocks = (2 * i, 2 * i + 1)
                    t, tp = [None] * 4, [None] * 4
                    for d in range(CP, 31):
                        for j in blocks:
                            tp[j] = taps(GP, tmp[j][:, :], j, d, tp[j])
                    for d in range(CP):
                        for j in blocks:
                            t[j] = taps(VE, yb[:, j, :], j, d, t[j])
                        yield 16 / CP
                    for j in blocks:
                        t_add = tt(VE, yb[:, j, :], yb[:, j, :], tmp[j][:, :], ADD, t[j], tp[j])
                        t_y[j] = act(yb[:, j, :], yb[:, j, :], ACT.Identity, t_add, scale=0.5, bias=v(vo + VL_CB + j))
                    yield 1

            def qk(i, n):
                dst, tl, bias, sc = ((qT, t_q, bq8, 0.125), (kT, t_k, v(vo + VL_BIN + 12, 4), 1.0))[n]
                for j in (2 * i, 2 * i + 1):
                    b, pb, tk = block(*hh, T, t_hT)
                    tl[j] = act(dst[:, j, :], pb, ACT.Identity, tk, t_bq, t_lay, bias=bias[:, j:j + 1], scale=sc)
                    mark(b, tl[j])
                    yield 2.6

            pn, ptt, trd, od = [None] * 8, [None] * 8, [None] * 8, [None] * 4

            def score(st):
                for h in (2 * st, 2 * st + 1):
                    b, r = 2 + h % 2, 64 * (h % 2)
                    w = take(b)
                    for t in range(2):
                        tk = mm(ps[:, b, T * t:T * t + T], qT[r:r + 64, st, P * t:P * t + P], kT[r:r + 64, st, :], True, True, w, t_q[st], t_k[st], inc=t == 1)
                    p = Pn[h % 4]
                    c = 2 * h
                    es = []
                    for t in range(2):
                        tm_ = neg_max(p[:, t, :], ps[:, b, T * t:T * t + T], na[st % 2][:, t, h % 2, :], nmx[:, c + t:c + t + 1], tk, t_na[st], trd[h - 4] if h > 3 else None, t_lay)
                        es.append(act(p[:, t, :], p[:, t, :], ACT.Exp, tm_, bias=nmx[:, c + t:c + t + 1], scale=-1.0, acc=rsm[:, c + t:c + t + 1]))
                    mark(b, tm_)
                    na_rd[st % 2] = tm_
                    rr = rcp(riv[:, c:c + 2], rsm[:, c:c + 2], es)
                    for t in range(2):
                        pn[h] = act(p[:, t, :], p[:, t, :], ACT.Copy, rr, scale=riv[:, c + t:c + t + 1])
                if st < 2:
                    load_na(st + 2)
                yield 0.2

            def turn_p(st):
                for h in (2 * st, 2 * st + 1):
                    b = 4 + h % 2
                    w = take(b)
                    for kb in range(2):
                        for t in range(2):
                            trd[h] = tr(ps[:, b, T * kb + P * t:T * kb + P * t + P], Pn[h % 4][:, t, P * kb:P * kb + P], w, pn[h], inc=kb + t == 2)
                    ptt[h] = cp((AC, VE)[h % 2], PTn[h % 4][:, :, :].rearrange("p k t -> p (k t)"), ps[:, b, :], trd[h], od[h // 2 - 2] if h > 3 else None, t_lay)
                    mark(b, ptt[h])
                yield 0.7

            def values(i):
                w = take(7)
                for kb in range(2):
                    for h in (2 * i, 2 * i + 1):
                        r = 64 * (h % 2)
                        tk = mm(ps[r:r + 64, 7, 0:T], vk[:, kb, 64 * h:64 * h + 64], PTn[h % 4][:, kb, :], kb == 0, kb == 1, w, ptt[h], t_v, inc=kb == 1)
                od[i] = tk
                te = act(mix[0][:, 4 + i, :], ps[:, 7, 0:T], ACT.Copy, tk, t_lay, scale=2.0)
                t_mix[4 + i] = stt(mix[1][:, 4 + i, :], ps[:, 7, 0:T], 2.0, f32(mix[0][:, 4 + i, :]), MUL, SUB, te)
                mark(7, t_mix[4 + i])
                yield 0.4

            def conv_ln():
                tx = [None, None]
                for h in range(2):
                    b = (6, 0)[h]
                    w = take(b)
                    for j in range(4):
                        tk = tr(ps[:, b, P * j:P * j + P], yb[:, j, P * h:P * h + P], w, t_y[j], inc=j == 3)
                    t = ln_stats(lambda i: ps[:, b, :], h, 1, tk)
                    tx[h] = ts(VE, f2(cz[h]), ps[:, b, :], lmv[:, h, 0:1], lmv[:, h, 3:4], SUB, MUL, t, t_y)
                    mark(b, tx[h])
                    yield 0.1
                for h in range(2):
                    z, zt = cz[h], ct[h]
                    b = (1, 6)[h]
                    w = take(b)
                    for j in range(4):
                        tk = tr(ps[:, b, P * j:P * j + P], z[:, j, :], w, tx[h], inc=j == 3)
                    for j in range(4):
                        te = act(z[:, j, :], ps[:, b, P * j:P * j + P], ACT.Identity, tk, scale=v(vo + VL_CG + j), bias=v(vo + VL_CBT + j))
                    mark(b, te)
                    t = act(f2(zt), f2(z), ACT.Tanh, te, t_y, scale=0.5)
                    t = stt(f2(z), f2(zt), 1.0, f2(z), ADD, MUL, t)
                    oH, oL = (x[:, 0:4, P * h:P * h + P] for x in mix)
                    te = act(oH, z[:, :, :], ACT.Copy, t, t_lay)
                    t_mix[h] = tt(VE, oL, z[:, :, :], f32(oH), SUB, te)
                    yield 0.1

            def chain(*parts):
                for p in parts:
                    yield from p

            def one(g):
                yield next(g)

            q2, k2, ln2, pl2 = qk(1, 0), qk(1, 1), conv_ln(), ple(1, t_pp, t_old)
            m = chain(ag(), qk(0, 0), qk(0, 1), score(0), one(q2), score(1), one(q2), turn_p(0), one(k2), turn_p(1), one(k2),
                      values(0), score(2), values(1), one(ln2), score(3), one(ln2), turn_p(2), one(pl2), one(ln2), values(2),
                      one(ln2), turn_p(3), one(pl2), values(3))
            for _ in range(4):
                next(m)
            weave(m, conv(), 1)
            t_ac = []
            for h in range(2):
                t_ac.append(stt(acc[:, h, :], res[:, h, :], ALPHA, r_bo, MUL, ADD, t_h[h], t_bo))
            rfree[i_bo] = t_ac[1]
            t_nat = [PE.last(), VE.last(), AC.last()]
            if l == 0:
                t_pT = ple_load(1, t_pl)
            i_g, r_g, t_rg = bc(ln1_g[l:l + 1, :])
            i_b, r_b, t_rb = bc(ln1_b[l:l + 1, :])
            i_gb, r_gb, t_gbr = bc(gate_b[l:l + 1, :])
            if l == 1:
                load_first(0, t_nat)
            lows[:] = [VE, GP]
            if l == 0:
                U.lend([unit_at(f"ln{i}", 72 * KI + 512 + 8192 * i) for i in range(4)], UB[1], t_nat)

            def after_mix(h, tk):
                src, done = both(h)
                t = stt(res[:, h, :], src, 0.5, acc[:, h, :], MUL, ADD, tk, t_ac)
                done(t)
                t_h[h] = ln(res[:, h, :], h, r_g, r_b, t, t_rg, t_rb)

            t_qk = PE.last()
            tk_m = product(mix, lambda h: lambda k: t_mix[0:2] if k < 4 else t_mix[k], after_mix, l == 0,
                           (lambda: turn_first(t_qk)) if l == 0 else None)
            t_mixd = PE.last()
            if l == 1:
                load_first(1, t_nat)
                load_first(2, t_mixd)
            t_e, routed = [], []

            def before_gate(h):
                if h == 0 and l == 1:
                    turn_first(t_qk)
                if h == 1:
                    t_hT.extend(turn_h(1, t_h[1], t_qk))
                if h == 0:
                    after_mix(1, tk_m)
                if l == 1 and h == 1:
                    routed.append(route(t_hT))
                return list(t_hT)

            def after_gate(h, tk):
                src, done = both(h)
                t = tt(VE, et[:, h, :], src, r_gb, ADD, tk, t_gbr, t_mix[1])
                done(t)
                if l == 1 and h == 1:
                    VE.do(lambda e: e.memset(cur[:, 0, :], 0.0), inc=s_ysb)
                t = act(et[:, h, :], et[:, h, :], ACT.Tanh, t, scale=0.5)
                t = stt(et[:, h, :], et[:, h, :], 1.0, plev[:, h, :], ADD, MUL, t, t_pl)
                t_e.append(stt(acc[:, h, :], res[:, h, :], ALPHA, et[:, h, :], MUL, ADD, t, t_h[h], t_ac))

            tk_g = product(hT, before_gate, after_gate, l == 0, place_first if l == 1 else None)
            after_gate(1, tk_g)
            if l == 1:
                break
            rfree[i_g] = rfree[i_b] = t_h[1]
            rfree[i_gb] = t_e[1]
            i_g, r_g, t_rg = bc(ln2_g[0:1, :])
            i_b, r_b, t_rb = bc(ln2_b[0:1, :])
            t_l2 = [t_rg, t_rb]
            i_bv, r_bv, t_bv = bc(b_in2[1:2, 2048:2560], 512)
            i_bo, r_bo, t_bo = bc(b_out2[1:2, :])
            t_wr = ld.once(wr[:, :, :], w_router.rearrange("(k p) c -> p k c", p=P), t_b1)
            t_pp = ple_parts(t_pT, t_pl)
            t_a = [None] * 22
            trel = [None] * 4
            t_w2 = [PE.last(), VE.last(), AC.last()]
            for i in range(11):
                s_ = []
                for j in (2 * i, 2 * i + 1):
                    b, pb, tk = block(*hh, T, t_hT, b=j % 2)
                    t = act(tmp[j % 4][:, :], pb, ACT.Silu, tk, trel[j % 4])
                    mark(b, t)
                    s_.append(t)
                for j in (2 * i, 2 * i + 1):
                    b, pb, tk = block(*hh, T, t_hT, b=2 + j % 2)
                    z = tmp[j % 4]
                    t = tt(VE, z[:, :], z[:, :], pb, MUL, tk, s_)
                    mark(b, t)
                    te = act(aT[0][:, j, :], z[:, :], ACT.Copy, t, t_w2)
                    t_a[j] = trel[j % 4] = tt(VE, aT[1][:, j, :], z[:, :], f32(aT[0][:, j, :]), SUB, te, t_w2)
            t_old = [PE.last(), VE.last(), AC.last()]
            U.lend([unit_at("lf0", 64 * KI), unit_at("lf1", 117 * KI)], UB[2], t_w2)
            for n in range(11):
                us = [U.get()]
                for h in range(2):
                    rows(us, aT, 2 + 2 * h, h, 2 * n, n == 0, n == 10, t_a[2 * n:2 * n + 2], give=h == 1)
            for n in range(6):
                us = [U.get()]
                for h in range(2):
                    rows(us, aT, 3 + 2 * h, h, 2 * n, n == 0, False, t_a, give=h == 1)
            us = [U.get() for _ in range(5)]

            def after_ffn(h, tk):
                src, done = both(h)
                t = tt(VE, res[:, h, :], src, acc[:, h, :], ADD, tk, t_e[h])
                done(t)
                t_h[h] = ln(res[:, h, :], h, r_g, r_b, t, t_l2)

            after_ffn(0, rows(us, aT, 3, 0, 12, False, True))
            tk_f = late(us, 1, aT, 5, 1, 12, False, lambda: turn_first(t_old))

            def second_half():
                after_ffn(1, tk_f)
                rfree[i_g] = rfree[i_b] = t_h[1]

        raw_, part_ = U.left(parts)
        for n, w in enumerate((raw_[0:2], [raw_[2], part_[0]], part_[1:3], part_[3:5])):
            load_first(3 + n, w)
        for n in range(NS, NT):
            load_first(n, (s_rel, n - NS + 1))
        SP.wait(t_route)
        SP.q.append(load_others)

        xTf = wk("xTf", [P, KB, T], 0)
        xTH = wk("xTH", [P, KB, T], 0, F32R)
        xTL = wk("xTL", [P, KB, T], 8 * KI, F32R)
        ysb = wk("ysb", [P, 2, D], 16 * KI)
        s1 = [wk(f"s1_{i}", [P, 512], 16 * KI + 2048 * i) for i in range(2)]
        ab = [wk(f"ab{i}", [P, 512], 20 * KI + 2048 * i) for i in range(2)]
        Hb = [wk(f"Hb{i}", [P, 1024], k * KI, F32R) for i, k in enumerate((24, 28, 34, 48, 52))]
        Pg = wk("Pg", [P, 2, T], 38 * KI)
        aTf = [wk(f"aTf{i}", [P, 4, T], (56 + 4 * i) * KI) for i in range(2)]
        aTH = [wk(f"aTH{i}", [P, 4, T], (56 + 4 * i) * KI, F32R) for i in range(2)]
        aTL = [wk(f"aTL{i}", [P, 4, T], (64 + 4 * i) * KI, F32R) for i in range(2)]
        PE.wait(t_route, t_h)
        VE.wait(t_route, t_e)
        AC.wait(t_route, t_e, t_h)
        for E in (PE, VE, AC):
            E.loop()
        for limit, blocks in VAR:
            for E in (PE, VE, AC):
                E.variant()
            BF = [[VE.start(), AC.start()] for _ in range(4)] + [[(s_ysb, 1, EACH), AC.start()] for _ in range(4)]
            ns = 128 if limit <= 128 else 256
            nbk = len(blocks)
            split = [k for k in range(nbk) if blocks[k][2]]
            whole = [k for k in range(nbk) if not blocks[k][2]]

            t_H, t_L, t_use, t_raw = [], [], [], {}

            def highs():
                while split and len(t_H) < min(4 * NT, len(t_use) + NH - 1):
                    m = len(t_H)
                    raw = slots[m // 4 % NS][:, 1024 * (m % 4):1024 * (m % 4) + 1024]
                    t_H.append(act(Hb[m % NH][:, :], raw, ACT.Copy, landed[m // 4], t_use[m - NH] if m >= NH else PE.start()))
                    if not whole:
                        low(m)

            def low(m):
                sl = slice(1024 * (m % 4), 1024 * (m % 4) + 1024)
                j = m // 4 % NS
                t_L.append(tt(VE, lowp[j][:, sl], slots[j][:, sl], f32(Hb[m % NH][:, :]), SUB, t_H[m], t_raw.get(m)))

            highs()
            t_x = []
            for k in range(KB):
                b = 4 + k // 2
                w = take(b) if k % 2 == 0 else None
                for h in range(2):
                    tk = mm(ps[:, b, T * (k % 2):T * (k % 2) + ns], res[:, h, P * k:P * k + P], Pt[:, h, 0:ns], h == 0, h == 1, w, (s_pt, 1, EACH), inc=h == 1)
                if k % 2:
                    src = ps[:, b, :].rearrange("p (k t) -> p k t", k=2)
                    t = tk
                    for B, off, r in blocks:
                        o = (slice(None), slice(k - 1, k + 1), slice(off, off + B))
                        if r:
                            te = act(xTH[o], src[o[0], :, o[2]], ACT.Copy, t)
                            t = tt(VE, xTL[o], src[o[0], :, o[2]], f32(xTH[o]), SUB, te)
                        else:
                            t = cp(VE if split or k % 4 == 3 else AC, xTf[o], src[o[0], :, o[2]], t)
                    mark(b, t)
                    t_x.append(t)
            t_gath = tk
            t_P = []

            def scatter_prep():
                t_c = VE.do(lambda e: e.tensor_copy(cur[:, 0, :], stab[:, bass.ds(VE.i, 1), :].rearrange("p o f -> p (o f)")))
                for k, (B, off, r) in enumerate(blocks):
                    nq = P // B
                    for h in range(2):
                        t = ts(VE, Pgt[:, k, h, :].rearrange("p (q b) -> p q b", q=nq),
                               cst[:, C_IO + off:C_IO + off + B].unsqueeze(1).broadcast_to([P, nq, B]),
                               cur[:, 0, h:h + 1], cur[:, 0, 2 + h:3 + h], ALU.is_equal, MUL, t_c)
                places(lambda: bass.ds(VE.i + 1, 1), t_gath)
                w = take(3)
                for k in range(nbk):
                    for h in range(2):
                        tk = tr(ps[:, 3, T * k + P * h:T * k + P * h + P], Pgt[:, k, h, :], w, t, inc=h == 1)
                t_P.append(cp(VE, Pg[:, 0:nbk, :], ps[:, 3, 0:T * nbk].rearrange("p (k t) -> p k t", k=nbk), tk))
                mark(3, t_P[0])

            hb = [0]

            def view(n, k):
                return slots[n % NS][:, :].rearrange("p (k c) -> p k c", k=k)

            def up(kind, i):
                n = num[kind, i]
                wt = view(n, 8)
                out_ = []
                for k in whole:
                    B, off, _ = blocks[k]
                    nq = P // B
                    N = 512 // nq
                    b = hb[0] % 3
                    hb[0] += 1
                    w = take(b)
                    for kk in range(8):
                        for q in range(nq):
                            end = q == nq - 1 and (kk % 2 == 1 if split else kk == 7)
                            inc = s_rel if end and not split else end
                            t = mm(ps[B * q:B * q + B, b, 0:N], xTf[:, kk, off:off + B], wt[:, kk, N * q:N * q + N], kk == 0, kk == 7, w, landed[n], t_x[kk // 2], inc=inc)
                        if split and kk % 2:
                            t_raw[4 * n + kk // 2] = t
                    out_.append((k, b, N, t if split else (s_rel, n + 1, STEP_R)))
                if split and whole:
                    for m in range(4 * n, 4 * n + 4):
                        low(m)
                if split:
                    bs = []
                    for k in split:
                        bs.append((hb[0] % 3, take(hb[0] % 3)))
                        hb[0] += 1
                    for j in range(4):
                        m = 4 * n + j
                        H = Hb[m % NH][:, :].rearrange("p (k c) -> p k c", k=2)
                        L = lowp[n % NS][:, 1024 * j:1024 * j + 1024].rearrange("p (k c) -> p k c", k=2)
                        for k, (b, w) in zip(split, bs):
                            xs_ = slice(blocks[k][1], blocks[k][1] + P)
                            for q in range(2):
                                kk = 2 * j + q
                                mm(ps[:, b, :], xTH[:, kk, xs_], H[:, q, :], kk == 0, False, w, t_H[m], t_x[j])
                                mm(ps[:, b, :], xTL[:, kk, xs_], H[:, q, :], False, False)
                                end = q == 1
                                t = mm(ps[:, b, :], xTH[:, kk, xs_], L[:, q, :], False, kk == 7, t_L[m], inc=end and (s_rel if j == 3 and k == split[-1] else True))
                                if end and j == 3 and k == split[-1]:
                                    t = (s_rel, n + 1, STEP_R)
                        t_use.append(t)
                        highs()
                        if j == 3:
                            for k, (b, w) in zip(split, bs):
                                out_.append((k, b, 512, t))
                return out_

            t_s, t_ab, t_at = [None] * 2, [None] * 2, [[None] * 2, [None] * 2]
            t_tr = [PE.start(), PE.start()]
            t_y = [[None, None], [None, None]]

            def tile1(i):
                for k, b, N, t in up("1", i):
                    t_s[k] = act(s1[k][:, 0:N], ps[:, b, 0:N], ACT.Silu, t, t_ab[k] or PE.start())
                    mark(b, t_s[k])

            def tile3(i):
                for k, b, N, t in up("3", i):
                    t_ab[k] = tt(VE, ab[k][:, 0:N], s1[k][:, 0:N], ps[:, b, 0:N], MUL, t, t_s[k], t_tr[k])
                    mark(b, t_ab[k])

            def turn(i):
                free = (s_rel, num["2", i - 2] + 1, STEP_R) if i > 1 else PE.start()
                for k, (B, off, r) in enumerate(blocks):
                    nq = P // B
                    nn = 4 // nq
                    b = 3
                    if k == 1:
                        b = hb[0] % 3
                        hb[0] += 1
                    w = take(b)
                    for n in range(nn):
                        t_tr[k] = tr(ps[:, b, P * n:P * n + P], ab[k][:, P * n:P * n + P], w, t_ab[k], inc=n == nn - 1)
                    if r:
                        s_ = ps[:, b, :].rearrange("p (n b) -> p n b", n=4)
                        oH, oL = aTH[i % 2][:, :, off:off + P], aTL[i % 2][:, :, off:off + P]
                        te = act(oH, s_, ACT.Copy, t_tr[k], free)
                        t_at[i % 2][k] = tt(VE, oL, s_, f32(oH), SUB, te, free)
                    else:
                        o = aTf[i % 2][:, :, off:off + B].rearrange("p (q n) b -> p n q b", q=nq)
                        s_ = ps[:, b, 0:P * nn].rearrange("p (n q b) -> p n q b", n=nn, q=nq)
                        t_at[i % 2][k] = cp(VE, o, s_, t_tr[k], free)
                    mark(b, t_at[i % 2][k])

            def tile2(i):
                n = num["2", i]
                wt = view(n, 4)
                steps = [(kk, j) for kk in range(4) for j in range(2)] if i < 6 else [(kk, j) for j in range(2) for kk in range(4)]
                for k in whole:
                    B, off, _ = blocks[k]
                    nq = P // B
                    w = [take(4 + 2 * k), take(5 + 2 * k)] if i == 0 else None
                    for kk, j in steps:
                        q = kk % nq
                        end = kk == 3 and j == 1
                        t = mm(ps[B * q:B * q + B, 4 + 2 * k + j, :], aTf[i % 2][:, kk, off:off + B], wt[:, kk, 512 * j:512 * j + 512],
                               i == 0 and kk < nq, i == 6 and kk >= 4 - nq, w, landed[n], t_at[i % 2][k],
                               inc=s_rel if end and not split else j == 1 or kk == 3)
                        if end and not split:
                            t = (s_rel, n + 1, STEP_R)
                        if j == 1:
                            t_raw[4 * n + kk] = t
                        t_y[k][j] = t
                if split and whole:
                    for m in range(4 * n, 4 * n + 4):
                        low(m)
                if split:
                    for kk, j in steps:
                        m = 4 * n + kk
                        H = Hb[m % NH]
                        L = lowp[n % NS][:, 1024 * kk:1024 * kk + 1024]
                        js = slice(512 * j, 512 * j + 512)
                        for k in split:
                            w = [take(4 + 2 * k), take(5 + 2 * k)] if i == 0 and kk == 0 else None
                            xs_ = slice(blocks[k][1], blocks[k][1] + P)
                            aH, aL = aTH[i % 2][:, kk, xs_], aTL[i % 2][:, kk, xs_]
                            first, last = i == 0 and kk == 0, i == 6 and kk == 3
                            o = ps[:, 4 + 2 * k + j, :]
                            mm(o, aH, H[:, js], first, False, w, t_H[m], t_at[i % 2][k])
                            mm(o, aL, H[:, js], False, False)
                            rel = j == 1 and kk == 3 and k == split[-1]
                            t = mm(o, aH, L[:, js], False, last, t_L[m], inc=s_rel if rel else j == 1 or kk == 3)
                            if rel:
                                t = (s_rel, n + 1, STEP_R)
                            t_y[k][j] = t
                        if j == 1:
                            t_use.append(t)
                            highs()

            tile1(0)
            tile3(0)
            scatter_prep()
            for i in range(1, 7):
                tile1(i)
                turn(i - 1)
                tile3(i)
                tile2(i - 1)
            turn(6)
            tile2(6)
            t_yy = [[], (s_ysb, 2, EACH)]
            for k in range(nbk):
                t_yy[0].append(act(ysb[:, k, 0:512], ps[:, 4 + 2 * k, :], ACT.Copy, t_y[k][0], t_tr))
            for k in range(nbk):
                VE.do(lambda e, k=k: e.tensor_copy(ysb[:, k, 512:1024], ps[:, 5 + 2 * k, :]), t_y[k][1], t_tr, inc=s_ysb if k == nbk - 1 else True)
            for j in range(2):
                for h in range(2):
                    b = 2 * h + j
                    w = take(b)
                    for k in range(nbk):
                        tk = mm(ps[:, b, :], Pg[:, k, P * h:P * h + P], ysb[:, k, 512 * j:512 * j + 512], k == 0, k == nbk - 1, w, t_P, t_yy[j], inc=k == nbk - 1)
                    if j:
                        tt(VE, acc[:, h, :], acc[:, h, :], ps[:, 2 * h:2 * h + 2, :].rearrange("p j f -> p (j f)"), ADD, tk)
            for E in (PE, VE, AC):
                E.end_variant()
        for E in (PE, VE, AC):
            E.end_loop(NE)

        orow = wk("orow", [P, 2, D], 16 * KI)
        r_g, r_b = slots[0][:, 0:D], slots[0][:, D:2 * D]
        done = (s_rel, (NE - 1) * NT + (NT - 1) // NS * NS + 1)
        t_l2 = [ld.once(r_g, ln2_g[1:2, :].broadcast_to([P, D]), done), ld.once(r_b, ln2_b[1:2, :].broadcast_to([P, D]), done)]
        t_out = []
        t_end = [VE.last(), PE.last()]
        for h in range(2):
            t = ln_stats(lambda i: acc[:, h, 512 * i:512 * i + 512], h, 2, t_end)
            t = stt(orow[:, h, :], acc[:, h, :], lmv[:, h, 0:1], r_g, SUB, MUL, t, t_l2)
            t = stt(orow[:, h, :], orow[:, h, :], lmv[:, h, 3:4], r_b, MUL, ADD, t)
            t_out.append(ld.once(out[0, P * h:P * h + P, :], orow[:, h, :], t))
        SP.wait(t_out)

        block_ = ctx.enter_context(nc.Block())
        block_.sync(lambda e: SP.emit(e))
        def count(i):
            return cnt[0:1, 0, bass.ds(i, 1)]

        limits = [lim for lim, _ in VAR]
        block_.tensor(lambda e: PE.emit(e, NE, count, limits))
        block_.vector(lambda e: VE.emit(e, NE, count, limits))
        block_.scalar(lambda e: AC.emit(e, NE, count, limits))
        block_.gpsimd(lambda e: GP.emit(e))


def fcols(a):
    return a.reshape(-1, P).T


def layout(inputs):
    import numpy as np

    g = {k: np.asarray(a) for k, a in inputs.items()}
    i = np.arange(P)
    c = np.zeros((P, NCONST), np.float32)
    c[:, C_ID:C_ID + 128] = i[:, None] == i
    c[:, C_U:C_U + 128] = i[:, None] > i
    c[:, C_T:C_T + TT] = i[:, None] <= np.arange(TT)
    c[:, C_ONE:C_ONE + 128] = 1.0
    c[:, C_MASK:C_MASK + TT] = np.where(np.arange(TT) - 144 <= i[:, None], 0.0, -1e30)
    c[:, C_IO:C_IO + T] = np.arange(T)
    c[:, C_KEY:C_KEY + 8] = -np.arange(8)
    c[:, C_KEY] = 8192
    c[:, C_RANK:C_RANK + 8] = RANKS
    v = np.zeros((P, NVEC), np.float32)
    v[:, V_PRE:V_PRE + 8] = fcols(g["norm_pre"][0])
    v[:, V_CW:V_CW + 96] = g["conv_w"][0].reshape(4, 24, P).transpose(2, 1, 0).reshape(P, 96)
    v[:, V_CB:V_CB + 24] = fcols(g["conv_b"][0])
    v[:, V_DSK:V_DSK + 16] = fcols(np.repeat(g["d_skip"][0], 64))
    v[:, V_SSDN:V_SSDN + 16] = fcols(g["ssd_norm"][0])
    v[:, V_GB:V_GB + 16] = fcols(g["gate_bias"][0])
    v[:, V_ING:V_ING + 8] = fcols(g["ln_in_g_2"])
    v[:, V_INB:V_INB + 8] = fcols(g["ln_in_b_2"])
    v[0:32, V_DTFB] = g["dt_bias"][0]
    v[32:48, V_DTFB] = g["fgate_bias"][0]
    v[0:32, V_SGN] = 1.0
    v[32:48, V_SGN] = -1.0
    for l in range(2):
        o = V_L + l * VL_N
        v[:, o + VL_BIN:o + VL_BIN + 16] = fcols(g["b_in_2"][l, 0:2048])
        v[:, o + VL_CW:o + VL_CW + 124] = g["conv_w_2"][l].reshape(31, 4, P).transpose(2, 1, 0).reshape(P, 124)
        for col, name in ((VL_CB, "conv_b_2"), (VL_CG, "conv_ln_g_2"), (VL_CBT, "conv_ln_b_2"), (VL_G1, "ln1_g_2"),
                          (VL_B1, "ln1_b_2"), (VL_G2, "ln2_g_2"), (VL_B2, "ln2_b_2")):
            a = fcols(g[name][l])
            v[:, o + col:o + col + a.shape[1]] = a
    q = np.arange(T)
    r, cc = q // 64, q % 64
    dr = r[None, :] - r[:, None] + 7
    dc = np.clip(cc[None, :] - cc[:, None] + 15, 0, 30)
    win = np.clip(cc - 8, 0, 48)[:, None]
    ok = (cc[None, :] >= win) & (cc[None, :] < win + 16)
    nb = g["rpb_2"][:, :, dr, dc]
    nb = np.where(ok, nb, np.float32(-1e30)).astype(np.float32)
    nb = nb.reshape(2, 8, 2, P, T).transpose(0, 3, 2, 1, 4)
    d = {
        "x": g["x"], "meta": g["meta_tokens"], "consts": c, "vecs": v,
        "onehot": np.ascontiguousarray(np.broadcast_to(np.eye(16, dtype=np.float32)[:, :, None], (16, 16, T))), "w_in": g["w_in"][0], "norm_post": g["norm_post"],
        "w_att": g["w_proj_att"][0], "w_ssd": g["w_proj_ssd"][0], "w_out": g["w_out"][0], "a_log": g["a_log"],
        "ln_in_g": g["ln_in_g_2"][None], "ln_in_b": g["ln_in_b_2"][None], "w_in2": g["w_in_2"], "b_in2": g["b_in_2"],
        "na_bias": nb, "w_out2": g["w_out_2"], "b_out2": g["b_out_2"], "ln1_g": g["ln1_g_2"], "ln1_b": g["ln1_b_2"],
        "w1": g["ffn_w1_2"][0], "w3": g["ffn_w3_2"][0], "w2": g["ffn_w2_2"][0],
        "pT": g["p_2"][:, 0].transpose(0, 2, 1), "ple_w": g["ple_w_2"], "gate_w": g["ple_gate_w_2"],
        "gate_b": g["ple_gate_b_2"], "ln2_g": g["ln2_g_2"], "ln2_b": g["ln2_b_2"], "w_router": g["w_router_2"][0],
        "mw1": g["moe_w1_2"][0], "mw3": g["moe_w3_2"][0], "mw2": g["moe_w2_2"][0],
    }
    return {k: np.ascontiguousarray(a) for k, a in d.items()}


def kernel(**inputs):
    import numpy as np
    import concourse.bacc as _bacc
    from concourse.bass_utils import run_bass_kernel_spmd as _run

    arrays = layout(inputs)
    nc = _bacc.Bacc("TRN2", target_bir_lowering=False, num_devices=1)
    args = [nc.dram_tensor(k, a.shape, mybir.dt.from_np(a.dtype), kind="ExternalInput").ap() for k, a in arrays.items()]
    out = nc.dram_tensor("out", (1, T, D), F32, kind="ExternalOutput").ap()
    bass_hybrid_conformer_moe(nc, *args, out)
    return _run(nc, [arrays], core_ids=[0]).results[0]["out"]
```

```python
import math
from contextlib import ExitStack

import concourse.bass as bass
from concourse import mybir

ALU = mybir.AluOpType
ACT = mybir.ActivationFunctionType
F32 = mybir.dt.float32
F32R = mybir.dt.float32r
I32 = mybir.dt.int32

P = 128
D = 1024
T = 256
NM = 16
TT = T + NM
KB = D // P
EPS = 1e-6
RANKS = (0, 1, 6, 2, 5, 3, 4, 7)
LN_EPS = 1e-5
ALPHA = 4.0 ** 0.25
BIG = 3.0e38
SB0 = 16512

C_ID, C_U, C_T, C_ONE, C_MASK, C_IO = 0, 128, 256, 528, 656, 928
C_KEY, C_RANK = 1184, 1192
NCONST = 1200

V_PRE, V_CW, V_CB, V_DSK, V_SSDN, V_GB = 0, 8, 104, 128, 144, 160
V_ING, V_INB, V_DTFB, V_SGN, V_ALOG = 176, 184, 192, 193, 194
V_L = 195
VL_BIN, VL_CW, VL_CB, VL_CG, VL_CBT, VL_G1, VL_B1, VL_G2, VL_B2, VL_N = 0, 16, 140, 144, 148, 152, 160, 168, 176, 184
NVEC = V_L + 2 * VL_N


def flat(ws):
    for w in ws:
        if isinstance(w, list):
            yield from flat(w)
        elif w is not None:
            yield w


class Eng:

    def __init__(self, name, sem):
        self.name, self.sem, self.n, self.q, self.seen = name, sem, 0, [], {}
        self.step, self.bodies, self.i, self.lastinc, self.inside = [0], None, 0, None, False

    def wait(self, *toks):
        for t in flat(toks):
            s, v = t[0], t[1]
            if self.seen.get(s.name, 0) < v:
                self.seen[s.name] = v
                if len(t) == 2:
                    self.q.append(lambda e, s=s, v=v: e.wait_ge(s, v))
                else:
                    self.q.append(lambda e, s=s, v=v, k=t[2]: e.wait_ge(s, self.i * k[0] + v))

    def do(self, fn, *toks, inc=True):
        self.wait(*toks)
        if not inc:
            self.q.append(fn)
            return None
        if inc is not True:
            self.q.append(lambda e: fn(e).then_inc(inc, 1))
            return None
        self.n += 1
        add = [1]
        self.lastinc = add
        self.q.append(lambda e: fn(e).then_inc(self.sem, add[0]))
        return self.last()

    def last(self):
        return (self.sem, self.n, self.step) if self.inside else (self.sem, self.n)

    def loop(self):
        self.pre, self.n0, self.bodies, self.inside = self.q, self.n, [], True

    def variant(self):
        self.q, self.n, self.seen = [], self.n0, {}

    def end_variant(self):
        self.bodies.append((self.q, self.n - self.n0, self.lastinc))

    def end_loop(self, iters):
        self.step[0] = max(n for _, n, _ in self.bodies)
        for _, n, add in self.bodies:
            add[0] += self.step[0] - n
        self.q, self.seen, self.inside = [], {}, False
        self.n = self.n0 + iters * self.step[0]

    def start(self):
        return (self.sem, self.n0, self.step)

    def emit(self, e, iters=0, count=None, limits=None):
        if self.bodies is not None:
            for f in self.pre:
                f(e)
            with e.Fori(0, iters) as i:
                self.i = i
                n = e.value_load(count(i), min_val=0, max_val=T)

                def pick(v):
                    if v == len(self.bodies) - 1:
                        for f in self.bodies[v][0]:
                            f(e)
                        return
                    with e.If(n < limits[v] + 1):
                        for f in self.bodies[v][0]:
                            f(e)
                    with e.Else():
                        pick(v + 1)

                pick(0)
        for f in self.q:
            f(e)


class Load:

    def __init__(self, eng, sems):
        self.eng, self.sems, self.count, self.next = eng, sems, {}, 0

    def slot(self):
        s = self.sems[self.next]
        self.next += 1
        return s

    def start(self, sem, dst, src, *toks):
        self.eng.wait(*toks)
        self.count[sem.name] = self.count.get(sem.name, 0) + 16
        self.eng.q.append(lambda e: e.dma_start(dst, src).then_inc(sem, 16))
        return (sem, self.count[sem.name])

    def once(self, dst, src, *toks):
        return self.start(self.slot(), dst, src, *toks)


class Ring:

    def __init__(self, load, slots):
        self.load, self.slots = load, slots
        self.sems = [load.slot() for _ in slots]
        self.plan, self.landed = [], []
        self.issued = 0
        self.back = []

    def issue(self, *toks):
        i = self.issued
        if i >= len(self.plan):
            return
        j = i % len(self.slots)
        k, c, src = self.plan[i]
        dst = self.slots[j][:, 0:k * c].rearrange("p (k c) -> p k c", k=k)
        self.landed.append(self.load.start(self.sems[j], dst, src, *toks))
        self.issued += 1

    def view(self, i):
        k, c, _ = self.plan[i]
        return self.slots[i % len(self.slots)][:, 0:k * c].rearrange("p (k c) -> p k c", k=k), self.landed[i]

    def give(self, tok):
        self.back.append(tok)
        self.issue(tok)


class Units:

    def __init__(self, ring, parts, split):
        self.ring, self.split = ring, split
        self.plan, self.made, self.where, self.cut = [], [], [], []
        self.free, self.rest = [(p, None, None) for p in parts], []
        self.taken = 0

    def tile(self, k, c, src, units):
        self.ring.plan.append((k, c, src))
        for n, u in enumerate(units):
            self.plan.append((len(self.ring.plan) - 1, u, n == len(units) - 1))

    def ahead(self, upto=None):
        while len(self.made) < (upto or len(self.plan)):
            m = len(self.made)
            i = next((i for i, f in enumerate(self.free) if f[2] is None or m < f[2]), None)
            if i is None:
                return
            part, last, limit = self.free.pop(i)
            t, (k0, k1, c0, c1), end = self.plan[m]
            raw, landed = self.ring.view(t)
            H, L = (x[:, :].rearrange("p (k c) -> p k c", k=k1 - k0) for x in part)
            tok = self.split(m, raw[:, k0:k1, c0:c1], H, L, landed, last)
            self.made.append((H, L, tok, m))
            self.where.append((part, limit))
            self.cut.append(tok)
            if end:
                self.ring.give(self.cut)
                self.cut = []

    def lend(self, parts, limit, *toks):
        self.free += [(p, list(toks), limit) for p in parts]
        self.ahead()

    def flush(self):
        self.free += self.rest
        self.rest = []
        self.ahead()

    def get(self):
        if self.taken == len(self.made):
            self.flush()
        self.taken += 1
        return self.made[self.taken - 1]

    def give(self, unit, tok):
        part, limit = self.where[unit[3]]
        self.free += self.rest
        self.rest = [(part, tok, limit)]
        self.ahead()


    def left(self, parts):
        n = len(self.ring.slots)
        raw = [self.ring.back[max(i for i in range(len(self.ring.back)) if i % n == j)] for j in range(n)]
        return raw, [next(t for p, t, _ in self.free + self.rest if p is q) for q in parts]


def weave(main, fill, n):
    acc = 0.0
    for m in main:
        acc += m * n
        while acc > 0:
            w = next(fill, None)
            acc = acc - w if w else -1e9


def chain(*gens):
    for g in gens:
        yield from g


def run(gen):
    for _ in gen:
        pass


def bass_hybrid_conformer_moe(nc, x, meta, consts, vecs, onehot, norm_pre, w_in, norm_post, w_att, w_ssd, w_out, a_log, ln_in_g, ln_in_b,
                              w_in2, b_in2, na_bias, w_out2, b_out2, ln1_g, ln1_b, w1, w3, w2, pT, ple_w, gate_w,
                              gate_b, ln2_g, ln2_b, w_router, mw1, mw3, mw2, out):
    with ExitStack() as ctx:
        def sem(name):
            return ctx.enter_context(nc.semaphore(name))

        PE, VE, AC, GP, SP = (Eng(n, sem("s_" + n)) for n in ("pe", "dve", "act", "pool", "sp"))
        ld = Load(SP, [sem(f"d{i}") for i in range(44)])
        ps = ctx.enter_context(nc.psum_tensor("ps", [P, 8, 512], F32))
        BF = [[] for _ in range(8)]

        top = [SB0]

        def sb(name, shape, off=None, dt=F32):
            n = 4
            for s in shape[1:]:
                n *= s
            n = (n + 31) // 32 * 32
            if off is None:
                off = top[0]
                top[0] += n
            assert off + n <= 229344, (name, off, n)
            return nc.alloc_sbuf_tensor_at(name, shape, dt, offset=off)

        def mm(o, l, r, start, stop, *w, inc=False):
            return PE.do(lambda e: e.matmul(o, l, r, start=start, stop=stop), *w, inc=inc)

        def tr(o, i, *w, inc=False):
            n = i.shape[0]
            b = i.base_partition() if callable(i.base_partition) else i.base_partition
            return PE.do(lambda e: e.transpose(o, i, ident[b:b + n, b:b + n]), *w, inc=inc)

        def act(o, i, f, *w, bias=0.0, scale=1.0, acc=None):
            if acc is None:
                return AC.do(lambda e: e.activation(o, i, f, bias=bias, scale=scale), *w)
            return AC.do(lambda e: e.activation(o, i, f, bias=bias, scale=scale, accum_out=acc), *w)

        def ts(E, o, i, s1, s2, op0, op1, *w):
            if s2 is None:
                return E.do(lambda e: e.tensor_scalar(o, i, s1, None, op0), *w)
            return E.do(lambda e: e.tensor_scalar(o, i, s1, s2, op0, op1), *w)

        def stt(o, i0, s, i1, op0, op1, *w):
            return VE.do(lambda e: e.scalar_tensor_tensor(out=o, in0=i0, scalar=s, in1=i1, op0=op0, op1=op1), *w)

        def tt(E, o, a, b, op, *w):
            return E.do(lambda e: e.tensor_tensor(o, a, b, op=op), *w)

        def cp(E, o, i, *w):
            if E is AC:
                return act(o, i, ACT.Copy, *w)
            return E.do(lambda e: e.tensor_copy(o, i), *w)

        def ms(E, o, v, *w):
            return E.do(lambda e: e.memset(o, v), *w)

        def rcp(o, i, *w):
            return VE.do(lambda e: e.reciprocal(o, i), *w)

        def neg_max(o, i0, i1, acc, *w):
            return VE.do(lambda e: e.tensor_tensor_reduce(o, i0, i1, -1.0, BIG, ALU.add, ALU.min, acc), *w)

        MUL, ADD, SUB, MAX = ALU.mult, ALU.add, ALU.subtract, ALU.max

        def mark(b, *toks):
            BF[b] = list(toks)

        def take(b):
            w = BF[b]
            BF[b] = []
            return w

        cst = sb("cst", [P, NCONST])
        vec = sb("vec", [P, NVEC])
        small = sb("small", [P, 256])
        tokv = sb("tokv", [P, 3, 48])
        adt = sb("adt", [P, 3, 32])
        dth = sb("dth", [P, 2, 32])
        dsx = sb("dsx", [P, 4, 32])
        ecsT = sb("ecsT", [32, T])
        arow = sb("arow", [P, 32])
        ident = cst[:, C_ID:C_ID + 128]
        strict = cst[:, C_U:C_U + 128]
        tri = cst[:, C_T:C_T + TT]
        ones = cst[:, C_ONE:C_ONE + 128]
        fmask = cst[:, C_MASK:C_MASK + TT]

        def v(c, n=1, p=P):
            return vec[0:p, c:c + n]

        res = sb("res", [P, 2, D])
        W0 = top[0]
        NR, NU = 3, 5
        ring = Ring(ld, [sb(f"raw{i}", [P, 2048], 229344 - 8192 * (i + 1)) for i in range(NR)])
        parts = [[sb(f"u{c}{i}", [P, 1024], 229344 - 8192 * (NR + i + 1) + 4096 * n, F32R) for n, c in enumerate("HL")]
                 for i in range(NU)]
        WTOP = 229344 - 8192 * (NR + NU) - W0

        def wk(name, shape, off, dt=F32):
            n = 4
            for d in shape[1:]:
                n *= d
            assert off + n <= WTOP, (name, off + n, WTOP)
            return sb(name, shape, W0 + off, dt)

        def pair(name, shape, off):
            n = 4
            for d in shape[1:]:
                n *= d
            return wk(name + "H", shape, off, F32R), wk(name + "L", shape, off + n, F32R)

        def f32(ap):
            return ap.bitcast(F32)

        lows = [GP, VE]

        def split(m, raw, H, L, *w):
            t = act(H, raw, ACT.Copy, *w)
            return [t, tt(lows[m % len(lows)], L, raw, f32(H), SUB, t, *w)]

        U = Units(ring, parts, split)

        def fm(w, c0, n, k0=0):
            for c in range(c0, c0 + n, 256):
                m = min(256, c0 + n - c)
                U.tile(8, m, w[k0 * P:(k0 + 8) * P, c:c + m].rearrange("(k p) c -> p k c", p=P),
                       [(0, 8, i, i + 128) for i in range(0, m, 128)])

        def tm(w, c0, nk):
            for k in range(0, nk, 4):
                m = min(4, nk - k)
                U.tile(m, 512, w[k * P:(k + m) * P, c0:c0 + 512].rearrange("(k p) c -> p k c", p=P),
                       [(i, i + 2, 0, 512) for i in range(0, m, 2)])

        XB, DT, ZA, Q, K, V, FG, GA = 2048, 5120, 5152, 6176, 7200, 8224, 9248, 9264
        U.tile(8, 128, None, [(0, 8, 0, 128)])
        for c0, n in ((K, 1024), (Q, 1024), (V, 1024), (XB + 2048, 1024), (XB, 2048), (0, 2048), (ZA, 1024),
                      (GA + 1024, 1024), (GA, 1024)):
            fm(w_in, c0, n)
        fm(w_att, 0, 1024)
        for c in range(0, 1024, 256):
            fm(w_ssd, c, 256, 0)
            fm(w_ssd, c, 256, 8)
        tm(w_out, 0, 8)
        tm(w_out, 512, 8)
        UB = [len(U.plan)]

        def layer_plan(l):
            tm(ple_w[l], 0, 2)
            tm(w_in2[l], 2048, 8)
            for c in (0, 512, 256, 768, 1024, 1536, 1280, 1792):
                fm(w_in2[l], c, 256)
            tm(ple_w[l], 512, 2)
            tm(w_out2[l], 0, 8)
            tm(w_out2[l], 512, 8)
            tm(gate_w[l], 0, 8)
            tm(gate_w[l], 512, 8)
            UB.append(len(U.plan))

        layer_plan(0)
        for c in range(0, 2816, 256):
            fm(w1, c, 256)
            fm(w3, c, 256)
        tm(w2, 0, 22)
        tm(w2, 512, 22)
        UB.append(len(U.plan))
        layer_plan(1)

        uH, uL = pair("u", [P, KB, TT], 0)
        xhat = wk("xhat", [P, 2, D], 17408)
        mhat = wk("mhat", [NM, D], 25600)
        min_ = wk("min_", [NM, D], 29696)
        sq = wk("sqj", [P, D], 33792)
        sp = wk("sp", [48, TT], 37888)
        dx = wk("dx", [48, 6, TT], 38976)

        grow = wk("grow", [P, D], 45568)
        t_x = [ld.once(res[:, 0, :], x[0, 0:P, :])]
        t_c = ld.once(ident, consts[:, C_ID:C_ID + 128])
        t_pre = ld.once(grow[:, :], norm_pre.broadcast_to([P, D]))
        t_x.append(ld.once(res[:, 1, :], x[0, P:T, :]))
        t_m = ld.once(min_[:, :], meta)
        qa = wk("qa", [80, 16, T], 51712)
        wdf = ring.slots[0][:, 0:1024].rearrange("p (k c) -> p k c", k=8)
        t = ms(GP, ring.slots[0][:, 0:1024], 0.0)
        ld.start(ring.sems[0], wdf[:, :, 0:32], w_in[:, DT:DT + 32].rearrange("(k p) c -> p k c", p=P), t)
        ring.landed.append(ld.start(ring.sems[0], wdf[:, :, 32:48], w_in[:, FG:FG + 16].rearrange("(k p) c -> p k c", p=P)))
        ring.issued = 1
        ring.issue()
        t_v = ld.once(vec[:, :], vecs)
        ring.issue()
        t_c2 = ld.once(cst[:, 128:NCONST], consts[:, 128:NCONST])
        t_oh = ld.once(qa[64:80, :, :], onehot)
        t_al = ld.once(arow[:, :], a_log.broadcast_to([P, 32]))

        t_half = ms(GP, small[:, 0:1], -0.5)
        t_eps = ms(GP, small[:, 2:3], EPS)

        def rsqrt(o, i, *w):
            n, c = i.shape
            return GP.do(lambda e: e.tensor_tensor(o, i, small[0:n, 0:1].broadcast_to([n, c]), op=ALU.pow), t_half, *w)

        toks = ((0, res[:, 0, :], xhat[:, 0, :], P, NM, t_x[0]), (1, res[:, 1, :], xhat[:, 1, :], P, NM + P, t_x[1]),
                (2, min_[:, :], mhat[:, :], NM, 0, t_m))
        t_n = []
        for i, src, dst, n, col, t in toks:
            ss, mq, rs = small[0:n, 4 + i:5 + i], small[0:n, 8 + i:9 + i], small[0:n, 12 + i:13 + i]
            if i == 1:
                t = VE.do(lambda e, src=src, ss=ss: e.tensor_tensor_reduce(xhat[:, 1, :], src, src, 1.0, 0.0, MUL, ADD, ss), t)
            else:
                t = act(sq[0:n, :], src, ACT.Square, AC.last(), t, acc=ss)
            t = ts(VE, mq, ss, 1.0 / D, EPS, MUL, ADD, t)
            t = rsqrt(rs, mq, t)
            t_n.append(stt(dst, src, rs, grow[0:n, :], MUL, MUL, t, t_pre))
        t_u = []
        for i, src, dst, n, col, _ in toks:
            for g in range(2):
                b = 2 * i + g
                for k in range(4):
                    kk = 4 * g + k
                    tk = tr(ps[:, b, n * k:n * k + n], dst[:, 128 * kk:128 * kk + 128], t_n[i], t_c, inc=k == 3)
                s_ = ps[:, b, 0:4 * n].rearrange("p (k t) -> p k t", k=4)
                oH, oL = (x_[:, 4 * g:4 * g + 4, col:col + n] for x_ in (uH, uL))
                te = act(oH, s_, ACT.Copy, tk)
                t_u.append(tt(VE, oL, s_, f32(oH), SUB, te))
                mark(b, t_u[-1])
            if i == 0:
                U.ahead(1)
        U.ahead()

        PB = [0]

        def mm3(o, xH, xL, k, n, h, first, last, *w, inc=False):
            H, L, tu, _ = h
            mm(o, H[:, k, :], xH, first, False, tu, *w)
            mm(o, H[:, k, :], xL, False, False)
            return mm(o, L[:, k, :], xH, False, last, inc=inc)

        def block(rH, rL, n, *acts, b=None, part=(True, True), unit=None):
            h = unit or U.get()
            if b is None:
                b = PB[0]
                PB[0] = 1 - b
            w = take(b) if part[0] else None
            for k in range(KB):
                tk = mm3(ps[:, b, 0:n], rH(k), rL(k), k, n, h, part[0] and k == 0, part[1] and k == KB - 1, w, list(acts), inc=k == KB - 1)
            U.give(h, tk)
            return b, ps[:, b, 0:n], tk

        u_all = (lambda k: uH[:, k, :], lambda k: uL[:, k, :])
        u_x = (lambda k: uH[:, k, NM:TT], lambda k: uL[:, k, NM:TT])

        b, pb, tk = block(*u_all, TT, t_u, b=6)
        X, E_, S1, S2, R, A6 = (dx[:, i, :] for i in range(6))
        t1 = ts(VE, X, pb[0:48], v(V_DTFB, p=48), v(V_SGN, p=48), ADD, MUL, tk, t_v)
        mark(6, t1)

        def softplus():
            t2 = stt(S1, X, -1.0, X, MUL, MAX, t1)
            te = act(E_, S1, ACT.Exp, t2, scale=-1.0)
            yield
            t3 = ts(VE, S1, E_, 2.0, None, ADD, None, te)
            t4 = rcp(R, S1, t3)
            yield
            t5 = tt(VE, S1, E_, R, MUL, t4)
            t6 = tt(VE, S2, S1, S1, MUL, t5)
            yield
            t7 = ts(VE, A6, S2, 1.0 / 15, None, MUL, None, t6)
            for n in (13, 11, 9, 7, 5, 3):
                t7 = stt(A6, A6, 1.0 / n, S2, ADD, MUL, t7)
                if n in (11, 7, 3):
                    yield
            t7 = stt(A6, A6, 1.0, S1, ADD, MUL, t7)
            yield
            t8 = ts(VE, X, X, 0.0, None, MAX, None, t1)
            t_sp.append(stt(sp[:, :], A6, 2.0, X, MUL, ADD, t7, t8))
            yield

        t_sp = []
        f_sp = softplus()

        def token_decays():
            for E in (PE, VE, AC, GP):
                E.wait(t_c2)
            b = 7
            w = take(b)
            for c, (c0, n) in enumerate(((0, NM), (NM, P), (NM + P, P))):
                tk = tr(ps[0:n, b, 48 * c:48 * c + 48], sp[:, c0:c0 + n], t_sp, w, inc=c == 2)
            tv1 = cp(VE, tokv[0:NM, 0, :], ps[0:NM, b, 0:48], tk)
            tv2 = cp(VE, tokv[:, 1:3, :], ps[:, b, 48:144].rearrange("p (c f) -> p c f", c=2), tk)
            mark(b, tv2)
            t_a = act(arow[:, :], arow[:, :], ACT.Exp, t_al)
            for c, n in enumerate((NM, P, P)):
                t_adt = stt(adt[0:n, c, :], tokv[0:n, c, 0:32], -1.0, arow[0:n, :], MUL, MUL, tv1, tv2, t_a)
            t_dth = ts(VE, dth[:, :, :], tokv[:, 1:3, 0:32], 0.5, None, MUL, None, tv2)
            b = 6
            w = take(b)
            mm(ps[0:NM, b, 0:TT], tokv[0:NM, 0, 32:48], tri[0:NM, 0:TT], True, False, w, tv1, tv2)
            mm(ps[0:NM, b, NM:TT], tokv[:, 1, 32:48], tri[:, 0:T], False, False)
            tk = mm(ps[0:NM, b, NM + P:TT], tokv[:, 2, 32:48], tri[:, 0:P], False, True, inc=True)
            t_ck = []
            for i in range(4):
                o = ka[64:80, 4 * i:4 * i + 4, :]
                s = ps[0:NM, b, 0:TT].unsqueeze(1).broadcast_to([NM, 4, TT])
                t_ck.append(act(o, s, ACT.Copy, tk))
            mark(b, t_ck[-1])
            return tv1, tv2, t_adt, t_dth, t_ck

        xbcT = wk("xbcT", [P, 24, TT], 17408)
        oT = wk("oT", [P, 8, T], 43520)
        ka = wk("ka", [80, 16, TT], 68096)
        vt = wk("vt", [P, 3, D], 85504)
        Pb = [wk(f"Pb{i}", [P, 416], 97792 + 1664 * i) for i in range(4)]
        PTb = [wk(f"PTb{i}", [P, 384], 104448 + 1536 * i) for i in range(4)]
        PMb = [wk(f"PMb{i}", [NM, 512], 110592 + 2048 * i) for i in range(2)]
        cacc = [wk(f"cacc{i}", [P, TT], 114688 + 1088 * i) for i in range(4)]
        ctn = [wk(f"ctn{i}", [P, TT], 119040 + 1088 * i) for i in range(2)]
        xc = [wk(f"xc{i}", [P, TT], 121216 + 1088 * i) for i in range(4)]
        vtmp = [wk(f"vtmp{i}", [P, TT], 125568 + 1088 * i) for i in range(2)]

        t_q, t_k = [None] * 16, [None] * 16
        for dst, rhs, n, sc, tl in ((ka, u_all, TT, 1.0, t_k), (qa, u_x, T, 0.125, t_q)):
            for j in range(8):
                b, pb, tk = block(*rhs, n, t_u)
                tl[2 * j] = act(dst[0:64, 2 * j, :], pb[0:64], ACT.Copy, tk, scale=sc)
                tl[2 * j + 1] = ts(VE, dst[0:64, 2 * j + 1, :], pb[64:128], sc, None, MUL, None, tk)
                mark(b, tl[2 * j], tl[2 * j + 1])
                next(f_sp, None)
            if dst is ka:
                tv1, tv2, t_adt, t_dth, t_ck = token_decays()
        t_vt = []
        use = [None, None]

        def turn_v(j, te):
            b = 6 + j % 2
            w = take(b)
            for c, (c0, n) in enumerate(((0, NM), (NM, P), (NM + P, P))):
                use[j % 2] = tr(ps[0:n, b, 128 * c:128 * c + 128], vtmp[j % 2][:, c0:c0 + n], te, w, inc=c == 2)
            ta = cp(VE, vt[0:NM, 0, 128 * j:128 * j + 128], ps[0:NM, b, 0:128], use[j % 2])
            tb = cp(VE, vt[:, 1:3, 128 * j:128 * j + 128], ps[:, b, 128:384].rearrange("p (c f) -> p c f", c=2), use[j % 2])
            mark(b, ta, tb)
            t_vt.extend([ta, tb])

        te = None
        for j in range(8):
            b, pb, tk = block(*u_all, TT, t_u)
            if j:
                turn_v(j - 1, te)
            te = act(vtmp[j % 2][:, :], pb, ACT.Copy, tk, use[j % 2])
            mark(b, te)
        turn_v(7, te)

        t_xb = [None] * 24

        def xbc():
            rel, relz = [None] * 4, [None] * 2
            pend = []

            def finish(j, n, t):
                a, z = cacc[n % 4], ctn[n % 2]
                te = act(z[:, :], a[:, :], ACT.Tanh, t, relz[n % 2], scale=0.5)
                t_xb[j] = rel[n % 4] = relz[n % 2] = stt(xbcT[:, j, :], z[:, :], 1.0, a[:, :], ADD, MUL, te, fr_x)

            for n, j in enumerate([j0 + i for j0 in (16, 20, 0, 4, 8, 12) for i in range(4)]):
                b, pb, tk = block(*u_all, TT, t_u)
                a, x_ = cacc[n % 4], xc[n % 4]
                cw = V_CW + 4 * j
                act(x_[:, :], pb, ACT.Copy, tk, rel[n % 4])
                t = act(a[:, :], pb, ACT.Identity, scale=v(cw + 3), bias=v(V_CB + j))
                mark(b, t)
                for d in (1, 2, 3):
                    t = stt(a[:, d:TT], x_[:, 0:TT - d], v(cw + 3 - d), a[:, d:TT], MUL, ADD, t)
                pend.append((j, n, t))
                if n > 1:
                    finish(*pend.pop(0))
                yield 1
            for p in pend:
                finish(*p)
            yield 1

        t_o = [None] * 8
        nmx = small[:, 32:64]
        rsm = small[:, 64:96]
        riv = small[:, 96:128]

        def fox():
            pn = [None] * 16
            ptt, pmt = [None] * 16, [None] * 8
            trd, od = [None] * 16, [None] * 8
            for st in range(10):
                if st < 8:
                    for h in (2 * st, 2 * st + 1):
                        b = 2 + h % 2
                        w = take(b)
                        mm(ps[:, b, 0:144], qa[:, h, 0:P], ka[:, h, 0:144], True, True, w, t_q[h], t_k[h], t_oh, t_ck[h // 4])
                        tk = mm(ps[:, b, 144:416], qa[:, h, P:T], ka[:, h, :], True, True, inc=True)
                        p = Pb[h % 4]
                        t0 = neg_max(p[:, 0:144], ps[:, b, 0:144], fmask[:, 128:272], nmx[:, 2 * h:2 * h + 1], tk, trd[h - 4] if h > 3 else None)
                        t1 = neg_max(p[:, 144:416], ps[:, b, 144:416], fmask, nmx[:, 2 * h + 1:2 * h + 2], tk)
                        mark(b, t1)
                        e0 = act(p[:, 0:144], p[:, 0:144], ACT.Exp, t0, bias=nmx[:, 2 * h:2 * h + 1], scale=-1.0, acc=rsm[:, 2 * h:2 * h + 1])
                        e1 = act(p[:, 144:416], p[:, 144:416], ACT.Exp, t1, bias=nmx[:, 2 * h + 1:2 * h + 2], scale=-1.0, acc=rsm[:, 2 * h + 1:2 * h + 2])
                        r = rcp(riv[:, 2 * h:2 * h + 2], rsm[:, 2 * h:2 * h + 2], e0, e1)
                        ts(VE, p[:, 0:144], p[:, 0:144], riv[:, 2 * h:2 * h + 1], None, MUL, None, r)
                        pn[h] = ts(VE, p[:, 144:416], p[:, 144:416], riv[:, 2 * h + 1:2 * h + 2], None, MUL, None, r)
                    yield 1
                if 1 <= st <= 8:
                    wm = take(6)
                    i = st - 1
                    for h in (2 * i, 2 * i + 1):
                        b = 4 + h % 2
                        w = take(b)
                        p = Pb[h % 4]
                        m0 = 256 * (h % 2)
                        tr(ps[:, b, 0:128], p[:, 16:144], w, pn[h])
                        tr(ps[:, b, 128:256], p[:, 160:288])
                        tk = tr(ps[:, b, 256:384], p[:, 288:416], inc=True)
                        tr(ps[0:NM, 6, m0:m0 + 128], p[:, 0:16], wm)
                        trd[h] = tr(ps[0:NM, 6, m0 + 128:m0 + 256], p[:, 144:160], inc=True)
                        ptt[h] = act(PTb[h % 4][:, :], ps[:, b, 0:384], ACT.Copy, tk, od[i - 2] if i > 1 else None)
                        mark(b, ptt[h])
                    pmt[i] = cp(VE, PMb[i % 2][:, :], ps[0:NM, 6, :], trd[2 * i + 1], od[i - 2] if i > 1 else None)
                    mark(6, pmt[i])
                    yield 1
                if st >= 2:
                    i = st - 2
                    w = take(7)
                    for c in range(3):
                        for h in (2 * i, 2 * i + 1):
                            r0 = 64 * (h % 2)
                            o = ps[r0:r0 + 64, 7, 0:T]
                            hs = slice(64 * h, 64 * h + 64)
                            if c == 0:
                                mm(o, vt[:, 1, hs], PTb[h % 4][:, 0:256], True, False, w, ptt[h], t_vt)
                            elif c == 1:
                                mm(o, vt[0:NM, 0, hs], PMb[i % 2][:, 256 * (h % 2):256 * (h % 2) + 256], False, False, pmt[i])
                            else:
                                tk = mm(ps[r0:r0 + 64, 7, P:T], vt[:, 2, hs], PTb[h % 4][:, 256:384], False, True, inc=True)
                    od[i] = tk
                    t_o[i] = act(oT[:, i, :], ps[:, 7, 0:T], ACT.Copy, tk)
                    mark(7, t_o[i])
                    yield 0.6

        fr_x = [t_u, t_sp, tv2]
        f = xbc()
        lows[:] = [GP]
        weave(fox(), f, 1)
        run(f)
        t_fox = [PE.last(), VE.last(), AC.last()]

        zT = wk("zT", [P, 16, T], 51712)
        xdt = [wk(f"xdt{i}", [P, 2, 512], 68096 + 4096 * i) for i in range(2)]
        hin = [wk(f"hin{i}", [P, 2, 512], 76288 + 4096 * i) for i in range(2)]
        cbT = wk("cbT", [P, 8, P], 84480)
        Btok = wk("Btok", [P, 512], 88576)
        Bm = wk("Bm", [NM, 512], 90624)
        xds = [wk(f"xds{i}", [P, 512], 92672 + 2048 * i) for i in range(2)]
        adT = [pair(f"adT{i}", [P, 4, P], 96768 + 4096 * i) for i in range(2)]
        Mb = [[wk(f"Mb{i}{c}", [P, 4, P], 104960 + 4096 * i + 2048 * c) for c in range(2)] for i in range(2)]
        ecB = wk("ecB", [P, 2, T], 113152)
        t1b = [wk(f"t1b{i}", [P, 2, T], 115200 + 2048 * i) for i in range(2)]
        sqb = [wk(f"sqb{i}", [P, 2, T], 119296 + 2048 * i) for i in range(2)]
        ztn = [wk(f"ztn{i}", [P, T], 123392 + 1024 * i) for i in range(3)]
        gsel = wk("gsel", [P, 4, 4], 126464)
        strictR = wk("strictR", [P, P], 126528, F32R)
        adp = [wk(f"adp{i}", [P, 2, 32], 127040 + 256 * i, dt) for i, dt in enumerate((F32R, F32))]
        rst = wk("rst", [4, T], 92672)
        rst2 = wk("rst2", [4, T], 94720)
        dskh = small[:, 128:144]
        t_sr = act(strictR[:, :], strict, ACT.Copy, t_fox)
        te = act(adp[0][:, :, :], adt[:, 1:3, :], ACT.Copy, t_adt, t_fox)
        t_ap = tt(VE, adp[1][:, :, :], adt[:, 1:3, :], f32(adp[0][:, :, :]), SUB, te, t_fox)
        t_gs = ms(GP, gsel[:, :, :], 0.0, t_fox)
        for g in range(4):
            t_gs = ms(GP, gsel[:, g, g:g + 1], 1.0, t_gs)
        t_dk = ts(VE, dskh, v(V_DSK, 16), 0.5, None, MUL, None, t_v)
        t_z = [None] * 16
        t_oz = [None] * 8
        t_yd = [None] * 8
        zrel = [None] * 3

        def zproj():
            for j in range(16):
                b, pb, tk = block(*u_x, T, t_u)
                z = ztn[j % 3]
                te = act(z[:, :], pb, ACT.Tanh, tk, zrel[j % 3], t_fox, scale=0.5)
                t_z[j] = zrel[j % 3] = stt(zT[:, j, :], z[:, :], 1.0, pb, ADD, MUL, te, t_fox)
                mark(b, t_z[j])
                yield 1
            for k in range(8):
                b, pb, tk = block(*u_x, T, t_u)
                z = ztn[k % 3]
                te = act(z[:, :], pb, ACT.Tanh, tk, zrel[k % 3], scale=0.5)
                t = stt(z[:, :], z[:, :], 1.0, pb, ADD, MUL, te)
                mark(b, t)
                t_oz[k] = zrel[k % 3] = stt(oT[:, k, :], oT[:, k, :], 0.5, z[:, :], MUL, MUL, t, t_o[k])
                yield 1

        gT = wk("gT", [P, 16, T], 17408)
        gt = [ztn[1 + j][:, :] if j < 2 else gT[:, j, :] for j in range(16)]
        gbh = small[:, 144:160]
        t_gb = ts(VE, gbh, v(V_GB, 16), 0.5, None, MUL, None, t_v)
        t_g = [None] * 16

        def gate(j):
            b, pb, tk = block(*u_x, T, t_u)
            sl = (j + 8) % 16
            t_g[j] = act(gt[j], pb, ACT.Tanh, tk, zrel[1 + j] if j < 2 else t_ssd, t_gb, bias=gbh[:, sl:sl + 1], scale=0.5)
            mark(b, t_g[j])
            yield 1

        def h8(ap, n):
            return ap.unsqueeze(2).broadcast_to([n, 8, 64])

        def hd(ap):
            return ap.rearrange("p (h d) -> p h d", h=8)

        def f2(a):
            return a[:, :, :].rearrange("p j t -> p (j t)")

        sqrd = [None, None]

        def ssd():
            ta, segd = [None, None], [None, None]
            SE = VE

            def prep(q):
                for c in range(2):
                    ta[c] = []
                    for E, o, i in zip((GP, SE), adT[c], (adp[0][:, :, :].bitcast(F32), adp[1])):
                        ta[c].append(tt(E, o[:, :, :], tri[:, 0:P].unsqueeze(1).broadcast_to([P, 4, P]),
                                        i[:, c, 4 * q:4 * q + 4].unsqueeze(2).broadcast_to([P, 4, P]), MUL, t_ap, t_fox, segd[c]))

            prep(0)
            w = take(2)
            for c in range(2):
                mm(ps[0:32, 2, P * c:P * c + P], adt[:, c + 1, :], tri[:, 0:P], True, True, w, t_adt)
            mm(ps[0:NM, 2, 256:288], strict[0:NM, 0:NM], adt[0:NM, 0, :], True, True)
            mm(ps[:, 2, 288:320], strict, adt[:, 1, :], True, True)
            tk = mm(ps[:, 2, 320:352], ones, adt[:, 1, :], True, True, inc=True)
            t_ecs = act(ecsT[:, :], ps[0:32, 2, 0:T], ACT.Exp, tk)
            te0 = act(dsx[0:NM, 0, :], ps[0:NM, 2, 256:288], ACT.Exp, tk)
            te1 = act(dsx[:, 1:3, :], ps[:, 2, 288:352].rearrange("p (c f) -> p c f", c=2), ACT.Exp, tk)
            mark(2, te1)
            w = take(3)
            for g in range(4):
                tk = tr(ps[:, 3, P * g:P * g + P], xbcT[:, 16 + g, NM:NM + P], w, t_xb[16:20], inc=g == 3)
            t_b1 = act(Btok[:, :], ps[:, 3, :], ACT.Copy, tk, t_fox)
            mark(3, t_b1)
            w = take(4)
            for g in range(4):
                tk = tr(ps[0:NM, 4, P * g:P * g + P], xbcT[:, 16 + g, 0:NM], w, inc=g == 3)
            t_b0 = act(Bm[:, :], ps[0:NM, 4, :], ACT.Copy, tk, t_fox)
            mark(4, t_b0)
            t_d0 = stt(dsx[0:NM, 0, :], tokv[0:NM, 0, 0:32], 0.25, dsx[0:NM, 0, :], MUL, MUL, te0)
            t_d1 = stt(dsx[:, 1, :], tokv[:, 1, 0:32], 0.25, dsx[:, 1, :], MUL, MUL, te1)
            yield 1
            t_cb = []
            for c in range(2):
                b = 2 + c
                w = take(b)
                c0 = NM + P * c
                for g in range(4):
                    tk = mm(ps[:, b, P * g:P * g + P], xbcT[:, 16 + g, c0:c0 + P], xbcT[:, 20 + g, c0:c0 + P], True, True, w, t_xb[20 + g], inc=g == 3)
                t_cb.append(stt(cbT[:, 4 * c:4 * c + 4, :], ps[:, b, :].rearrange("p (g s) -> p g s", g=4), 0.25,
                                tri[:, 0:P].unsqueeze(1).broadcast_to([P, 4, P]), MUL, MUL, tk, t_fox))
                mark(b, t_cb[c])
                yield 1
            rel = [None, None]
            t_xd = [[None] * 4 for _ in range(2)]
            t_h = [[None] * 4 for _ in range(2)]
            fr_x, fr_h = [None, None], [None, None]
            cnt_ = [0]

            def gprep(g, c):
                c0, m = ((0, NM), (NM, P), (NM + P, P))[c]
                g8 = slice(8 * g, 8 * g + 8)
                w = take(6)
                for j in range(4):
                    tk = tr(ps[0:m, 6, P * j:P * j + P], xbcT[:, 4 * g + j, c0:c0 + m], w, t_xb[4 * g + j], inc=j == 3)
                src = hd(ps[0:m, 6, :])
                if c > 0:
                    t = t_xd[c - 1][g] = tt(VE, hd(xdt[g % 2][:, c - 1, :]), src, h8(dth[:, c - 1, g8], P), MUL, tk, t_fox, t_dth, fr_x[g % 2])
                if c < 2:
                    n = cnt_[0]
                    cnt_[0] += 1
                    xd = xds[n % 2]
                    t = tt(VE, hd(xd[0:m, :]), src, h8(dsx[0:m, c, g8], m), MUL, tk, rel[n % 2], t_d0, t_d1, t_fox)
                mark(6, t)
                if c < 2:
                    yield 1
                    w = take(5)
                    bt = Bm if c == 0 else Btok
                    rel[n % 2] = tk = mm(ps[:, 5, :], bt[0:m, P * g:P * g + P], xd[0:m, :], True, True, w, t, t_b0, t_b1, inc=True)
                    if c == 0:
                        t_h[0][g] = act(hin[g % 2][:, 0, :], ps[:, 5, :], ACT.Copy, tk, t_fox, fr_h[g % 2])
                        mark(5, t_h[0][g])
                    else:
                        t = tt(VE, hd(hin[g % 2][:, 1, :]), hd(hin[g % 2][:, 0, :]), h8(dsx[:, 2, g8], P), MUL, t_h[0][g], te1, t_fox, fr_h[g % 2])
                        t_h[1][g] = tt(VE, hin[g % 2][:, 1, :], hin[g % 2][:, 1, :], ps[:, 5, :], ADD, t, tk)
                        mark(5, t_h[1][g])

            for c in range(3):
                yield from gprep(0, c)
                yield 1
            tM = [[None, None], [None, None]]
            Mrd = [[None, None], [None, None]]
            yrel, srd = [None], [None, None]
            wsum = take(7)
            sqt = []

            def seg(q):
                g = q // 2
                for c in range(2):
                    b = 2 + c
                    w = take(b)
                    mm(ps[:, b, :], strictR[:, :], f2(adT[c][0]), True, False, w, ta[c][0], t_sr)
                    segd[c] = tk = mm(ps[:, b, :], strictR[:, :], f2(adT[c][1]), False, True, ta[c][1], inc=True)
                    m = Mb[q % 2][c]
                    te = act(f2(m), ps[:, b, :], ACT.Exp, tk, Mrd[q % 2][c], t_fox)
                    mark(b, te)
                    tM[q % 2][c] = tt(VE, m[:, :, :], m[:, :, :], cbT[:, 4 * c + g:4 * c + g + 1, :].broadcast_to([P, 4, P]), MUL, te, t_cb)
                if q < 7:
                    prep(q + 1)

            def sums(q):
                for j in range(2):
                    i = 2 * q + j
                    tk = mm(ps[0:4, 7, 0:T], gsel[:, i // 4, :], sqb[q % 2][:, j, :], i == 0, i == 15, wsum, sqt[q], t_gs, inc=j == 1)
                sqrd[q % 2] = tk

            seg(0)
            for q in range(8):
                g = q // 2
                if q < 7:
                    seg(q + 1)
                w = take(5)
                for j in range(2):
                    for c in range(2):
                        c0 = NM + P * c
                        r0 = P * (2 * (q % 2) + j)
                        ty = mm(ps[:, 5, 256 * j + P * c:256 * j + P * c + P], hin[g % 2][:, c, r0:r0 + P], xbcT[:, 20 + g, c0:c0 + P], True, True, w, t_h[c][g], inc=(j == 1 and c == 1))
                fr_h[g % 2] = ty
                w = take(6)
                for j in range(2):
                    for r in range(2):
                        h = 4 * q + 2 * j + r
                        te = mm(ps[64 * r:64 * r + 64, 6, 256 * j:256 * j + 256], ident[0:32, h:h + 1].broadcast_to([32, 64]), ecsT[:, :], True, True, w, t_ecs, inc=j == 1 and r == 1)
                tb = act(f2(ecB), ps[:, 6, :], ACT.Copy, te, yrel[0], t_fox)
                mark(6, tb)
                y = t1b[q % 2]
                t = yrel[0] = stt(f2(y), ps[:, 5, :], 0.5, f2(ecB), MUL, MUL, ty, tb, srd[q % 2], t_fox)
                mark(5, t)
                if q % 2 == 0 and g < 3:
                    yield from gprep(g + 1, 0)
                yield 0.6
                w = take(4)
                for c in range(2):
                    for j in range(2):
                        for r in range(2):
                            hl = 4 * (q % 2) + 2 * j + r
                            tk = mm(ps[64 * r:64 * r + 64, 4, 256 * j + P * c:256 * j + P * c + P], xdt[g % 2][:, c, 64 * hl:64 * hl + 64], Mb[q % 2][c][:, 2 * j + r, :], True, True, w, tM[q % 2][c], t_xd[c][g], inc=(j == 1 and r == 1))
                    Mrd[q % 2][c] = tk
                fr_x[g % 2] = tk
                t = tt(VE, f2(y), f2(y), ps[:, 4, :], ADD, t, tk)
                mark(4, t)
                for j in range(2):
                    i = 2 * q + j
                    t2 = stt(y[:, j, :], xbcT[:, i, NM:TT], dskh[:, i:i + 1], y[:, j, :], MUL, ADD, t, t_dk)
                zq = zT[:, 2 * q:2 * q + 2, :].rearrange("p j t -> p (j t)")
                t = stt(zq, f2(y), 0.5, zq, MUL, MUL, t2, t_z[2 * q], t_z[2 * q + 1])
                srd[q % 2] = t
                sqt.append(act(f2(sqb[q % 2]), zq, ACT.Square, t, sqrd[q % 2], t_fox))
                t_yd[q] = sqt[q]
                if q > 0:
                    sums(q - 1)
                if g < 3:
                    yield from gprep(g + 1, 1 + q % 2)
                yield 0.6
            yield 1
            sums(7)
            yield 1

        lows[:] = [GP]
        f = chain(zproj(), gate(0), gate(1))
        weave(ssd(), f, 1.1)
        t_ssd = [PE.last(), VE.last(), AC.last(), GP.last()]
        t = act(rst[:, :], ps[0:4, 7, 0:T], ACT.Sqrt, sqrd[1], t_eps, t_ssd, scale=1.0 / 512, bias=small[0:4, 2:3])
        mark(7, t)
        t_rs = rcp(rst2[:, :], rst[:, :], t)

        pTs = wk("pTs", [P, 2, T], 34 * 1024)
        pp = pair("pp", [P, 2, T], 36 * 1024)

        def ple_load(l, *w):
            return ld.once(pTs[:, :, :], pT[l].rearrange("(k p) t -> p k t", p=P), *w)

        def ple_parts(t, *w):
            te = act(pp[0][:, :, :], pTs[:, :, :], ACT.Copy, t, *w)
            return tt(VE, pp[1][:, :, :], pTs[:, :, :], f32(pp[0][:, :, :]), SUB, te, *w)

        t_pT = ple_load(0, t_ssd)

        yaH, yaL = pair("ya", [P, 8, T], 68096)
        yH = wk("yH", [P, 16, T], 84480, F32R)
        yL = wk("yL", [P, 16, T], 51712, F32R)
        mH, mL = pair("mg", [P, 8, T], WTOP - 16384)
        t_ya = [None] * 8
        for k in range(8):
            te = act(yaH[:, k, :], oT[:, k, :], ACT.Copy, t_oz[k], t_ssd)
            t_ya[k] = tt(VE, yaL[:, k, :], oT[:, k, :], f32(yaH[:, k, :]), SUB, te)

        t_y = [None] * 16

        def norm(j):
            g = j // 4
            t = stt(zT[:, j, :], zT[:, j, :], v(V_SSDN + j), ps[:, 2 + g // 2, 256 * (g % 2):256 * (g % 2) + 256], MUL, MUL, t_bcs, t_yd[j // 2])
            if j % 8 == 7:
                mark(2 + j // 8, t)
            te = act(yH[:, j, :], zT[:, j, :], ACT.Copy, t, t_ssd)
            t_y[j] = tt(VE, yL[:, j, :], zT[:, j, :], f32(yH[:, j, :]), SUB, te)

        run(f)
        for j in range(2, 16):
            run(gate(j))
            if j == 3:
                w = [take(2), take(3)]
                for g in range(4):
                    t_bcs = mm(ps[:, 2 + g // 2, 256 * (g % 2):256 * (g % 2) + 256], ident[0:4, g:g + 1].broadcast_to([4, P]), rst2[:, :], True, True, w, t_rs, inc=True)
            if j > 3:
                norm(j - 4)
        for j in range(12, 16):
            norm(j)

        t_pp = ple_parts(t_pT, t_ssd)

        for j in range(8):
            b, pb, tk = block(lambda k: yaH[:, k, :], lambda k: yaL[:, k, :], T, t_ya)
            t_g[j] = stt(gt[j], gt[j], 1.0, pb, ADD, MUL, tk, t_g[j])
            mark(b, t_g[j])
        t_mg = []
        U.lend([pair(f"la{i}", [P, D], 68096 + 8192 * i) for i in range(2)], UB[0], PE.last())
        for i in range(4):
            for part in range(2):
                for j in range(2):
                    o = 8 * part
                    b, pb, tk = block(lambda k: yH[:, o + k, :], lambda k: yL[:, o + k, :], T, t_y[o:o + 8], b=2 + 2 * (i % 2) + j, part=(part == 0, part == 1))
                    if part:
                        jj = 2 * i + j
                        t = stt(gt[8 + jj], gt[8 + jj], 1.0, pb, ADD, MUL, tk, t_g[8 + jj])
                        mark(b, t)
                        t = tt(VE, gt[jj], gt[jj], gt[8 + jj], ADD, t, t_g[jj])
                        te = act(mH[:, jj, :], gt[jj], ACT.Copy, t, t_ssd)
                        t_mg.append(tt(VE, mL[:, jj, :], gt[jj], f32(mH[:, jj, :]), SUB, te))
        t_b1 = [PE.last(), VE.last(), AC.last()]

        KI = 1024
        hT = pair("h", [P, KB, T], 0)
        R = [wk(f"R{i}", [P, D], (16 + 4 * i if i < 4 else 60) * KI) for i in range(5)]
        tmp = [wk(f"tmp{i}", [P, T], 56 * KI + 1024 * i) for i in range(4)]
        acc = wk("acc", [P, 2, D], 40 * KI)
        rows_ = [0]
        rfree = [t_b1] * 5

        def bc(src, n=D):
            i = rows_[0] % 5
            rows_[0] += 1
            return i, R[i][:, 0:n], ld.once(R[i][:, 0:n], src.broadcast_to([P, n]), rfree[i])

        lst = small[:, 160:184].rearrange("p (h f) -> p h f", h=2)
        lmv = small[:, 184:192].rearrange("p (h f) -> p h f", h=2)

        def ln_stats(src, h, n, *w):
            st, mv = lst[:, h, 0:6 * n], lmv[:, h, :]
            for i in range(n):
                t = VE.do(lambda e, i=i, x=src(i): e.bn_stats(st[:, 6 * i:6 * i + 6], x), *w)
            t = VE.do(lambda e: e.bn_aggr(mv[:, 0:2], st), t)
            t = ts(VE, mv[:, 2:3], mv[:, 1:2], LN_EPS, None, ADD, None, t)
            return rsqrt(mv[:, 3:4], mv[:, 2:3], t)

        HC = (slice(0, 512), slice(512, 1024))

        def ln(src, h, pre, grow, brow, *w):
            st, mv = lst[:, h, :], lmv[:, h, :]
            for j, c in enumerate(HC):
                t = pre(j, c)
                t = VE.do(lambda e, j=j, c=c: e.bn_stats(st[:, 6 * j:6 * j + 6], src[:, c]), t)
            t = VE.do(lambda e: e.bn_aggr(mv[:, 0:2], st), t)
            t = ts(VE, mv[:, 2:3], mv[:, 1:2], LN_EPS, None, ADD, None, t)
            t_r = rsqrt(mv[:, 3:4], mv[:, 2:3], t)
            out = []
            for c in HC:
                t = stt(src[:, c], src[:, c], mv[:, 0:1], grow[:, c], SUB, MUL, t_r, *w)
                out.append(stt(src[:, c], src[:, c], mv[:, 3:4], brow[:, c], MUL, ADD, t))
            return out

        def turn_h(h, th, *w):
            out_t = []
            for g in range(2):
                b = 6 + g
                wb_ = take(b)
                for k in range(4):
                    kk = 4 * g + k
                    tk = tr(ps[:, b, P * k:P * k + P], res[:, h, P * kk:P * kk + P], wb_, th[g], list(w), inc=k == 3)
                s_ = ps[:, b, :].rearrange("p (k t) -> p k t", k=4)
                oH, oL = (x[:, 4 * g:4 * g + 4, P * h:P * h + P] for x in hT)
                te = act(oH, s_, ACT.Copy, tk)
                tl = tt(VE, oL, s_, f32(oH), SUB, te)
                mark(b, tl)
                out_t.append([te, tl])
            return out_t

        def xh(p):
            return (lambda k: p[0][:, k, :]), (lambda k: p[1][:, k, :])

        def rows(us, x, b, h, k0, first, last, wH, wL=None, give=False):
            def at(w, k):
                return w(k) if callable(w) else w

            wb_ = take(b) if first else None
            hs = slice(P * h, P * h + P)
            n = 0
            for i, u in enumerate(us):
                H, L, tu, _ = u
                for k in range(2):
                    kk = k0 + 2 * i + k
                    mm(ps[:, b, :], x[0][:, kk, hs], H[:, k, :], first and n == 0, False, wb_, tu, at(wH, kk))
                    mm(ps[:, b, :], x[0][:, kk, hs], L[:, k, :], False, False)
                    n += 1
                    tk = mm(ps[:, b, :], x[1][:, kk, hs], H[:, k, :], False, last and n == 2 * len(us), at(wL, kk), inc=True)
                if give:
                    U.give(u, tk)
            return tk

        def late(us, n, x, b, h, k0, first, middle, *w):
            m = len(us) - n
            rows(us[:m], x, b, h, k0, first, False, *w, give=True)
            middle()
            return rows(us[m:], x, b, h, k0 + 2 * m, False, True, *w, give=True)

        def product(x, before, after, wide, middle=None):
            us, w, tk = {}, {}, {0: [None, None], 1: [None, None]}
            U.flush()
            for h, j in ((0, 0), (0, 1), (1, 0), (1, 1)) if wide else ((0, 0), (1, 0), (0, 1), (1, 1)):
                if j == 0:
                    w[h] = before(h)
                    if h == 1 and wide:
                        after(0, tk[0])
                if h == 0:
                    us[j] = [U.get() for _ in range(4)]
                if middle and h == 1 and j == 1:
                    tk[h][j] = late(us[j], 2, x, 5, 1, 0, True, middle, *w[h])
                else:
                    tk[h][j] = rows(us[j], x, 2 + 2 * h + j, h, 0, True, True, *w[h], give=h == 1)
                if j == 1 and h == 0 and not wide:
                    after(h, tk[0])
            return tk[1]

        rb = [0]

        def rt(name, shape, dt=F32):
            n = 4
            for d in shape[1:]:
                n *= d
            o = W0 + 32 * KI + rb[0]
            rb[0] += (n + 31) // 32 * 32
            assert rb[0] <= 2048, rb[0]
            return sb(name, shape, o, dt)

        wr = rt("wr", [P, KB, 8])
        wrs = rt("wrs", [P, KB, 16], F32R)
        tab = rt("tab", [P, 8, 6])
        stab = rt("stab", [P, 9, 6])
        cnt = rt("cnt", [1, 2, 8], I32)
        key = rt("key", [P, 2, 8])
        cmp_ = rt("cmp", [P, 8, 8])
        lg = rt("lg", [P, 2, 8])
        m8 = rt("m8", [P, 2, 8])
        ixf = rt("ixf", [P, 2, 8])
        ix = rt("ix", [P, 2, 8], mybir.dt.uint32)
        gv = rt("gv", [P, 2, 4])
        sel = rt("sel", [P, 2, 8])
        g2 = rt("g2", [P, 2, 8])

        def route(t_in):
            io8 = cst[:, C_IO:C_IO + 8]
            te = act(wrs[:, :, 0:8], wr[:, :, :], ACT.Copy, t_wr)
            tw = tt(VE, wrs[:, :, 8:16], wr[:, :, :], f32(wrs[:, :, 0:8]), SUB, te)
            b = 0
            w = take(b)
            for h in range(2):
                hs = slice(P * h, P * h + P)
                for k in range(KB):
                    mm(ps[:, b, 16 * h:16 * h + 16], hT[0][:, k, hs], wrs[:, k, :], k == 0, False, w, t_in, tw)
                    tk = mm(ps[:, b, 16 * h:16 * h + 8], hT[1][:, k, hs], wrs[:, k, 0:8], False, k == 7, inc=k == 7)
            lp = ps[:, b, 0:32].rearrange("p (h c e) -> p h c e", h=2, c=2)
            tl = cp(VE, lg[:, :, :], lp[:, :, 1, :], tk)
            tl = tt(VE, lg[:, :, :], lg[:, :, :], lp[:, :, 0, :], ADD, tl)
            mark(b, tl)
            ts_ = []
            for h in range(2):
                t = VE.do(lambda e, h=h: e.max(out=m8[:, h, :], in_=lg[:, h, :]), tl)
                t = VE.do(lambda e, h=h: e.max_index(out=ix[:, h, :], in_max=m8[:, h, :], in_values=lg[:, h, :]), t)
                t = cp(VE, ixf[:, h, :], ix[:, h, :], t)
                tm = tt(VE, gv[:, h, 0:1], m8[:, h, 1:2], m8[:, h, 0:1], SUB, t)
                te = act(gv[:, h, 1:2], gv[:, h, 0:1], ACT.Exp, tm)
                tm = ts(VE, gv[:, h, 2:3], gv[:, h, 1:2], 1.0, None, ADD, None, te)
                tm = rcp(gv[:, h, 2:3], gv[:, h, 2:3], tm)
                tm = tt(VE, gv[:, h, 3:4], gv[:, h, 1:2], gv[:, h, 2:3], MUL, tm)
                ta = ts(VE, sel[:, h, :], io8, ixf[:, h, 0:1], None, ALU.is_equal, None, t)
                ts_.append(stt(sel[:, h, :], io8, ixf[:, h, 1:2], sel[:, h, :], ALU.is_equal, ADD, ta))
                ta = ts(VE, g2[:, h, :], io8, ixf[:, h, 0:1], gv[:, h, 2:3], ALU.is_equal, MUL, tm)
                tb = ts(VE, lg[:, h, :], io8, ixf[:, h, 1:2], gv[:, h, 3:4], ALU.is_equal, MUL, tm)
                tg = tt(VE, tab[:, :, 2 + h:3 + h].rearrange("p e o -> p (e o)"), g2[:, h, :], lg[:, h, :], ADD, ta, tb)
            return ts_, tg

        def slots_of(ts_, tg):
            b = 1
            w = take(b)
            mm(ps[:, b, 0:8], tri[:, 0:P], sel[:, 0, :], True, True, w, ts_)
            mm(ps[:, b, 8:16], tri[:, 0:P], sel[:, 1, :], True, False)
            mm(ps[:, b, 8:16], ones, sel[:, 0, :], False, True)
            mm(ps[:, b, 16:24], ones, sel[:, 0, :], True, False)
            tk = mm(ps[:, b, 16:24], ones, sel[:, 1, :], False, True, inc=True)

            def field(a, b=None):
                x = tab[:, :, a:b or a + 1]
                return x.rearrange("p e f -> p f e") if b else x.rearrange("p e f -> p (e f)")

            tot = ps[:, b, 16:24]
            io8 = cst[:, C_IO:C_IO + 8]
            t = tt(VE, sel[:, :, :], sel[:, :, :], ps[:, b, 0:16].rearrange("p (h e) -> p h e", h=2), MUL, tk)
            ti = cp(VE, field(5), io8)
            tc = cp(VE, field(4), tot, tk)
            tq = stt(key[:, 0, :], tot, 8.0, cst[:, C_KEY:C_KEY + 8], MUL, ADD)
            mark(b, tq)
            tp = ts(VE, field(0, 2), sel[:, :, :], -1.0, None, ADD, None, t)
            t = tt(VE, cmp_[:, :, :], key[:, 0:1, :].broadcast_to([P, 8, 8]), key[:, 0, :].unsqueeze(2).broadcast_to([P, 8, 8]), ALU.is_gt, tq)
            t = VE.do(lambda e: e.tensor_reduce(key[:, 1, :], cmp_[:, :, :], mybir.AxisListType.X, ADD), t)
            t = tt(VE, cmp_[:, :, :], key[:, 1:2, :].broadcast_to([P, 8, 8]), cst[:, C_RANK:C_RANK + 8].unsqueeze(2).broadcast_to([P, 8, 8]), ALU.is_equal, t)
            t = tt(VE, prod[:, :, :, :], cmp_[:, :, :].unsqueeze(2).broadcast_to([P, 8, 6, 8]), field(0, 6).unsqueeze(1).broadcast_to([P, 8, 6, 8]), MUL, t, ti, tc, tp, tg)
            t = VE.do(lambda e: e.tensor_reduce(stab[:, 0:8, :], prod[:, :, :, :], mybir.AxisListType.X, ADD), t)
            tm = ms(VE, stab[:, 8, :], -1.0)
            return [tm, cp(VE, cnt[:, :, :], stab[0:1, 0:8, 4:6].rearrange("p e f -> p f e"), t)]

        VAR = ((32, [(32, 0, 0)]), (64, [(64, 0, 0)]), (128, [(128, 0, 1)]), (160, [(128, 0, 1), (32, 128, 0)]),
               (192, [(128, 0, 1), (64, 128, 0)]), (256, [(128, 0, 1), (128, 128, 1)]))
        NE, NT, NS, NH = 8, 21, 7, 5
        order = [("1", 0), ("3", 0)]
        for i in range(1, 7):
            order += [("1", i), ("3", i), ("2", i - 1)]
        order.append(("2", 6))
        where = [229344 - 16384 * (NS - i) for i in (0, 1, 2, 6, 5, 4, 3)]
        slots = [sb(f"eslot{i}", [P, 4096], o) for i, o in enumerate(where)]
        lowp = [sb(f"elow{i}", [P, 4096], o, F32R) for i, o in enumerate(where)]
        s_m = [sem(f"m{i}") for i in range(NS)]
        s_rel = sem("rel")
        STEP_D, STEP_R = [48], [NT]
        num = {o: n for n, o in enumerate(order)}
        landed = [(s_m[n % NS], 16 * (n // NS + 1), STEP_D) for n in range(NT)]

        def tile_of(n, e):
            kind, i = order[n]
            c = slice(512 * i, 512 * i + 512)
            src = mw2[e, c, :] if kind == "2" else (mw1 if kind == "1" else mw3)[e, :, c]
            return src.rearrange("o (k p) c -> p (o k) c", p=P)

        def slot(n):
            return slots[n % NS][:, :].rearrange("p (k c) -> p k c", k=4 if order[n][0] == "2" else 8)

        def load_first(n, *w):
            ld.start(s_m[n % NS], slot(n), tile_of(n, slice(0, 1)), *w)

        def load_others(e):
            with e.Fori(1, NE) as i:
                x = e.value_load(cnt[0:1, 1, bass.ds(i, 1)], min_val=0, max_val=7)
                for n in range(NT):
                    e.wait_ge(s_rel, i * NT + (n - NS + 1))
                    e.dma_start(slot(n), tile_of(n, bass.ds(x, 1))).then_inc(s_m[n % NS], 16)

        plev = wk("plev", [P, 2, D], 48 * KI)
        upad = wk("upad", [P, 4, 286], 64 * KI)
        cz = [wk(f"cz{i}", [P, 4, P], 2048 * i) for i in range(2)]
        ct = [wk(f"ct{i}", [P, 4, P], 4 * KI + 2048 * i) for i in range(2)]
        et = wk("et", [P, 2, D], 64 * KI)
        aT = pair("aT", [P, 22, T], 73 * KI)
        yb = wk("yb", [P, 4, T], 68 * KI + 512)
        qT = wk("qT", [P, 4, T], 72 * KI + 512)
        kT = wk("kT", [P, 4, T], 76 * KI + 512)
        vk = wk("vk", [P, 2, 512], 80 * KI + 512)
        Pn = [wk(f"Pn{i}", [P, 2, T], 84 * KI + 512 + 2048 * i) for i in range(4)]
        PTn = [wk(f"PTn{i}", [P, 2, T], 92 * KI + 512 + 2048 * i) for i in range(4)]
        na = [wk(f"na{i}", [P, 2, 2, T], 100 * KI + 512 + 4096 * i) for i in range(2)]
        ctap = [wk(f"ctap{i}", [P, T], 108 * KI + 512 + 1024 * i) for i in range(2)]
        mix = pair("mix", [P, 8, T], WTOP - 16 * KI)
        prod = wk("prod", [P, 8, 6, 8], 56 * KI)

        def unit_at(name, off):
            return pair(name, [P, D], off)

        t_pl = []

        def ple(j, t_pp, *w):
            us = [U.get()]
            for h in range(2):
                b = h if j == 0 else 1 - h
                tk = rows(us, pp, b, h, 0, True, True, t_pp, give=h == 1)
                t_pl.append(act(plev[:, h, 512 * j:512 * j + 512], ps[:, b, :], ACT.Copy, tk, *w, scale=0.5))
                mark(b, t_pl[-1])
                yield 1

        Pt = wk("Pt", [P, 2, T], 72 * KI)
        Pgt = wk("Pgt", [P, 2, 2, P], 74 * KI)
        cur = rt("cur", [P, 2, 6])
        s_pt, s_ysb = sem("pt"), sem("ysb")
        EACH = [1]

        def places(i, *w):
            t = VE.do(lambda e: e.tensor_copy(cur[:, 1, :], stab[:, i(), :].rearrange("p o f -> p (o f)")), *w)
            for h in range(2):
                VE.do(lambda e, h=h: e.tensor_scalar(Pt[:, h, :], cst[:, C_IO:C_IO + T], cur[:, 1, h:h + 1], None, ALU.is_equal), t,
                      inc=True if h == 0 else s_pt)

        def place_first():
            t_route.extend(slots_of(*routed[0]))
            places(lambda: slice(0, 1), t_route)

        i_np, r_np, t_np = bc(norm_post)
        i_ig, r_ig, t_ig = bc(ln_in_g)
        i_ib, r_ib, t_ib = bc(ln_in_b)
        U.lend([unit_at(f"lw{i}", 84480 + 8192 * i) for i in range(2)], UB[0], t_b1)
        t_h = [None, None]

        def after_out(h, tk):
            ss, mq, rs = small[:, 20 + 2 * h:22 + 2 * h], small[:, 24 + h:25 + h], small[:, 26 + h:27 + h]
            ta = []
            for j, c in enumerate(HC):
                b = 2 + 2 * h + j
                te = act(acc[:, h, c], ps[:, b, :], ACT.Square, tk[j], t_b1, acc=ss[:, j:j + 1])
                ta.append(tt(VE, acc[:, h, c], ps[:, b, :], r_np[:, c], MUL, te, t_np))
                mark(b, ta[j])
            t = tt(VE, mq, ss[:, 0:1], ss[:, 1:2], ADD)
            t = ts(VE, mq, mq, 1.0 / D, 4 * EPS, MUL, ADD, t)
            t = rsqrt(rs, mq, t)
            t_h[h] = ln(res[:, h, :], h, lambda j, c: stt(res[:, h, c], acc[:, h, c], rs, res[:, h, c], MUL, ADD, t, ta[j]),
                        r_ig, r_ib, t_ig, t_ib)

        t_hT, t_route = [None, None], []

        def hH(h):
            return (lambda k: t_hT[h][k // 4][0]), (lambda k: t_hT[h][k // 4][1])

        def turn_first(*w):
            t_hT[0] = turn_h(0, t_h[0], *w)

        tk_o = product((mH, mL), lambda h: (lambda k: t_mg[k],), after_out, True, lambda: turn_first(t_b1))

        def second_half():
            after_out(1, tk_o)
            rfree[i_np] = rfree[i_ig] = rfree[i_ib] = t_h[1]


        t_w2 = None
        t_old = t_b1
        for l in range(2):
            vo = V_L + VL_N * l
            if l == 0:
                i_bv, r_bv, t_bv = bc(b_in2[0:1, 2048:2560], 512)
                i_bo, r_bo, t_bo = bc(b_out2[0:1, :])
            t_lay = [PE.last(), VE.last(), AC.last()]
            t_v = []
            t_pl.clear()
            for h in range(2):
                if h:
                    t_hT[1] = turn_h(1, t_h[1], t_old)
                if h == 0:
                    second_half()
                if h == 0:
                    run(ple(0, t_pp, t_old))
                    us = [U.get() for _ in range(4)]
                tk = rows(us, hT, 2 + h, h, 0, True, True, *hH(h), give=h == 1)
                t_v.append(tt(VE, vk[:, h, :], ps[:, 2 + h, :], r_bv, ADD, tk, t_bv, t_lay))
                mark(2 + h, t_v[h])
            rfree[i_bv] = t_v[1]
            bgh, bq8 = small[:, 192 + 8 * l:196 + 8 * l], small[:, 196 + 8 * l:200 + 8 * l]
            bah = small[:, 208 + 4 * l:212 + 4 * l]
            ts(VE, bah, v(vo + VL_BIN, 4), 0.5, None, MUL, None)
            t_bg = ts(VE, bgh, v(vo + VL_BIN + 4, 4), 0.5, None, MUL, None)
            t_bq = ts(VE, bq8, v(vo + VL_BIN + 8, 4), 0.125, None, MUL, None)
            hh = xh(hT)
            lows[:] = [GP]
            tz = [ms(GP, upad[:, :, 0:15], 0.0, t_lay), ms(GP, upad[:, :, 271:286], 0.0)]
            t_uu = []
            trel = [None] * 4
            t_y = [None] * 4
            t_q, t_k = [None] * 4, [None] * 4
            t_mix = [None] * 8
            t_na = [None] * 4
            na_rd = [t_lay, t_lay]

            def load_na(i):
                t_na[i] = ld.once(na[i % 2][:, :, :, :], na_bias[l][:, :, 2 * i:2 * i + 2, :], na_rd[i % 2])

            load_na(0)
            load_na(1)

            def ag():
                for i in range(2):
                    ua, ug = ([U.get() for _ in range(2)] for _ in range(2))
                    for n, j in enumerate((2 * i, 2 * i + 1)):
                        b, pb, tk = block(*hh, T, t_hT, unit=ua[n])
                        ta = act(yb[:, j, :], pb, ACT.Identity, tk, t_lay, t_bg, bias=bah[:, j:j + 1], scale=0.5)
                        mark(b, ta)
                        yield 2.6
                        b, pb, tk = block(*hh, T, t_hT, unit=ug[n])
                        g_ = act(tmp[j % 4][:, :], pb, ACT.Tanh, tk, t_bg, trel[j % 4], bias=bgh[:, j:j + 1], scale=0.5)
                        mark(b, g_)
                        trel[j % 4] = stt(upad[:, j, 15:271], tmp[j % 4][:, :], 1.0, yb[:, j, :], ADD, MUL, ta, g_, tz)
                        t_uu.append(trel[j % 4])
                        yield 2.4

            CD, CG, CT = 24, 3, 4
            assert CD + CG + CT == 31
            t_tp, t_dg = [None] * 4, [None] * 3
            conv_done = []
            i_dg = [(rows_[0] + i) % 5 for i in range((CT + 1) // 2)]

            def diag(j, x):
                n = 4 * x + j
                return R[i_dg[n // 8]][:, P * (n % 8):P * (n % 8) + P]

            for x in range(CT):
                for j in range(4):
                    n = 4 * x + j
                    t_dg[n // 8] = act(diag(j, x), ident, ACT.Copy, rfree[i_dg[n // 8]], scale=v(vo + VL_CW + 31 * j + CD + CG + x))

            def conv():
                for i in range(2):
                    blocks = (2 * i, 2 * i + 1)
                    todo = [(d, j) for d in range(CD, CD + CG) for j in blocks]
                    for n in range(CD):
                        if n % 3 == 0 and todo:
                            d, j = todo.pop(0)
                            w, src = v(vo + VL_CW + 31 * j + d), upad[:, j, d:d + T]
                            if d == CD:
                                t_tp[j] = ts(GP, tmp[j][:, :], src, w, None, MUL, None, t_uu[j])
                            else:
                                t = ts(GP, ctap[j % 2][:, :], src, w, None, MUL, None, t_tp[j], t_lay)
                                t_tp[j] = tt(GP, tmp[j][:, :], tmp[j][:, :], ctap[j % 2][:, :], ADD, t)
                        for j in blocks:
                            w, src, o = v(vo + VL_CW + 31 * j + n), upad[:, j, n:n + T], yb[:, j, :]
                            t_y[j] = stt(o, src, w, o, MUL, ADD, t_y[j]) if n else ts(VE, o, src, w, v(vo + VL_CB + j), MUL, ADD, t_uu[j])
                        yield 16 / CD
                    conv_done.append(i)
                    yield 1

            def qk(i, n):
                dst, tl, bias, sc = ((qT, t_q, bq8, 0.125), (kT, t_k, v(vo + VL_BIN + 12, 4), 1.0))[n]
                for j in (2 * i, 2 * i + 1):
                    b, pb, tk = block(*hh, T, t_hT)
                    tl[j] = act(dst[:, j, :], pb, ACT.Identity, tk, t_bq, t_lay, bias=bias[:, j:j + 1], scale=sc)
                    mark(b, tl[j])
                    yield 2.6

            pn, ptt, trd, od = [None] * 8, [None] * 8, [None] * 8, [None] * 4

            def score(st):
                for h in (2 * st, 2 * st + 1):
                    b, r = 2 + h % 2, 64 * (h % 2)
                    w = take(b)
                    for t in range(2):
                        tk = mm(ps[:, b, T * t:T * t + T], qT[r:r + 64, st, P * t:P * t + P], kT[r:r + 64, st, :], True, True, w, t_q[st], t_k[st], inc=t == 1)
                    p = Pn[h % 4]
                    c = 2 * h
                    es = []
                    for t in range(2):
                        tm_ = neg_max(p[:, t, :], ps[:, b, T * t:T * t + T], na[st % 2][:, t, h % 2, :], nmx[:, c + t:c + t + 1], tk, t_na[st], trd[h - 4] if h > 3 else None, t_lay)
                        es.append(act(p[:, t, :], p[:, t, :], ACT.Exp, tm_, bias=nmx[:, c + t:c + t + 1], scale=-1.0, acc=rsm[:, c + t:c + t + 1]))
                    mark(b, tm_)
                    na_rd[st % 2] = tm_
                    rr = rcp(riv[:, c:c + 2], rsm[:, c:c + 2], es)
                    for t in range(2):
                        pn[h] = act(p[:, t, :], p[:, t, :], ACT.Copy, rr, scale=riv[:, c + t:c + t + 1])
                if st < 2:
                    load_na(st + 2)
                yield 0.2

            def turn_p(st):
                for h in (2 * st, 2 * st + 1):
                    b = 4 + h % 2
                    w = take(b)
                    for kb in range(2):
                        for t in range(2):
                            trd[h] = tr(ps[:, b, T * kb + P * t:T * kb + P * t + P], Pn[h % 4][:, t, P * kb:P * kb + P], w, pn[h], inc=kb + t == 2)
                    ptt[h] = cp((AC, VE)[h % 2], PTn[h % 4][:, :, :].rearrange("p k t -> p (k t)"), ps[:, b, :], trd[h], od[h // 2 - 2] if h > 3 else None, t_lay)
                    mark(b, ptt[h])
                yield 0.7

            def values(i):
                w = take(7)
                for kb in range(2):
                    for h in (2 * i, 2 * i + 1):
                        r = 64 * (h % 2)
                        tk = mm(ps[r:r + 64, 7, 0:T], vk[:, kb, 64 * h:64 * h + 64], PTn[h % 4][:, kb, :], kb == 0, kb == 1, w, ptt[h], t_v, inc=kb == 1)
                od[i] = tk
                te = act(mix[0][:, 4 + i, :], ps[:, 7, 0:T], ACT.Copy, tk, t_lay, scale=2.0)
                t_mix[4 + i] = stt(mix[1][:, 4 + i, :], ps[:, 7, 0:T], 2.0, f32(mix[0][:, 4 + i, :]), MUL, SUB, te)
                mark(7, t_mix[4 + i])
                yield 0.4

            def conv_ln():
                tx = [None, None]
                assert conv_done == [0, 1]
                for h in range(2):
                    b = (6, 0)[h]
                    w = take(b)
                    hs = slice(P * h, P * h + P)
                    o = [ps[:, b, P * j:P * j + P] for j in range(4)]
                    for x in range(CT):
                        for j in range(4):
                            tk = mm(o[j], upad[:, j, CD + CG + x + P * h:CD + CG + x + P * h + P], diag(j, x), x + j == 0, False, w, t_uu, t_dg, inc=True)
                    for i in i_dg:
                        rfree[i] = tk
                    for j in range(4):
                        if CG:
                            mm(o[j], tmp[j][:, hs], ident, not CT and j == 0, False, w, t_tp[j])
                    for j in range(4):
                        tk = mm(o[j], yb[:, j, hs], ident, False, j == 3, t_y[j], inc=j == 3)
                    t = ln_stats(lambda i: ps[:, b, :], h, 1, tk)
                    tx[h] = ts(VE, f2(cz[h]), ps[:, b, :], lmv[:, h, 0:1], lmv[:, h, 3:4], SUB, MUL, t, t_k)
                    mark(b, tx[h])
                    yield 0.1
                for h in range(2):
                    z, zt = cz[h], ct[h]
                    b = (1, 6)[h]
                    w = take(b)
                    for j in range(4):
                        tk = tr(ps[:, b, P * j:P * j + P], z[:, j, :], w, tx[h], inc=j == 3)
                    for j in range(4):
                        te = act(z[:, j, :], ps[:, b, P * j:P * j + P], ACT.Identity, tk, scale=v(vo + VL_CG + j), bias=v(vo + VL_CBT + j))
                    mark(b, te)
                    t = act(f2(zt), f2(z), ACT.Tanh, te, scale=0.5)
                    t = stt(f2(z), f2(zt), 1.0, f2(z), ADD, MUL, t)
                    oH, oL = (x[:, 0:4, P * h:P * h + P] for x in mix)
                    te = act(oH, z[:, :, :], ACT.Copy, t, t_lay)
                    t_mix[h] = tt(VE, oL, z[:, :, :], f32(oH), SUB, te)
                    yield 0.1

            def blocks():
                yield from ag()
                for i in range(2):
                    yield from qk(i, 0)
                    yield from qk(i, 1)

            order_ = "BBBBBBBBBBBSBBSBTBBVTSCVPSCTCVTCPV"
            gens = {"B": blocks(), "C": conv_ln(), "P": ple(1, t_pp, t_old)}
            for c, f in (("S", score), ("T", turn_p), ("V", values)):
                gens[c] = iter([g for i in range(4) for g in [f(i)]])

            def steps():
                for c in order_:
                    g = gens[c]
                    yield next(g) if c in "BCP" else next(next(g))

            m = steps()
            for _ in range(4):
                next(m)
            weave(m, conv(), 1.0)
            t_ac = []
            for h in range(2):
                t_ac.append(stt(acc[:, h, :], res[:, h, :], ALPHA, r_bo, MUL, ADD, t_h[h], t_bo))
            rfree[i_bo] = t_ac[1]
            t_nat = [PE.last(), VE.last(), AC.last()]
            if l == 0:
                t_pT = ple_load(1, t_pl)
            i_g, r_g, t_rg = bc(ln1_g[l:l + 1, :])
            i_b, r_b, t_rb = bc(ln1_b[l:l + 1, :])
            i_gb, r_gb, t_gbr = bc(gate_b[l:l + 1, :])
            if l == 1:
                load_first(0, t_nat)
            lows[:] = [VE, GP]
            if l == 0:
                U.lend([unit_at(f"ln{i}", 72 * KI + 512 + 8192 * i) for i in range(4)], UB[1], t_nat)

            t_qk = PE.last()

            def after_mix(h, tk):
                def pre(j, c):
                    b = 2 + 2 * h + j
                    t = stt(res[:, h, c], ps[:, b, :], 0.5, acc[:, h, c], MUL, ADD, tk[j], t_ac)
                    mark(b, t)
                    return t
                t_h[h] = ln(res[:, h, :], h, pre, r_g, r_b, t_rg, t_rb)

            tk_m = product(mix, lambda h: (lambda k: t_mix[0:2] if k < 4 else t_mix[k],), after_mix, l == 0,
                           (lambda: turn_first(t_qk, t_mix)) if l == 0 else None)
            t_mixd = PE.last()
            if l == 1:
                load_first(1, t_nat)
                load_first(2, t_mixd)
            t_e, routed = [], []

            def before_gate(h):
                if h == 0 and l == 1:
                    turn_first(t_qk, t_mix)
                if h == 1:
                    t_hT[1] = turn_h(1, t_h[1], t_qk)
                if h == 0:
                    after_mix(1, tk_m)
                if l == 1 and h == 1:
                    routed.append(route(t_hT))
                return hH(h)

            def after_gate(h, tk):
                t_e.append([])
                for j, c in enumerate(HC):
                    b = 2 + 2 * h + j
                    t = tt(VE, et[:, h, c], ps[:, b, :], r_gb[:, c], ADD, tk[j], t_gbr, t_mix[1])
                    mark(b, t)
                    if l == 1 and h == 1 and j == 1:
                        VE.do(lambda e: e.memset(cur[:, 0, :], 0.0), inc=s_ysb)
                    t = act(et[:, h, c], et[:, h, c], ACT.Tanh, t, scale=0.5)
                    t = stt(et[:, h, c], et[:, h, c], 1.0, plev[:, h, c], ADD, MUL, t, t_pl)
                    t_e[h].append(stt(acc[:, h, c], res[:, h, c], ALPHA, et[:, h, c], MUL, ADD, t, t_h[h], t_ac))

            tk_g = product(hT, before_gate, after_gate, l == 0, place_first if l == 1 else None)
            after_gate(1, tk_g)
            if l == 1:
                break
            rfree[i_g] = rfree[i_b] = t_h[1]
            rfree[i_gb] = t_e[1]
            i_g, r_g, t_rg = bc(ln2_g[0:1, :])
            i_b, r_b, t_rb = bc(ln2_b[0:1, :])
            t_l2 = [t_rg, t_rb]
            i_bv, r_bv, t_bv = bc(b_in2[1:2, 2048:2560], 512)
            i_bo, r_bo, t_bo = bc(b_out2[1:2, :])
            t_wr = ld.once(wr[:, :, :], w_router.rearrange("(k p) c -> p k c", p=P), t_b1)
            t_pp = ple_parts(t_pT, t_pl)
            t_a = [None] * 22
            trel = [None] * 4
            t_w2 = [PE.last(), VE.last(), AC.last()]
            for i in range(11):
                s_ = []
                for j in (2 * i, 2 * i + 1):
                    b, pb, tk = block(*hh, T, t_hT, b=j % 2)
                    t = act(tmp[j % 4][:, :], pb, ACT.Silu, tk, trel[j % 4])
                    mark(b, t)
                    s_.append(t)
                for j in (2 * i, 2 * i + 1):
                    b, pb, tk = block(*hh, T, t_hT, b=2 + j % 2)
                    z = tmp[j % 4]
                    t = tt(VE, z[:, :], z[:, :], pb, MUL, tk, s_)
                    mark(b, t)
                    te = act(aT[0][:, j, :], z[:, :], ACT.Copy, t, t_w2)
                    t_a[j] = trel[j % 4] = tt(VE, aT[1][:, j, :], z[:, :], f32(aT[0][:, j, :]), SUB, te, t_w2)
            t_old = [PE.last(), VE.last(), AC.last()]
            U.lend([unit_at("lf0", 64 * KI), unit_at("lf1", 117 * KI)], UB[2], t_w2)
            for n in range(11):
                us = [U.get()]
                t_f0 = [rows(us, aT, 2 + 2 * h, h, 2 * n, n == 0, n == 10, t_a[2 * n:2 * n + 2], give=h == 1) for h in range(2)]
            for n in range(6):
                us = [U.get()]
                for h in range(2):
                    rows(us, aT, 3 + 2 * h, h, 2 * n, n == 0, False, t_a, give=h == 1)
            us = [U.get() for _ in range(5)]

            def after_ffn(h, tk):
                def pre(j, c):
                    b = 2 + 2 * h + j
                    t = tt(VE, res[:, h, c], ps[:, b, :], acc[:, h, c], ADD, tk[j], t_e[h])
                    mark(b, t)
                    return t
                t_h[h] = ln(res[:, h, :], h, pre, r_g, r_b, t_l2)

            after_ffn(0, [t_f0[0], rows(us, aT, 3, 0, 12, False, True, t_a)])
            tk_f = late(us, 1, aT, 5, 1, 12, False, lambda: turn_first(t_old), t_a)

            def second_half():
                after_ffn(1, [t_f0[1], tk_f])
                rfree[i_g] = rfree[i_b] = t_h[1]

        raw_, part_ = U.left(parts)
        for n, w in enumerate((raw_[0:2], [raw_[2], part_[0]], part_[1:3], part_[3:5])):
            load_first(3 + n, w)
        for n in range(NS, NT):
            load_first(n, (s_rel, n - NS + 1))
        SP.wait(t_route)
        SP.q.append(load_others)

        xTf = wk("xTf", [P, KB, T], 0)
        xTH = wk("xTH", [P, KB, T], 0, F32R)
        xTL = wk("xTL", [P, KB, T], 8 * KI, F32R)
        ysb = wk("ysb", [P, 2, D], 16 * KI)
        s1 = [wk(f"s1_{i}", [P, 512], 16 * KI + 2048 * i) for i in range(2)]
        ab = [wk(f"ab{i}", [P, 512], 20 * KI + 2048 * i) for i in range(2)]
        Hb = [wk(f"Hb{i}", [P, 1024], k * KI, F32R) for i, k in enumerate((24, 28, 34, 48, 52))]
        Pg = wk("Pg", [P, 2, T], 38 * KI)
        aTf = [wk(f"aTf{i}", [P, 4, T], (56 + 4 * i) * KI) for i in range(2)]
        aTH = [wk(f"aTH{i}", [P, 4, T], (56 + 4 * i) * KI, F32R) for i in range(2)]
        aTL = [wk(f"aTL{i}", [P, 4, T], (64 + 4 * i) * KI, F32R) for i in range(2)]
        PE.wait(t_route, t_h)
        VE.wait(t_route, t_e)
        AC.wait(t_route, t_e, t_h)
        for E in (PE, VE, AC):
            E.loop()
        for limit, blocks in VAR:
            for E in (PE, VE, AC):
                E.variant()
            BF = [[VE.start(), AC.start()] for _ in range(4)] + [[(s_ysb, 1, EACH), AC.start()] for _ in range(4)]
            ns = 128 if limit <= 128 else 256
            nbk = len(blocks)
            split = [k for k in range(nbk) if blocks[k][2]]
            whole = [k for k in range(nbk) if not blocks[k][2]]

            t_H, t_L, t_use, t_raw = [], [], [], {}

            def highs():
                while split and len(t_H) < min(4 * NT, len(t_use) + NH - 1):
                    m = len(t_H)
                    raw = slots[m // 4 % NS][:, 1024 * (m % 4):1024 * (m % 4) + 1024]
                    t_H.append(act(Hb[m % NH][:, :], raw, ACT.Copy, landed[m // 4], t_use[m - NH] if m >= NH else PE.start()))
                    if not whole:
                        low(m)

            def low(m):
                sl = slice(1024 * (m % 4), 1024 * (m % 4) + 1024)
                j = m // 4 % NS
                t_L.append(tt(VE, lowp[j][:, sl], slots[j][:, sl], f32(Hb[m % NH][:, :]), SUB, t_H[m], t_raw.get(m)))

            act(small[:, 30:31], small[:, 0:1], ACT.Silu)
            highs()
            t_x = []
            for k in range(KB):
                b = 4 + k // 2
                w = take(b) if k % 2 == 0 else None
                for h in range(2):
                    tk = mm(ps[:, b, T * (k % 2):T * (k % 2) + ns], res[:, h, P * k:P * k + P], Pt[:, h, 0:ns], h == 0, h == 1, w, (s_pt, 1, EACH), inc=h == 1)
                if k % 2:
                    src = ps[:, b, :].rearrange("p (k t) -> p k t", k=2)
                    t = tk
                    for B, off, r in blocks:
                        o = (slice(None), slice(k - 1, k + 1), slice(off, off + B))
                        if r:
                            te = act(xTH[o], src[o[0], :, o[2]], ACT.Copy, t)
                            t = tt(VE, xTL[o], src[o[0], :, o[2]], f32(xTH[o]), SUB, te)
                        else:
                            t = cp(VE if split or k % 4 == 3 else AC, xTf[o], src[o[0], :, o[2]], t)
                    mark(b, t)
                    t_x.append(t)
            t_gath = tk
            t_P = []

            def scatter_prep():
                t_c = VE.do(lambda e: e.tensor_copy(cur[:, 0, :], stab[:, bass.ds(VE.i, 1), :].rearrange("p o f -> p (o f)")))
                for k, (B, off, r) in enumerate(blocks):
                    nq = P // B
                    for h in range(2):
                        t = ts(VE, Pgt[:, k, h, :].rearrange("p (q b) -> p q b", q=nq),
                               cst[:, C_IO + off:C_IO + off + B].unsqueeze(1).broadcast_to([P, nq, B]),
                               cur[:, 0, h:h + 1], cur[:, 0, 2 + h:3 + h], ALU.is_equal, MUL, t_c)
                places(lambda: bass.ds(VE.i + 1, 1), t_gath)
                w = take(3)
                for k in range(nbk):
                    for h in range(2):
                        tk = tr(ps[:, 3, T * k + P * h:T * k + P * h + P], Pgt[:, k, h, :], w, t, inc=h == 1)
                t_P.append(cp(VE, Pg[:, 0:nbk, :], ps[:, 3, 0:T * nbk].rearrange("p (k t) -> p k t", k=nbk), tk))
                mark(3, t_P[0])

            hb = [0]

            def view(n, k):
                return slots[n % NS][:, :].rearrange("p (k c) -> p k c", k=k)

            def up(kind, i):
                n = num[kind, i]
                wt = view(n, 8)
                out_ = []
                for k in whole:
                    B, off, _ = blocks[k]
                    nq = P // B
                    N = 512 // nq
                    b = hb[0] % 3
                    hb[0] += 1
                    w = take(b)
                    for kk in range(8):
                        for q in range(nq):
                            end = q == nq - 1 and (kk % 2 == 1 if split else kk == 7)
                            inc = s_rel if end and not split else end
                            t = mm(ps[B * q:B * q + B, b, 0:N], xTf[:, kk, off:off + B], wt[:, kk, N * q:N * q + N], kk == 0, kk == 7, w, landed[n], t_x[kk // 2], inc=inc)
                        if split and kk % 2:
                            t_raw[4 * n + kk // 2] = t
                    out_.append((k, b, N, t if split else (s_rel, n + 1, STEP_R)))
                if split and whole:
                    for m in range(4 * n, 4 * n + 4):
                        low(m)
                if split:
                    bs = []
                    for k in split:
                        bs.append((hb[0] % 3, take(hb[0] % 3)))
                        hb[0] += 1
                    for j in range(4):
                        m = 4 * n + j
                        H = Hb[m % NH][:, :].rearrange("p (k c) -> p k c", k=2)
                        L = lowp[n % NS][:, 1024 * j:1024 * j + 1024].rearrange("p (k c) -> p k c", k=2)
                        for k, (b, w) in zip(split, bs):
                            xs_ = slice(blocks[k][1], blocks[k][1] + P)
                            for q in range(2):
                                kk = 2 * j + q
                                mm(ps[:, b, :], xTH[:, kk, xs_], H[:, q, :], kk == 0, False, w, t_H[m], t_x[j])
                                mm(ps[:, b, :], xTL[:, kk, xs_], H[:, q, :], False, False)
                                end = q == 1
                                t = mm(ps[:, b, :], xTH[:, kk, xs_], L[:, q, :], False, kk == 7, t_L[m], inc=end and (s_rel if j == 3 and k == split[-1] else True))
                                if end and j == 3 and k == split[-1]:
                                    t = (s_rel, n + 1, STEP_R)
                        t_use.append(t)
                        highs()
                        if j == 3:
                            for k, (b, w) in zip(split, bs):
                                out_.append((k, b, 512, t))
                return out_

            t_s, t_ab, t_at = [None] * 2, [None] * 2, [[None] * 2, [None] * 2]
            t_tr = [PE.start(), PE.start()]
            t_y = [[None, None], [None, None]]

            def tile1(i):
                for k, b, N, t in up("1", i):
                    t_s[k] = act(s1[k][:, 0:N], ps[:, b, 0:N], ACT.Silu, t, t_ab[k] or PE.start())
                    mark(b, t_s[k])

            def tile3(i):
                for k, b, N, t in up("3", i):
                    t_ab[k] = tt(VE, ab[k][:, 0:N], s1[k][:, 0:N], ps[:, b, 0:N], MUL, t, t_s[k], t_tr[k])
                    mark(b, t_ab[k])

            def turn(i):
                free = (s_rel, num["2", i - 2] + 1, STEP_R) if i > 1 else PE.start()
                for k, (B, off, r) in enumerate(blocks):
                    nq = P // B
                    nn = 4 // nq
                    b = 3
                    if k == 1:
                        b = hb[0] % 3
                        hb[0] += 1
                    w = take(b)
                    for n in range(nn):
                        t_tr[k] = tr(ps[:, b, P * n:P * n + P], ab[k][:, P * n:P * n + P], w, t_ab[k], inc=n == nn - 1)
                    if r:
                        s_ = ps[:, b, :].rearrange("p (n b) -> p n b", n=4)
                        oH, oL = aTH[i % 2][:, :, off:off + P], aTL[i % 2][:, :, off:off + P]
                        te = act(oH, s_, ACT.Copy, t_tr[k], free)
                        t_at[i % 2][k] = tt(VE, oL, s_, f32(oH), SUB, te, free)
                    else:
                        o = aTf[i % 2][:, :, off:off + B].rearrange("p (q n) b -> p n q b", q=nq)
                        s_ = ps[:, b, 0:P * nn].rearrange("p (n q b) -> p n q b", n=nn, q=nq)
                        t_at[i % 2][k] = cp(VE, o, s_, t_tr[k], free)
                    mark(b, t_at[i % 2][k])

            def tile2(i):
                n = num["2", i]
                wt = view(n, 4)
                steps = [(kk, j) for kk in range(4) for j in range(2)] if i < 6 else [(kk, j) for j in range(2) for kk in range(4)]
                for k in whole:
                    B, off, _ = blocks[k]
                    nq = P // B
                    w = [take(4 + 2 * k), take(5 + 2 * k)] if i == 0 else None
                    for kk, j in steps:
                        q = kk % nq
                        end = kk == 3 and j == 1
                        t = mm(ps[B * q:B * q + B, 4 + 2 * k + j, :], aTf[i % 2][:, kk, off:off + B], wt[:, kk, 512 * j:512 * j + 512],
                               i == 0 and kk < nq, i == 6 and kk >= 4 - nq, w, landed[n], t_at[i % 2][k],
                               inc=s_rel if end and not split else j == 1 or kk == 3)
                        if end and not split:
                            t = (s_rel, n + 1, STEP_R)
                        if j == 1:
                            t_raw[4 * n + kk] = t
                        t_y[k][j] = t
                if split and whole:
                    for m in range(4 * n, 4 * n + 4):
                        low(m)
                if split:
                    for kk, j in steps:
                        m = 4 * n + kk
                        H = Hb[m % NH]
                        L = lowp[n % NS][:, 1024 * kk:1024 * kk + 1024]
                        js = slice(512 * j, 512 * j + 512)
                        for k in split:
                            w = [take(4 + 2 * k), take(5 + 2 * k)] if i == 0 and kk == 0 else None
                            xs_ = slice(blocks[k][1], blocks[k][1] + P)
                            aH, aL = aTH[i % 2][:, kk, xs_], aTL[i % 2][:, kk, xs_]
                            first, last = i == 0 and kk == 0, i == 6 and kk == 3
                            o = ps[:, 4 + 2 * k + j, :]
                            mm(o, aH, H[:, js], first, False, w, t_H[m], t_at[i % 2][k])
                            mm(o, aL, H[:, js], False, False)
                            rel = j == 1 and kk == 3 and k == split[-1]
                            t = mm(o, aH, L[:, js], False, last, t_L[m], inc=s_rel if rel else j == 1 or kk == 3)
                            if rel:
                                t = (s_rel, n + 1, STEP_R)
                            t_y[k][j] = t
                        if j == 1:
                            t_use.append(t)
                            highs()

            tile1(0)
            tile3(0)
            scatter_prep()
            for i in range(1, 7):
                tile1(i)
                turn(i - 1)
                tile3(i)
                tile2(i - 1)
            turn(6)
            tile2(6)
            t_yy = [[], (s_ysb, 2, EACH)]
            for k in range(nbk):
                t_yy[0].append(act(ysb[:, k, 0:512], ps[:, 4 + 2 * k, :], ACT.Copy, t_y[k][0], t_tr))
            for k in range(nbk):
                VE.do(lambda e, k=k: e.tensor_copy(ysb[:, k, 512:1024], ps[:, 5 + 2 * k, :]), t_y[k][1], t_tr, inc=s_ysb if k == nbk - 1 else True)
            for j in range(2):
                for h in range(2):
                    b = 2 * h + j
                    w = take(b)
                    for k in range(nbk):
                        tk = mm(ps[:, b, :], Pg[:, k, P * h:P * h + P], ysb[:, k, 512 * j:512 * j + 512], k == 0, k == nbk - 1, w, t_P, t_yy[j], inc=k == nbk - 1)
                    tt(VE, acc[:, h, HC[j]], acc[:, h, HC[j]], ps[:, b, :], ADD, tk)
            for E in (PE, VE, AC):
                E.end_variant()
        for E in (PE, VE, AC):
            E.end_loop(NE)

        orow = wk("orow", [P, 2, D], 16 * KI)
        r_g, r_b = slots[0][:, 0:D], slots[0][:, D:2 * D]
        done = (s_rel, (NE - 1) * NT + (NT - 1) // NS * NS + 1)
        t_l2 = [ld.once(r_g, ln2_g[1:2, :].broadcast_to([P, D]), done), ld.once(r_b, ln2_b[1:2, :].broadcast_to([P, D]), done)]
        t_out, t_st, t_rs = [], [], []
        for h in range(2):
            for j, c in enumerate(HC):
                t = VE.do(lambda e, h=h, j=j, c=c: e.bn_stats(lst[:, h, 6 * j:6 * j + 6], acc[:, h, c]), VE.last() if h + j == 0 else None)
            t_st.append(t)
        for h in range(2):
            t = VE.do(lambda e, h=h: e.bn_aggr(lmv[:, h, 0:2], lst[:, h, :]), t_st[h])
            t = ts(VE, lmv[:, h, 2:3], lmv[:, h, 1:2], LN_EPS, None, ADD, None, t)
            t_rs.append(rsqrt(lmv[:, h, 3:4], lmv[:, h, 2:3], t))
        t = stt(lmv[:, 1, 2:3], lmv[:, 1, 0:1], -1.0, lmv[:, 1, 3:4], MUL, MUL, t_rs)
        o, c = orow[:, 1, HC[1]], HC[1]
        t = act(o, acc[:, 1, c], ACT.Identity, t, scale=lmv[:, 1, 3:4], bias=lmv[:, 1, 2:3])
        t = tt(GP, o, o, r_g[:, c], MUL, t, t_l2)
        t_gp = tt(GP, o, o, r_b[:, c], ADD, t)
        for h, c in ((0, HC[0]), (0, HC[1]), (1, HC[0])):
            o = orow[:, h, c]
            t = stt(o, acc[:, h, c], lmv[:, h, 0:1], r_g[:, c], SUB, MUL, t_rs, t_l2)
            t = stt(o, o, lmv[:, h, 3:4], r_b[:, c], MUL, ADD, t)
            if (h, c) != (0, HC[0]):
                c = slice(0, c.stop)
                t_out.append(ld.once(out[0, P * h:P * h + P, c], orow[:, h, c], t))
        t_out.append(ld.once(out[0, P:T, HC[1]], orow[:, 1, HC[1]], t_gp))
        SP.wait(t_out)

        block_ = ctx.enter_context(nc.Block())
        block_.sync(lambda e: SP.emit(e))
        def count(i):
            return cnt[0:1, 0, bass.ds(i, 1)]

        limits = [lim for lim, _ in VAR]
        block_.tensor(lambda e: PE.emit(e, NE, count, limits))
        block_.vector(lambda e: VE.emit(e, NE, count, limits))
        block_.scalar(lambda e: AC.emit(e, NE, count, limits))
        block_.gpsimd(lambda e: GP.emit(e))


def fcols(a):
    return a.reshape(-1, P).T


def layout(inputs):
    import numpy as np

    g = {k: np.asarray(a) for k, a in inputs.items()}
    i = np.arange(P)
    c = np.zeros((P, NCONST), np.float32)
    c[:, C_ID:C_ID + 128] = i[:, None] == i
    c[:, C_U:C_U + 128] = i[:, None] > i
    c[:, C_T:C_T + TT] = i[:, None] <= np.arange(TT)
    c[:, C_ONE:C_ONE + 128] = 1.0
    c[:, C_MASK:C_MASK + TT] = np.where(np.arange(TT) - 144 <= i[:, None], 0.0, -1e30)
    c[:, C_IO:C_IO + T] = np.arange(T)
    c[:, C_KEY:C_KEY + 8] = -np.arange(8)
    c[:, C_KEY] = 8192
    c[:, C_RANK:C_RANK + 8] = RANKS
    v = np.zeros((P, NVEC), np.float32)
    v[:, V_PRE:V_PRE + 8] = fcols(g["norm_pre"][0])
    v[:, V_CW:V_CW + 96] = g["conv_w"][0].reshape(4, 24, P).transpose(2, 1, 0).reshape(P, 96)
    v[:, V_CB:V_CB + 24] = fcols(g["conv_b"][0])
    v[:, V_DSK:V_DSK + 16] = fcols(np.repeat(g["d_skip"][0], 64))
    v[:, V_SSDN:V_SSDN + 16] = fcols(g["ssd_norm"][0])
    v[:, V_GB:V_GB + 16] = fcols(g["gate_bias"][0])
    v[:, V_ING:V_ING + 8] = fcols(g["ln_in_g_2"])
    v[:, V_INB:V_INB + 8] = fcols(g["ln_in_b_2"])
    v[0:32, V_DTFB] = g["dt_bias"][0]
    v[32:48, V_DTFB] = g["fgate_bias"][0]
    v[0:32, V_SGN] = 1.0
    v[32:48, V_SGN] = -1.0
    for l in range(2):
        o = V_L + l * VL_N
        v[:, o + VL_BIN:o + VL_BIN + 16] = fcols(g["b_in_2"][l, 0:2048])
        v[:, o + VL_CW:o + VL_CW + 124] = g["conv_w_2"][l].reshape(31, 4, P).transpose(2, 1, 0).reshape(P, 124)
        for col, name in ((VL_CB, "conv_b_2"), (VL_CG, "conv_ln_g_2"), (VL_CBT, "conv_ln_b_2"), (VL_G1, "ln1_g_2"),
                          (VL_B1, "ln1_b_2"), (VL_G2, "ln2_g_2"), (VL_B2, "ln2_b_2")):
            a = fcols(g[name][l])
            v[:, o + col:o + col + a.shape[1]] = a
    q = np.arange(T)
    r, cc = q // 64, q % 64
    dr = r[None, :] - r[:, None] + 7
    dc = np.clip(cc[None, :] - cc[:, None] + 15, 0, 30)
    win = np.clip(cc - 8, 0, 48)[:, None]
    ok = (cc[None, :] >= win) & (cc[None, :] < win + 16)
    nb = g["rpb_2"][:, :, dr, dc]
    nb = np.where(ok, nb, np.float32(-1e30)).astype(np.float32)
    nb = nb.reshape(2, 8, 2, P, T).transpose(0, 3, 2, 1, 4)
    d = {
        "x": g["x"], "meta": g["meta_tokens"], "consts": c, "vecs": v,
        "onehot": np.ascontiguousarray(np.broadcast_to(np.eye(16, dtype=np.float32)[:, :, None], (16, 16, T))), "norm_pre": g["norm_pre"], "w_in": g["w_in"][0], "norm_post": g["norm_post"],
        "w_att": g["w_proj_att"][0], "w_ssd": g["w_proj_ssd"][0], "w_out": g["w_out"][0], "a_log": g["a_log"],
        "ln_in_g": g["ln_in_g_2"][None], "ln_in_b": g["ln_in_b_2"][None], "w_in2": g["w_in_2"], "b_in2": g["b_in_2"],
        "na_bias": nb, "w_out2": g["w_out_2"], "b_out2": g["b_out_2"], "ln1_g": g["ln1_g_2"], "ln1_b": g["ln1_b_2"],
        "w1": g["ffn_w1_2"][0], "w3": g["ffn_w3_2"][0], "w2": g["ffn_w2_2"][0],
        "pT": g["p_2"][:, 0].transpose(0, 2, 1), "ple_w": g["ple_w_2"], "gate_w": g["ple_gate_w_2"],
        "gate_b": g["ple_gate_b_2"], "ln2_g": g["ln2_g_2"], "ln2_b": g["ln2_b_2"], "w_router": g["w_router_2"][0],
        "mw1": g["moe_w1_2"][0], "mw3": g["moe_w3_2"][0], "mw2": g["moe_w2_2"][0],
    }
    return {k: np.ascontiguousarray(a) for k, a in d.items()}


def kernel(**inputs):
    import numpy as np
    import concourse.bacc as _bacc
    from concourse.bass_utils import run_bass_kernel_spmd as _run

    arrays = layout(inputs)
    nc = _bacc.Bacc("TRN2", target_bir_lowering=False, num_devices=1)
    args = [nc.dram_tensor(k, a.shape, mybir.dt.from_np(a.dtype), kind="ExternalInput").ap() for k, a in arrays.items()]
    out = nc.dram_tensor("out", (1, T, D), F32, kind="ExternalOutput").ap()
    bass_hybrid_conformer_moe(nc, *args, out)
    return _run(nc, [arrays], core_ids=[0]).results[0]["out"]
```
